# Optimizing a Trainium2 kernel written in Bass

```python
import jax, jax.numpy as jnp
from jax import lax
import numpy as np

D_MODEL = 1024
BATCH = 1
SEQ = 1024
DEPTH = 1

CHUNK = 64
D_MIX = D_MODEL

GLA_W = D_MIX // 2
GLA_HEADS = 4
GLA_DV = GLA_W // GLA_HEADS
GLA_DK = GLA_DV // 2
GLA_QK_W = GLA_HEADS * GLA_DK
GLA_GATE_RANK = 16
GLA_GATE_TAU = 16.0

HGRN_W = D_MIX // 4
HGRN_HEADS = 4
HGRN_DV = HGRN_W // HGRN_HEADS
HGRN_DK = 64
HGRN_QK_W = HGRN_HEADS * HGRN_DK

SB_W = D_MIX - GLA_W - HGRN_W
SB_HEADS = 4
SB_DH = SB_W // SB_HEADS
SB_BLOCK = 128

IN_WIDTHS = (GLA_QK_W, GLA_QK_W, GLA_W, GLA_GATE_RANK, GLA_W,
             HGRN_QK_W, HGRN_QK_W, HGRN_W, HGRN_W,
             SB_W, SB_W, SB_W, SB_W)
D_IN = sum(IN_WIDTHS)
EPS = 1e-6


def rms_norm(x):
    xf = x.astype(jnp.float32)
    y = xf * lax.rsqrt(jnp.mean(xf * xf, axis=-1, keepdims=True) + EPS)
    return y.astype(x.dtype)

def split_heads(a, n_heads):
    b, t, w = a.shape
    return a.reshape(b, t, n_heads, w // n_heads).transpose(0, 2, 1, 3)

def merge_heads(a):
    b, h, t, d = a.shape
    return a.transpose(0, 2, 1, 3).reshape(b, t, h * d)

def chunk_gated_linear_attn(q, k, v, g):
    bsz, nh, t, dk = q.shape
    dv = v.shape[-1]
    n_chunks = t // CHUNK

    def to_chunks(a):
        return a.reshape(bsz, nh, n_chunks, CHUNK, a.shape[-1]).transpose(2, 0, 1, 3, 4)

    causal = jnp.tril(jnp.ones((CHUNK, CHUNK), dtype=bool))[:, :, None]

    def step(state, inp):
        q_c, k_c, v_c, g_c = inp
        b_cum = jnp.cumsum(g_c, axis=2)
        diff = b_cum[:, :, :, None, :] - b_cum[:, :, None, :, :]
        decay = jnp.exp(jnp.where(causal, diff, -jnp.inf))
        scores = jnp.einsum('bhtd,bhsd,bhtsd->bhts', q_c, k_c, decay)
        o_c = (jnp.einsum('bhts,bhsv->bhtv', scores, v_c)
               + jnp.einsum('bhtd,bhdv->bhtv', q_c * jnp.exp(b_cum), state))
        b_last = b_cum[:, :, -1:, :]
        state = (jnp.exp(b_last[:, :, 0, :, None]) * state
                 + jnp.einsum('bhsd,bhsv->bhdv', k_c * jnp.exp(b_last - b_cum), v_c))
        return state, o_c

    s0 = jnp.zeros((bsz, nh, dk, dv), dtype=v.dtype)
    _, o = lax.scan(step, s0, (to_chunks(q), to_chunks(k), to_chunks(v), to_chunks(g)))
    return o.transpose(1, 2, 0, 3, 4).reshape(bsz, nh, t, dv)

def stick_breaking_attn(q, k, v):
    bsz, nh, t, dh = q.shape
    scale = dh ** -0.5
    outs = []
    for i in range(t // SB_BLOCK):
        n_keys = (i + 1) * SB_BLOCK
        q_blk = q[:, :, i * SB_BLOCK:n_keys]
        k_blk = k[:, :, :n_keys]
        v_blk = v[:, :, :n_keys]
        z = jnp.einsum('bhtd,bhsd->bhts', q_blk, k_blk).astype(jnp.float32) * scale
        t_pos = i * SB_BLOCK + jnp.arange(SB_BLOCK)[:, None]
        s_pos = jnp.arange(n_keys)[None, :]
        strict = s_pos < t_pos
        log_beta = jax.nn.log_sigmoid(z)
        log_1m_beta = jnp.where(strict, jax.nn.log_sigmoid(-z), 0.0)
        between = lax.cumsum(log_1m_beta, axis=3, reverse=True) - log_1m_beta
        weights = jnp.where(strict, jnp.exp(log_beta + between), 0.0)
        outs.append(jnp.einsum('bhts,bhsv->bhtv', weights.astype(v.dtype), v_blk))
    return jnp.concatenate(outs, axis=2)

def split_columns(p):
    idx = []
    acc = 0
    for w in IN_WIDTHS[:-1]:
        acc += w
        idx.append(acc)
    return jnp.split(p, idx, axis=-1)

def first_inputs(seed: int = 0) -> dict:
    key = jax.random.key(seed)
    ks = jax.random.split(key, 12)
    f32 = jnp.float32
    x = jax.random.normal(ks[0], (BATCH, SEQ, D_MODEL), f32)
    c = jax.random.normal(ks[1], (BATCH, D_MODEL), f32)
    w_ada = jax.random.normal(ks[2], (DEPTH, D_MODEL, 3 * D_MODEL), f32) * (0.5 * D_MODEL ** -0.5)
    b_ada = 0.02 * jax.random.normal(ks[3], (DEPTH, 3 * D_MODEL), f32)
    w_in = jax.random.normal(ks[4], (DEPTH, D_MODEL, D_IN), f32) * D_MODEL ** -0.5
    w_gla_gate2 = jax.random.normal(ks[5], (DEPTH, GLA_GATE_RANK, GLA_QK_W), f32) * GLA_GATE_RANK ** -0.5
    b_gla_gate = 0.1 * jax.random.normal(ks[6], (DEPTH, GLA_QK_W), f32)
    gla_norm_w = 1.0 + 0.1 * jax.random.normal(ks[7], (DEPTH, GLA_DV), f32)
    hgrn_lb_logits = jax.random.normal(ks[8], (DEPTH, HGRN_QK_W), f32)
    hgrn_norm_w = 1.0 + 0.1 * jax.random.normal(ks[9], (DEPTH, HGRN_DV), f32)
    w_out = jax.random.normal(ks[10], (DEPTH, D_MIX, D_MODEL), f32) * D_MIX ** -0.5
    final_norm_w = 1.0 + 0.1 * jax.random.normal(ks[11], (D_MODEL,), f32)
    return {'x': x, 'c': c, 'w_ada': w_ada, 'b_ada': b_ada, 'w_in': w_in,
            'w_gla_gate2': w_gla_gate2, 'b_gla_gate': b_gla_gate, 'gla_norm_w': gla_norm_w,
            'hgrn_lb_logits': hgrn_lb_logits, 'hgrn_norm_w': hgrn_norm_w,
            'w_out': w_out, 'final_norm_w': final_norm_w}

def first_block(x, c, w_ada, b_ada, w_in, w_gla_gate2, b_gla_gate, gla_norm_w,
              hgrn_lb_logits, hgrn_norm_w, w_out, final_norm_w):
    c_act = jax.nn.silu(c)
    probs = jax.nn.softmax(hgrn_lb_logits.astype(jnp.float32), axis=0)
    cum = jnp.cumsum(probs, axis=0)
    lower_bounds = (cum - cum[0:1]).astype(x.dtype)

    for l in range(DEPTH):
        ada = c_act @ w_ada[l] + b_ada[l]
        shift, scale, gate = jnp.split(ada, 3, axis=-1)
        h = rms_norm(x) * (1.0 + scale[:, None, :]) + shift[:, None, :]
        p = h @ w_in[l]
        (qa, ka, va, lra, ga,
         qb, fb, ib, gb,
         qc, kc, vc, gc) = split_columns(p)

        log_alpha = jax.nn.log_sigmoid(lra @ w_gla_gate2[l] + b_gla_gate[l]) / GLA_GATE_TAU
        o_a = chunk_gated_linear_attn(split_heads(qa, GLA_HEADS) * GLA_DK ** -0.5,
                                      split_heads(ka, GLA_HEADS),
                                      split_heads(va, GLA_HEADS),
                                      split_heads(log_alpha, GLA_HEADS))
        o_a = merge_heads(rms_norm(o_a) * gla_norm_w[l]) * jax.nn.silu(ga)

        lb = lower_bounds[l]
        log_f = jnp.logaddexp(jnp.log(lb), jnp.log1p(-lb) + jax.nn.log_sigmoid(fb))
        k_b = (1.0 - lb) * jax.nn.sigmoid(-fb)
        o_b = chunk_gated_linear_attn(split_heads(jax.nn.silu(qb), HGRN_HEADS),
                                      split_heads(k_b, HGRN_HEADS),
                                      split_heads(ib, HGRN_HEADS),
                                      split_heads(log_f, HGRN_HEADS))
        o_b = merge_heads(rms_norm(o_b) * hgrn_norm_w[l]) * jax.nn.silu(gb)

        o_c = stick_breaking_attn(split_heads(qc, SB_HEADS),
                                  split_heads(kc, SB_HEADS),
                                  split_heads(vc, SB_HEADS))
        o_c = merge_heads(o_c) * jax.nn.silu(gc)

        y = jnp.concatenate([o_a, o_b, o_c], axis=-1) @ w_out[l]
        x = x + gate[:, None, :] * y

    return rms_norm(x) * final_norm_w


ROPE_THETA = 500000.0
Q_BLOCK = 128
A_HEADS = 8
A_KV_HEADS = 2
A_HEAD_DIM = 64
A_ROT_DIM = A_HEAD_DIM // 4
IDX_HEADS = 8
IDX_DIM = 64
IDX_ROT_DIM = IDX_DIM // 4
INDEX_TOPK_MAX = 256
B_HEADS = 8
B_Q_RANK = 256
B_KV_RANK = 128
B_NOPE_DIM = 64
B_ROPE_DIM = 32
B_V_DIM = 64
D_FF = 2816
CONV_WIDTH = 3

A_Q_W = A_HEADS * A_HEAD_DIM
A_KV_W = A_KV_HEADS * A_HEAD_DIM
IDX_Q_W = IDX_HEADS * IDX_DIM
B_OUT_W = B_HEADS * B_V_DIM
IN_SPLITS = [A_Q_W, A_KV_W, A_KV_W, IDX_Q_W, IDX_DIM, IDX_HEADS,
             B_Q_RANK, B_KV_RANK, B_ROPE_DIM, D_MODEL, D_MODEL]
IN_PROJ_W = int(sum(IN_SPLITS))
IN_OFFSETS = [int(o) for o in np.cumsum(IN_SPLITS)[:-1]]


def rmsnorm(x, g):
    xf = x.astype(jnp.float32)
    y = xf * lax.rsqrt(jnp.mean(xf * xf, axis=-1, keepdims=True) + EPS)
    return (y * g.astype(jnp.float32)).astype(x.dtype)

def rope_tables(positions, rot_dim):
    inv = ROPE_THETA ** (-jnp.arange(0, rot_dim, 2, dtype=jnp.float32) / rot_dim)
    ang = positions.astype(jnp.float32)[..., None] * inv
    return jnp.cos(ang), jnp.sin(ang)

def apply_rope(x, cos, sin, rot_dim):
    xr = x[..., :rot_dim].astype(jnp.float32)
    x1, x2 = jnp.split(xr, 2, axis=-1)
    c = cos[:, :, None, :]
    s = sin[:, :, None, :]
    rot = jnp.concatenate([x1 * c - x2 * s, x1 * s + x2 * c], axis=-1).astype(x.dtype)
    return jnp.concatenate([rot, x[..., rot_dim:]], axis=-1)

def to_blocks(t, nb):
    b = t.shape[0]
    return jnp.moveaxis(t.reshape(b, nb, Q_BLOCK, *t.shape[2:]), 1, 0)

def indexed_sparse_attention(q, k, v, qi, ki, wi, pos, topk):
    b, s = pos.shape
    nb = s // Q_BLOCK
    group = A_HEADS // A_KV_HEADS
    scale = A_HEAD_DIM ** -0.5
    bidx = jnp.arange(b)[:, None, None]

    def one_block(args):
        qb, qib, wib, posb = args
        dots = jnp.einsum('bqhd,bsd->bqhs', qib, ki, preferred_element_type=jnp.float32)
        iscore = jnp.einsum('bqh,bqhs->bqs', wib.astype(jnp.float32), jax.nn.relu(dots))
        causal = pos[:, None, :] <= posb[:, :, None]
        iscore = jnp.where(causal, iscore, -jnp.inf)
        _, idx = lax.top_k(iscore, topk)
        ksel = k[bidx, idx]
        vsel = v[bidx, idx]
        valid = pos[bidx, idx] <= posb[:, :, None]
        qg = qb.reshape(b, Q_BLOCK, A_KV_HEADS, group, A_HEAD_DIM)
        sc = jnp.einsum('bqgrd,bqkgd->bqgrk', qg, ksel, preferred_element_type=jnp.float32) * scale
        sc = jnp.where(valid[:, :, None, None, :], sc, -jnp.inf)
        p = jax.nn.softmax(sc, axis=-1)
        o = jnp.einsum('bqgrk,bqkgd->bqgrd', p.astype(v.dtype), vsel)
        return o.reshape(b, Q_BLOCK, A_HEADS * A_HEAD_DIM)

    out = lax.map(one_block, (to_blocks(q, nb), to_blocks(qi, nb), to_blocks(wi, nb), to_blocks(pos, nb)))
    return jnp.moveaxis(out, 0, 1).reshape(b, s, A_HEADS * A_HEAD_DIM)

def latent_attention(q_nope, q_rope, k_nope, k_rope, v, pos):
    b, s = pos.shape
    nb = s // Q_BLOCK
    scale = (B_NOPE_DIM + B_ROPE_DIM) ** -0.5

    def one_block(args):
        qn, qr, posb = args
        sc = (jnp.einsum('bqhd,bshd->bhqs', qn, k_nope, preferred_element_type=jnp.float32)
              + jnp.einsum('bqhd,bsd->bhqs', qr, k_rope, preferred_element_type=jnp.float32)) * scale
        causal = pos[:, None, None, :] <= posb[:, None, :, None]
        sc = jnp.where(causal, sc, -jnp.inf)
        p = jax.nn.softmax(sc, axis=-1)
        o = jnp.einsum('bhqs,bshd->bqhd', p.astype(v.dtype), v)
        return o.reshape(b, Q_BLOCK, B_HEADS * B_V_DIM)

    out = lax.map(one_block, (to_blocks(q_nope, nb), to_blocks(q_rope, nb), to_blocks(pos, nb)))
    return jnp.moveaxis(out, 0, 1).reshape(b, s, B_HEADS * B_V_DIM)

def causal_depthwise_conv(u, w, bias):
    s = u.shape[1]
    up = jnp.pad(u, ((0, 0), (CONV_WIDTH - 1, 0), (0, 0)))
    y = bias
    for j in range(CONV_WIDTH):
        y = y + w[j] * up[:, j:j + s]
    return y

def second_inputs(seed: int = 0) -> dict:
    key = jax.random.key(seed)
    ks = jax.random.split(key, 20)
    f32 = jnp.float32
    L = DEPTH

    def nrm(k, shape, fan_in):
        return jax.random.normal(k, shape, f32) * (fan_in ** -0.5)

    def gain(k, shape):
        return 1.0 + 0.02 * jax.random.normal(k, shape, f32)

    return {
        "x": jax.random.normal(ks[0], (BATCH, SEQ, D_MODEL), f32),
        "positions": jnp.broadcast_to(jnp.arange(SEQ, dtype=jnp.int32), (BATCH, SEQ)),
        "norm_mix_g": gain(ks[1], (L, D_MODEL)),
        "w_in": nrm(ks[2], (L, D_MODEL, IN_PROJ_W), D_MODEL),
        "idx_k_norm_g": gain(ks[3], (L, IDX_DIM)),
        "q_a_norm_g": gain(ks[4], (L, B_Q_RANK)),
        "kv_a_norm_g": gain(ks[5], (L, B_KV_RANK)),
        "w_uq": nrm(ks[6], (L, B_Q_RANK, B_HEADS, B_NOPE_DIM + B_ROPE_DIM), B_Q_RANK),
        "w_uk": nrm(ks[7], (L, B_KV_RANK, B_HEADS, B_NOPE_DIM), B_KV_RANK),
        "w_uv": nrm(ks[8], (L, B_KV_RANK, B_HEADS, B_V_DIM), B_KV_RANK),
        "w_branch_a": nrm(ks[9], (L, A_Q_W, D_MODEL), A_Q_W),
        "w_branch_b": nrm(ks[10], (L, B_OUT_W, D_MODEL), B_OUT_W),
        "w_out": nrm(ks[11], (L, D_MODEL, D_MODEL), D_MODEL),
        "norm_ffn_g": gain(ks[12], (L, D_MODEL)),
        "w_up": nrm(ks[13], (L, D_MODEL, 2 * D_FF), D_MODEL),
        "conv_w": nrm(ks[14], (L, CONV_WIDTH, 2 * D_FF), CONV_WIDTH),
        "conv_b": 0.01 * jax.random.normal(ks[15], (L, 2 * D_FF), f32),
        "w_down": nrm(ks[16], (L, D_FF, D_MODEL), D_FF),
        "norm_final_g": gain(ks[17], (D_MODEL,)),
    }

def second_block(x, positions, norm_mix_g, w_in, idx_k_norm_g, q_a_norm_g, kv_a_norm_g,
              w_uq, w_uk, w_uv, w_branch_a, w_branch_b, w_out, norm_ffn_g,
              w_up, conv_w, conv_b, w_down, norm_final_g):
    b, s, _ = x.shape
    topk = min(INDEX_TOPK_MAX, s // 4)
    cos_a, sin_a = rope_tables(positions, A_ROT_DIM)
    cos_i, sin_i = rope_tables(positions, IDX_ROT_DIM)
    cos_b, sin_b = rope_tables(positions, B_ROPE_DIM)
    h = x
    for l in range(DEPTH):
        hn = rmsnorm(h, norm_mix_g[l])
        proj = jnp.einsum('bsd,de->bse', hn, w_in[l])
        (a_q, a_k, a_v, i_q, i_k, i_w, b_cq, b_ckv, b_kr, g_a, g_b) = jnp.split(proj, IN_OFFSETS, axis=-1)

        a_q = apply_rope(a_q.reshape(b, s, A_HEADS, A_HEAD_DIM), cos_a, sin_a, A_ROT_DIM)
        a_k = apply_rope(a_k.reshape(b, s, A_KV_HEADS, A_HEAD_DIM), cos_a, sin_a, A_ROT_DIM)
        a_v = a_v.reshape(b, s, A_KV_HEADS, A_HEAD_DIM)
        i_q = apply_rope(i_q.reshape(b, s, IDX_HEADS, IDX_DIM), cos_i, sin_i, IDX_ROT_DIM) * (IDX_DIM ** -0.5)
        i_k = apply_rope(rmsnorm(i_k, idx_k_norm_g[l])[:, :, None, :], cos_i, sin_i, IDX_ROT_DIM)[:, :, 0, :]
        i_w = i_w * (IDX_HEADS ** -0.5)
        o_a = indexed_sparse_attention(a_q, a_k, a_v, i_q, i_k, i_w, positions, topk)

        c_q = rmsnorm(b_cq, q_a_norm_g[l])
        q_b = jnp.einsum('bsr,rhd->bshd', c_q, w_uq[l])
        q_nope = q_b[..., :B_NOPE_DIM]
        q_rope = apply_rope(q_b[..., B_NOPE_DIM:], cos_b, sin_b, B_ROPE_DIM)
        c_kv = rmsnorm(b_ckv, kv_a_norm_g[l])
        k_nope = jnp.einsum('bsr,rhd->bshd', c_kv, w_uk[l])
        v_b = jnp.einsum('bsr,rhd->bshd', c_kv, w_uv[l])
        k_rope = apply_rope(b_kr[:, :, None, :], cos_b, sin_b, B_ROPE_DIM)[:, :, 0, :]
        o_b = latent_attention(q_nope, q_rope, k_nope, k_rope, v_b, positions)

        y_a = jnp.einsum('bsc,cd->bsd', o_a, w_branch_a[l])
        y_b = jnp.einsum('bsc,cd->bsd', o_b, w_branch_b[l])
        merged = jax.nn.sigmoid(g_a) * y_a + jax.nn.sigmoid(g_b) * y_b
        h = h + jnp.einsum('bsd,de->bse', merged, w_out[l])

        hn = rmsnorm(h, norm_ffn_g[l])
        u = jnp.einsum('bsd,df->bsf', hn, w_up[l])
        u = causal_depthwise_conv(u, conv_w[l], conv_b[l])
        gate, val = jnp.split(u, 2, axis=-1)
        h = h + jnp.einsum('bsf,fd->bsd', jax.nn.silu(gate) * val, w_down[l])
    return rmsnorm(h, norm_final_g)


def setup_inputs(seed=0):
    out = dict(first_inputs(seed))
    for name, value in second_inputs(seed + 1).items():
        if name != "x":
            out[name + "_2"] = value
    return out


def reference(
    x, c, w_ada, b_ada, w_in, w_gla_gate2, b_gla_gate, gla_norm_w, hgrn_lb_logits, hgrn_norm_w,
    w_out, final_norm_w, positions_2, norm_mix_g_2, w_in_2, idx_k_norm_g_2, q_a_norm_g_2,
    kv_a_norm_g_2, w_uq_2, w_uk_2, w_uv_2, w_branch_a_2, w_branch_b_2, w_out_2, norm_ffn_g_2,
    w_up_2, conv_w_2, conv_b_2, w_down_2, norm_final_g_2,
):
    x = first_block(
        x, c, w_ada, b_ada, w_in, w_gla_gate2, b_gla_gate, gla_norm_w, hgrn_lb_logits,
        hgrn_norm_w, w_out, final_norm_w,
    )
    return second_block(
        x, positions_2, norm_mix_g_2, w_in_2, idx_k_norm_g_2, q_a_norm_g_2, kv_a_norm_g_2,
        w_uq_2, w_uk_2, w_uv_2, w_branch_a_2, w_branch_b_2, w_out_2, norm_ffn_g_2, w_up_2,
        conv_w_2, conv_b_2, w_down_2, norm_final_g_2,
    )


_drawn_inputs = setup_inputs


def setup_inputs(seed=0):
    import zlib

    import numpy as np

    out = dict(_drawn_inputs(seed))
    spreads = {}
    factors = {'b_ada': 2.772,
     'b_gla_gate': 5.941,
     'gla_norm_w': 2.953,
     'hgrn_norm_w': 3.839,
     'norm_mix_g_2': 6.475,
     'idx_k_norm_g_2': 8.0,
     'q_a_norm_g_2': 8.0,
     'kv_a_norm_g_2': 8.0,
     'norm_ffn_g_2': 3.757,
     'conv_b_2': 7.852,
     'norm_final_g_2': 2.847}
    for name, (base, spread) in spreads.items():
        noise = np.random.default_rng([zlib.crc32(name.encode()), seed]).standard_normal(out[name].shape)
        drawn = base * np.exp(spread * noise) if base else spread * noise
        out[name] = __import__('jax').numpy.asarray(drawn.astype(out[name].dtype))
    for name, factor in factors.items():
        out[name] = (out[name] * factor).astype(out[name].dtype)
    return out
```

```python
import math
import numpy as np
import concourse.bass as bass
from concourse import mybir

F32 = mybir.dt.float32
U32 = mybir.dt.uint32
I32 = mybir.dt.int32
ALU = mybir.AluOpType
ACT = mybir.ActivationFunctionType
AX = mybir.AxisListType

P = 128
T = 1024
NT = T // P
D = 1024
KB = D // P
W512 = 512
EPS = 1e-6
MASKED = -1e30
SBUF_BASE = 1280

QA, KA, VA, LRA, GA, QB, FB, IB, GB, QC, KC, VC, GC = (
    0, 256, 512, 1024, 1040, 1552, 1808, 2064, 2320, 2576, 2832, 3088, 3344)
GLA_TAU = 16.0
RANK = 16
HEADS1 = 4
DK = 64
AQ, AK, AV, IQ, IK, IW, CQ, CKV, KR, GTA, GTB = (
    0, 512, 640, 768, 1280, 1344, 1352, 1608, 1736, 1768, 2792)
TOPK = 256
THETA = 500000.0
DFF = 2816
FBLK = DFF // P


class Steps:

    def __init__(self, k, name):
        self.sem, self.n = k.sem(name), 0

    def mark(self, ins):
        ins.then_inc(self.sem, 1)
        self.n += 1
        return self.n


class Weights:

    RING = 2

    def __init__(self, nc, place):
        self.slot = [place(f"weights_{i}", [P, KB * W512], 8 + 16 * i) for i in range(self.RING)]
        self.landed = [nc.alloc_semaphore(name=f"weights_landed_{i}") for i in range(self.RING)]
        self.freed = {}
        self.chunks = []
        self.issued = 0
        self.count = [0] * self.RING
        self.need = []

    def add(self, pieces, blocks, width):
        self.chunks.append((pieces, blocks, width))
        return len(self.chunks) - 1

    def view(self, n):
        _, blocks, width = self.chunks[n]
        return self.slot[n % self.RING][:, 0:blocks * width].rearrange("p (k n) -> p k n", n=width)

    def load(self, sp, n):
        if n >= self.RING:
            sp.wait_ge(*self.freed[n - self.RING])
        v, i = self.view(n), n % self.RING
        for at, src, width in self.chunks[n][0]:
            sp.dma_start(v[:, :, at:at + width], src.rearrange("(k p) n -> p k n", p=P)).then_inc(self.landed[i], 16)
            self.count[i] += 16
        self.need.append(self.count[i])

    def load_up_to(self, sp, n):
        while self.issued <= min(n, len(self.chunks) - 1):
            self.load(sp, self.issued)
            self.issued += 1

    def wait(self, pe, n):
        pe.wait_ge(self.landed[n % self.RING], self.need[n])


class Kernel:

    def __init__(self, nc):
        self.nc, self.own, self.cleared = nc, [], []

    def sem(self, name):
        self.own.append(self.nc.alloc_semaphore(name=name))
        return self.own[-1]

    def kept_sem(self, name):
        return self.nc.alloc_semaphore(name=name)

    def end_stage(self):
        for sem in self.cleared:
            self.nc.release_semaphore(sem)
        for sem in self.own:
            self.nc.gpsimd.sem_clear(sem)
        self.own, self.cleared = [], self.own


def plan(nc, k):

    def place(name, shape, kb, dt=F32):
        return nc.alloc_sbuf_tensor_at(name, shape, dt, offset=SBUF_BASE + int(kb * 1024))

    k.place = place
    k.ident = place("ident", [P, P], 0)
    k.levels = place("level_masks", [P, 7, P], 0.5)
    k.strict = place("strict_mask", [P, P], 4)
    k.shiftcol = place("shift_col", [P, KB], 4.5)
    k.scalecol = place("scale_col", [P, KB], 4.5625)
    k.small = place("small", [P, 256], 5)
    k.w = Weights(nc, place)
    k.output_stored = k.kept_sem("output_stored")
    k.hT = place("hT", [P, KB, T], 40)
    k.keep = place("keep", [P, T], 208)
    k.oT = place("mixed_outT", [P, KB, T], 72)
    k.banks = nc.alloc_psum_tensor("banks", [P, 8, W512], F32)
    w = k.w
    cols = lambda a, lo, hi: a[:, lo:hi]
    w_in, w_in2 = k.w_in[0], k.w_in_2[0]
    k.c_qka = w.add([(0, cols(w_in, QA, VA), 512)], KB, 512)
    k.c_va = w.add([(0, cols(w_in, VA, LRA), 512)], KB, 512)
    k.c_ga = w.add([(0, cols(w_in, GA, QB), 512)], KB, 512)
    k.c_qfb = w.add([(0, cols(w_in, QB, IB), 512)], KB, 512)
    k.c_igb = w.add([(0, cols(w_in, IB, QC), 512)], KB, 512)
    k.c_qkc = w.add([(0, cols(w_in, QC, VC), 512)], KB, 512)
    k.c_vgc = w.add([(0, cols(w_in, VC, 3600), 512)], KB, 512)
    k.c_out = [w.add([(0, cols(k.w_out[0], h * 512, h * 512 + 512), 512)], KB, 512) for h in range(2)]
    k.c_aq = w.add([(0, cols(w_in2, AQ, AK), 512)], KB, 512)
    k.c_akv = w.add([(0, cols(w_in2, AK, IQ), 256)], KB, 256)
    k.c_iq = w.add([(0, cols(w_in2, IQ, IK), 512)], KB, 512)
    k.c_mix = w.add([(0, cols(w_in2, IK, GTA), GTA - IK)], KB, GTA - IK)
    k.c_gate = [w.add([(0, cols(w_in2, GTA + h * 512, GTA + h * 512 + 512), 512)], KB, 512) for h in range(4)]
    k.c_ba = w.add([(0, k.w_branch_a_2[0], D)], 4, D)
    k.c_bb = w.add([(0, k.w_branch_b_2[0], D)], 4, D)
    k.c_out2 = [w.add([(0, cols(k.w_out_2[0], h * 512, h * 512 + 512), 512)], KB, 512) for h in range(2)]
    up = k.w_up_2[0]
    k.c_up = [w.add([(0, cols(up, f * 256, f * 256 + 256), 256),
                     (256, cols(up, DFF + f * 256, DFF + f * 256 + 256), 256)], KB, 512) for f in range(FBLK // 2)]
    down = k.w_down_2[0]
    k.c_down = [[w.add([(0, down[b * P:min(b + 8, FBLK) * P, h * 512:h * 512 + 512], 512)], min(8, FBLK - b), 512)
                 for b in range(0, FBLK, 8)] for h in range(2)]


class NormTranspose:

    def __init__(self, nc, k, name, x, scratch, out=None):
        self.nc, self.k, self.x, self.scratch, self.bank0 = nc, k, x, scratch, 0
        self.out = x if out is None else out
        self.squares = k.small[:, 0:8]
        self.rms = k.small[:, 8:16]
        self.rstd = k.small[:, 16:24]
        self.root = k.small[:, 24:32]
        s = lambda n: k.sem(f"{name}_{n}")
        self.summed, self.mean, self.rooted, self.inverted = s("summed"), s("mean"), s("rooted"), s("inverted")
        self.divided, self.turned, self.by_act, self.by_dve = s("divided"), s("turned"), s("stored_act"), s("stored_dve")

    def act_stats(self, act, ready):
        for i in range(NT):
            ready(act, i)
            self.nc.scalar.activation(self.scratch[:, i, :], self.x[:, i, :], ACT.Square,
                                      accum_out=self.squares[:, i:i + 1]).then_inc(self.summed, 1)
        act.wait_ge(self.mean, 1)
        self.nc.scalar.activation(self.root, self.rms, ACT.Sqrt).then_inc(self.rooted, 1)

    def dve_stats(self, dve):
        dve.wait_ge(self.summed, NT)
        self.nc.vector.tensor_scalar(self.rms, self.squares, 1.0 / D, EPS, ALU.mult, ALU.add).then_inc(self.mean, 1)
        dve.wait_ge(self.rooted, 1)
        self.nc.vector.reciprocal(self.rstd, self.root).then_inc(self.inverted, 1)
        dve.wait_ge(self.inverted, 1)

    def dve_divide(self, dve):
        for i in range(NT):
            self.nc.vector.tensor_scalar(self.out[:, i, :], self.x[:, i, :], self.rstd[:, i:i + 1], None,
                                         ALU.mult).then_inc(self.divided, 1)

    def pe_transpose(self, pe):
        for i in range(NT):
            pe.wait_ge(self.divided, i + 1)
            for g in range(2):
                j = 2 * i + g
                if j >= 4:
                    pe.wait_ge(self.by_dve if g else self.by_act, (j - 4) // 2 + 1)
                for b in range(4):
                    ins = self.nc.tensor.transpose(self.k.banks[:, self.bank0 + j % 4, b * P:(b + 1) * P],
                                                   self.out[:, i, (4 * g + b) * P:(4 * g + b + 1) * P], self.k.ident[:, :])
                ins.then_inc(self.turned, 1)

    def store(self, eng, g):
        for i in range(NT):
            j = 2 * i + g
            eng.wait_ge(self.turned, j + 1)
            src = self.k.banks[:, self.bank0 + j % 4, :].rearrange("p (b t) -> p b t", t=P)
            dst = self.k.hT[:, 4 * g:4 * g + 4, i * P:(i + 1) * P]
            if g:
                self.nc.vector.tensor_copy(dst, src).then_inc(self.by_dve, 1)
            else:
                self.nc.scalar.activation(dst, src, ACT.Copy).then_inc(self.by_act, 1)


def stage_input(nc, k):
    x = k.place("x_tiles", [P, NT, D], 72)
    ada = k.place("ada_weights", [P, 6, KB, 512], 104)
    gate_bias = k.place("gate_bias", [P, D], 216)
    k.gate_row = k.place("gate_row", [P, D], 212)
    crow = k.place("c_broadcast", [P, KB, P], 204)
    ccol, cact, bcol = k.small[:, 32:40], k.small[:, 40:48], k.small[:, 48:64]
    norm = NormTranspose(nc, k, "norm1", x, k.hT)
    s = lambda n: k.sem(n)
    x_in = [s(f"x_in_{i}") for i in range(2)]
    vec_in, ada_in = s("c_in"), [s(f"ada_in_{i}") for i in range(6)]
    built, silu_done, spread = s("constants_built"), s("c_silu"), s("c_spread")
    ada_mm, gate_mm, cols_done, hmod = s("ada_cols"), s("ada_gate"), s("mod_cols_done"), s("h_modulated")
    pool_step = Steps(k, "pool_step1")
    xd = k.x[0].rearrange("(i p) d -> i p d", p=P)
    wd = k.w_ada[0]
    with nc.Block() as block:
        @block.sync
        def _(sp):
            for h in range(2):
                sp.dma_start(x[:, 4 * h:4 * h + 4, :], xd[4 * h:4 * h + 4].rearrange("i p d -> p i d")).then_inc(x_in[h], 16)
            for n in range(4):
                sp.dma_start(ada[:, n, :, :], wd[:, n * 512:(n + 1) * 512].rearrange("(k p) n -> p k n", p=P)).then_inc(ada_in[n], 16)
            k.w.load_up_to(sp, 0)
            for n in range(4, 6):
                sp.dma_start(ada[:, n, :, :], wd[:, n * 512:(n + 1) * 512].rearrange("(k p) n -> p k n", p=P)).then_inc(ada_in[n], 16)
            k.w.load_up_to(sp, 1)

        @block.gpsimd
        def _(pool):
            pool.memset(k.ident[:, :], 0.0).then_inc(pool_step.sem, 1)
            pool.memset(k.strict[:, :], 1.0).then_inc(pool_step.sem, 1)
            pool.memset(k.levels[:, :, :], 0.0).then_inc(pool_step.sem, 1)
            n = 3
            pool.wait_ge(pool_step.sem, n)
            pool.affine_select(out=k.ident[:, :], in_=k.ident[:, :], compare_op=ALU.not_equal, fill=1.0, base=0,
                               pattern=[[-1, P]], channel_multiplier=1).then_inc(built, 1)
            pool.affine_select(out=k.strict[:, :], in_=k.strict[:, :], compare_op=ALU.is_gt, fill=0.0, base=0,
                               pattern=[[-1, P]], channel_multiplier=1).then_inc(built, 1)
            for l in range(7):
                h = 1 << l
                v = k.levels[:, l, :].rearrange("p (b two h) -> p b two h", two=2, h=h)[:, :, 1, :]
                nb = P // (2 * h)
                pool.memset(v, 1.0).then_inc(pool_step.sem, 1)
                n += 1
                pool.wait_ge(pool_step.sem, n)
                pool.affine_select(out=v, in_=v, compare_op=ALU.is_ge, fill=0.0, base=0,
                                   pattern=[[-2 * h, nb], [0, h]], channel_multiplier=1).then_inc(pool_step.sem, 1)
                n += 1
                pool.wait_ge(pool_step.sem, n)
                pool.affine_select(out=v, in_=v, compare_op=ALU.is_ge, fill=0.0, base=h - 1,
                                   pattern=[[2 * h, nb], [0, h]], channel_multiplier=-1).then_inc(built, 1)

        @block.scalar
        def _(act):
            act.dma_start(ccol, k.c.rearrange("o (k p) -> p (o k)", p=P), allow_slow_non_contiguous=True).then_inc(vec_in, 16)
            act.dma_start(bcol, k.b_ada[0, 0:2 * D].rearrange("(k p) -> p k", p=P), allow_slow_non_contiguous=True).then_inc(vec_in, 16)
            act.dma_start(gate_bias[:, :], k.b_ada[0, 2 * D:3 * D].partition_broadcast(P)).then_inc(vec_in, 16)
            norm.act_stats(act, lambda e, i: e.wait_ge(x_in[i // 4], 16))
            act.wait_ge(vec_in, 48)
            nc.scalar.activation(cact, ccol, ACT.Silu).then_inc(silu_done, 1)
            norm.store(act, 0)
            act.wait_ge(cols_done, 2)
            act.wait_ge(norm.by_dve, NT)
            act.wait_ge(norm.by_act, NT)
            for b in range(0, KB, 2):
                nc.scalar.activation(k.hT[:, b, :], k.hT[:, b, :], ACT.Identity, bias=k.shiftcol[:, b:b + 1],
                                     scale=k.scalecol[:, b:b + 1]).then_inc(hmod, 1)

        @block.tensor
        def _(pe):
            pe.wait_ge(built, 1)
            norm.pe_transpose(pe)
            pe.wait_ge(silu_done, 1)
            for n in range(4):
                pe.wait_ge(ada_in[n], 16)
                for j in range(4):
                    for b in range(KB):
                        ins = nc.tensor.matmul(k.banks[:, 4, 4 * n + j:4 * n + j + 1], ada[:, n, b, j * P:(j + 1) * P],
                                               cact[:, b:b + 1], start=(b == 0), stop=(b == KB - 1))
                ins.then_inc(ada_mm, 1)
            pe.wait_ge(spread, 1)
            for n in range(4, 6):
                pe.wait_ge(ada_in[n], 16)
                for b in range(KB):
                    ins = nc.tensor.matmul(k.banks[:, n + 1, :], crow[:, b, :], ada[:, n, b, :],
                                           start=(b == 0), stop=(b == KB - 1))
                ins.then_inc(gate_mm, 1)

        @block.vector
        def _(dve):
            norm.dve_stats(dve)
            norm.dve_divide(dve)
            dve.wait_ge(silu_done, 1)
            nc.vector.tensor_copy(crow[:, :, :], cact.unsqueeze(2).to_broadcast([P, KB, P])).then_inc(spread, 1)
            norm.store(dve, 1)
            dve.wait_ge(vec_in, 48)
            dve.wait_ge(ada_mm, 4)
            nc.vector.tensor_tensor(k.shiftcol[:, :], k.banks[:, 4, 0:8], bcol[:, 0:8], ALU.add).then_inc(cols_done, 1)
            nc.vector.scalar_tensor_tensor(out=k.scalecol[:, :], in0=k.banks[:, 4, 8:16], scalar=1.0, in1=bcol[:, 8:16],
                                           op0=ALU.add, op1=ALU.add).then_inc(cols_done, 1)
            dve.wait_ge(cols_done, 2)
            dve.wait_ge(norm.by_act, NT)
            dve.wait_ge(norm.by_dve, NT)
            for b in range(1, KB, 2):
                nc.vector.tensor_scalar(k.hT[:, b, :], k.hT[:, b, :], k.scalecol[:, b:b + 1], k.shiftcol[:, b:b + 1],
                                        ALU.mult, ALU.add).then_inc(hmod, 1)
            for h in range(2):
                dve.wait_ge(gate_mm, h + 1)
                nc.vector.tensor_tensor(k.gate_row[:, h * 512:(h + 1) * 512], k.banks[:, 5 + h, :],
                                        gate_bias[:, h * 512:(h + 1) * 512], ALU.add).then_inc(hmod, 1)


class Projection:

    def __init__(self, nc, k, name, jobs, banks=8, src=None):
        self.nc, self.k, self.jobs, self.nb, self.src = nc, k, jobs, banks, src
        self.done = k.sem(f"{name}_product")
        self.stored = {e: k.sem(f"{name}_stored_{e}") for e in ("act", "dve")}
        self.nth = []
        count = {"act": 0, "dve": 0}
        for job in jobs:
            count[job["by"]] += 1
            self.nth.append(count[job["by"]])
            k.w.freed[job["chunk"]] = (self.done, len(self.nth))
        self.count = count

    def bank(self, j):
        return self.k.banks[:, j % self.nb, :]

    def pe_jobs(self, pe, lo, hi):
        k, w = self.k, self.k.w
        src = self.src if self.src is not None else k.hT
        for j in range(lo, hi):
            job = self.jobs[j]
            if j == 0 or self.jobs[j - 1]["chunk"] != job["chunk"]:
                w.wait(pe, job["chunk"])
            if j >= self.nb:
                o = j - self.nb
                pe.wait_ge(self.stored[self.jobs[o]["by"]], self.nth[o])
            wv = w.view(job["chunk"])
            for b in range(KB):
                if job["kind"] == "tokens":
                    i, c0, width = job["tile"], job["col"], job["width"]
                    ins = self.nc.tensor.matmul(self.bank(j)[:, 0:width], src[:, b, i * P:(i + 1) * P],
                                                wv[:, b, c0:c0 + width], start=(b == 0), stop=(b == KB - 1))
                else:
                    c, h = job["col"], job["half"]
                    ins = self.nc.tensor.matmul(self.bank(j), wv[:, b, c:c + P], src[:, b, h * 512:(h + 1) * 512],
                                                start=(b == 0), stop=(b == KB - 1))
            ins.then_inc(self.done, 1)


def feature_jobs(chunk, col, dest, how="copy", by=None):
    return [dict(chunk=chunk, kind="features", col=col, half=h, dest=dest, how=how,
                 by=by or ("act" if h == 0 else "dve")) for h in range(2)]


def token_jobs(chunk, col, width, dest, how="copy", by=None):
    return [dict(chunk=chunk, kind="tokens", tile=i, col=col, width=width, dest=dest, how=how,
                 by=by or ("act" if i % 2 == 0 else "dve")) for i in range(NT)]


def store_act(nc, out, src, how):
    if how == "copy":
        return nc.scalar.activation(out, src, ACT.Copy)
    if how == "silu":
        return nc.scalar.activation(out, src, ACT.Silu)
    if how == "sigmoid":
        return nc.scalar.activation(out, src, ACT.Sigmoid)
    return nc.scalar.activation(out, src, ACT.Copy, scale=float(how))


def store_dve(nc, out, src, how):
    if how == "copy":
        return nc.vector.tensor_copy(out, src)
    return nc.vector.tensor_scalar(out, src, float(how), None, ALU.mult)


def job_out(job):
    if job["kind"] == "tokens":
        return job["dest"](job["tile"])
    return job["dest"][:, job["half"] * 512:(job["half"] + 1) * 512]


def run_stores(nc, proj, eng, who):
    for j, job in enumerate(proj.jobs):
        if job["by"] != who:
            continue
        width = job["width"] if job["kind"] == "tokens" else 512
        eng.wait_ge(proj.done, j + 1)
        store = store_act if who == "act" else store_dve
        store(nc, job_out(job), proj.bank(j)[:, 0:width], job["how"]).then_inc(proj.stored[who], 1)


class Mixer:

    def __init__(self, k, name, dv):
        p = k.place
        self.name, self.dv = name, dv
        self.qT = p(f"{name}_qT", [P, 2, T], 104)
        self.kT = p(f"{name}_kT", [P, 2, T], 112)
        self.bT = p(f"{name}_bT", [P, 2, T], 120)
        self.v = p(f"{name}_v", [P, NT, 4 * dv], 128)
        self.g = p(f"{name}_g", [P, NT, 4 * dv], 144)
        self.t0 = p(f"{name}_t0", [P, 2, T], 160)
        self.t1 = p(f"{name}_t1", [P, 2, T], 168)
        self.t2 = p(f"{name}_t2", [P, 2, T], 176)
        self.keep = k.keep
        self.gain = p(f"{name}_gain", [P, dv], 6)


def softplus_act(nc, act, m, chain, ready):
    ready(act)
    n = chain.mark(nc.scalar.activation(m.t1[:, :, :], m.t0[:, :, :], ACT.Abs))
    act.wait_ge(chain.sem, n)
    n = chain.mark(nc.scalar.activation(m.t1[:, :, :], m.t1[:, :, :], ACT.Exp, scale=-1.0))
    act.wait_ge(chain.sem, n)
    return chain.mark(nc.scalar.activation(m.t1[:, :, :], m.t1[:, :, :], ACT.Ln, bias=1.0))


def summed_decay_dve(nc, dve, m, chain):
    for g in range(2):
        n = chain.mark(nc.vector.tensor_tensor_scan(m.bT[:, g, :], m.keep[:, :], m.t1[:, g, :], 0.0, ALU.mult, ALU.add))
    return n


def stage_gla_projection(nc, k):
    m = k.gla = Mixer(k, "gla", 128)
    p = k.place
    lra_w = p("lra_w", [P, KB, RANK], 184)
    gate2 = p("gate2_w", [RANK, 256], 185)
    lraT = p("lraT", [RANK, T], 188)
    bias = k.small[:, 64:66]
    jobs = []
    for g in range(2):
        jobs += feature_jobs(k.c_qka, g * P, m.qT[:, g, :], DK ** -0.5)
    for g in range(2):
        jobs += feature_jobs(k.c_qka, 256 + g * P, m.kT[:, g, :])
    jobs += token_jobs(k.c_va, 0, 512, lambda i: m.v[:, i, :])
    jobs += token_jobs(k.c_ga, 0, 512, lambda i: m.g[:, i, :], "silu", "act")
    proj = Projection(nc, k, "gla_proj", jobs, banks=6)
    s = lambda n: k.sem(n)
    vec_in, lra_mm, lra_st, z_mm, z_st = s("gla_vec_in"), s("lra_mm"), s("lra_stored"), s("gate_z"), s("gate_z_stored")
    a, d = Steps(k, "gla_gate_act"), Steps(k, "gla_gate_dve")
    with nc.Block() as block:
        @block.sync
        def _(sp):
            k.w.load_up_to(sp, k.c_qfb + 1)

        @block.gpsimd
        def _(pool):
            n = Steps(k, "pool_step2")
            c = n.mark(pool.memset(m.keep[:, :], 1.0))
            pool.wait_ge(n.sem, c)
            pool.memset(m.keep[:, :].rearrange("p (i t) -> p i t", t=P)[:, :, 0:1], 0.0).then_inc(d.sem, 1)

        d.n += 1

        @block.scalar
        def _(act):
            act.dma_start(lra_w[:, :, :], k.w_in[0][:, LRA:GA].rearrange("(k p) n -> p k n", p=P)).then_inc(vec_in, 16)
            act.dma_start(gate2[:, :], k.w_gla_gate2[0]).then_inc(vec_in, 16)
            act.dma_start(bias, k.b_gla_gate[0].rearrange("(k p) -> p k", p=P), allow_slow_non_contiguous=True).then_inc(vec_in, 16)
            act.dma_start(m.gain[:, :], k.gla_norm_w[0].partition_broadcast(P)).then_inc(vec_in, 16)
            for h in range(2):
                act.wait_ge(lra_mm, h + 1)
                nc.scalar.activation(lraT[:, h * 512:(h + 1) * 512], k.banks[0:RANK, 6 + h, :], ACT.Copy).then_inc(lra_st, 1)
            run_stores(nc, proj, act, "act")
            softplus_act(nc, act, m, a, lambda e: e.wait_ge(z_st, 4))

        @block.tensor
        def _(pe):
            pe.wait_ge(vec_in, 64)
            for h in range(2):
                for b in range(KB):
                    ins = nc.tensor.matmul(k.banks[0:RANK, 6 + h, :], lra_w[:, b, :], k.hT[:, b, h * 512:(h + 1) * 512],
                                           start=(b == 0), stop=(b == KB - 1))
                ins.then_inc(lra_mm, 1)
            proj.pe_jobs(pe, 0, 8)
            pe.wait_ge(lra_st, 2)
            for g in range(2):
                if g:
                    proj.pe_jobs(pe, 8, 16)
                    pe.wait_ge(z_st, 2)
                for h in range(2):
                    nc.tensor.matmul(k.banks[:, 6 + h, :], gate2[:, g * P:(g + 1) * P], lraT[:, h * 512:(h + 1) * 512],
                                     start=True, stop=True).then_inc(z_mm, 1)
            proj.pe_jobs(pe, 16, 24)

        @block.vector
        def _(dve):
            def negated(g):
                for h in range(2):
                    dve.wait_ge(z_mm, 2 * g + h + 1)
                    nc.vector.tensor_scalar(m.t0[:, g, h * 512:(h + 1) * 512], k.banks[:, 6 + h, :], bias[:, g:g + 1], -1.0,
                                            ALU.add, ALU.mult).then_inc(z_st, 1)
            dve.wait_ge(vec_in, 64)
            run_stores_range(nc, proj, dve, "dve", 0, 8)
            negated(0)
            run_stores_range(nc, proj, dve, "dve", 8, 16)
            negated(1)
            dve.wait_ge(a.sem, 3)
            dve.wait_ge(z_st, 4)
            n = d.mark(nc.vector.scalar_tensor_tensor(out=m.t1[:, :, :], in0=m.t0[:, :, :], scalar=0.0, in1=m.t1[:, :, :],
                                                      op0=ALU.max, op1=ALU.add))
            dve.wait_ge(d.sem, n)
            n = d.mark(nc.vector.tensor_scalar(m.t1[:, :, :], m.t1[:, :, :], -1.0 / GLA_TAU, None, ALU.mult))
            dve.wait_ge(d.sem, n)
            summed_decay_dve(nc, dve, m, d)


def run_stores_range(nc, proj, eng, who, lo, hi):
    for j in range(lo, hi):
        job = proj.jobs[j]
        if job["by"] != who:
            continue
        width = job["width"] if job["kind"] == "tokens" else 512
        eng.wait_ge(proj.done, j + 1)
        store = store_act if who == "act" else store_dve
        store(nc, job_out(job), proj.bank(j)[:, 0:width], job["how"]).then_inc(proj.stored[who], 1)


def stage_hgrn_projection(nc, k):
    m = k.hgrn = Mixer(k, "hgrn", 64)
    lg, ex, tot, pr, lb, om = (k.small[:, c:c + 2] for c in (66, 68, 70, 72, 74, 76))
    jobs = []
    for g in range(2):
        jobs += feature_jobs(k.c_qfb, g * P, m.qT[:, g, :], "silu", "act")
    for g in range(2):
        jobs += feature_jobs(k.c_qfb, 256 + g * P, m.t2[:, g, :], "copy", "dve")
    jobs += token_jobs(k.c_igb, 0, 256, lambda i: m.v[:, i, :])
    jobs += token_jobs(k.c_igb, 256, 256, lambda i: m.g[:, i, :], "silu", "act")
    proj = Projection(nc, k, "hgrn_proj", jobs)
    vec_in = k.sem("hgrn_vec_in")
    a, d = Steps(k, "hgrn_act"), Steps(k, "hgrn_dve")
    with nc.Block() as block:
        @block.sync
        def _(sp):
            k.w.load_up_to(sp, k.c_qkc + 1)

        @block.scalar
        def _(act):
            act.dma_start(lg, k.hgrn_lb_logits[0].rearrange("(k p) -> p k", p=P), allow_slow_non_contiguous=True).then_inc(vec_in, 16)
            act.dma_start(m.gain[:, :], k.hgrn_norm_w[0].partition_broadcast(P)).then_inc(vec_in, 16)
            run_stores_range(nc, proj, act, "act", 0, 4)
            act.wait_ge(proj.stored["dve"], 4)
            a.mark(nc.scalar.activation(m.kT[:, :, :], m.t2[:, :, :], ACT.Sigmoid, scale=-1.0))
            a.mark(nc.scalar.activation(m.t1[:, :, :], m.t2[:, :, :], ACT.Abs))
            act.wait_ge(d.sem, 1)
            a.mark(nc.scalar.activation(ex, tot, ACT.Exp))
            act.wait_ge(a.sem, 2)
            a.mark(nc.scalar.activation(m.t1[:, :, :], m.t1[:, :, :], ACT.Exp, scale=-1.0))
            act.wait_ge(a.sem, 4)
            a.mark(nc.scalar.activation(m.t1[:, :, :], m.t1[:, :, :], ACT.Ln, bias=1.0))
            act.wait_ge(a.sem, 5)
            a.mark(nc.scalar.activation(m.t0[:, :, :], m.t2[:, :, :], ACT.Exp, scale=-1.0))
            act.wait_ge(d.sem, 8)
            a.mark(nc.scalar.activation(m.t0[:, :, :], m.t0[:, :, :], ACT.Ln))
            run_stores_range(nc, proj, act, "act", 4, len(jobs))

        @block.tensor
        def _(pe):
            proj.pe_jobs(pe, 0, len(jobs))

        @block.vector
        def _(dve):
            run_stores_range(nc, proj, dve, "dve", 0, 8)
            dve.wait_ge(vec_in, 32)
            d.mark(nc.vector.tensor_tensor(tot, lg, lg, ALU.subtract))
            dve.wait_ge(a.sem, 3)
            d.mark(nc.vector.reciprocal(tot, ex))
            dve.wait_ge(d.sem, 2)
            d.mark(nc.vector.tensor_tensor(pr, ex, tot, ALU.mult))
            dve.wait_ge(d.sem, 3)
            d.mark(nc.vector.tensor_tensor(lb, pr, pr, ALU.subtract))
            dve.wait_ge(d.sem, 4)
            d.mark(nc.vector.tensor_scalar(om, lb, -1.0, 1.0, ALU.mult, ALU.add))
            dve.wait_ge(a.sem, 6)
            for g in range(2):
                d.mark(nc.vector.tensor_scalar(m.t0[:, g, :], m.t0[:, g, :], 3e38, lb[:, g:g + 1], ALU.min, ALU.mult))
            dve.wait_ge(d.sem, 7)
            n = d.mark(nc.vector.tensor_scalar(m.t0[:, :, :], m.t0[:, :, :], 1.0, 1.0, ALU.add, ALU.mult))
            for g in range(2):
                d.mark(nc.vector.tensor_scalar(m.kT[:, g, :], m.kT[:, g, :], om[:, g:g + 1], None, ALU.mult))
            n = d.mark(nc.vector.scalar_tensor_tensor(out=m.t1[:, :, :], in0=m.t2[:, :, :], scalar=0.0, in1=m.t1[:, :, :],
                                                      op0=ALU.min, op1=ALU.subtract))
            dve.wait_ge(a.sem, 7)
            dve.wait_ge(d.sem, n)
            n = d.mark(nc.vector.tensor_tensor(m.t1[:, :, :], m.t1[:, :, :], m.t0[:, :, :], ALU.add))
            dve.wait_ge(d.sem, n)
            summed_decay_dve(nc, dve, m, d)
            run_stores_range(nc, proj, dve, "dve", 8, len(jobs))


def stage_gated_attention(nc, k, m, first_block):
    dv, nm = m.dv, m.name
    p = k.place
    E = p(f"{nm}_decay", [P, 2, T], 160)
    C = p(f"{nm}_level", [P, 2, T], 168)
    S = p(f"{nm}_scores", [P, 2, NT, P], 176)
    O = p(f"{nm}_out", [P, NT, 2 * dv], 184)
    ktok = p(f"{nm}_k_tokens", [P, NT, P], 192)
    ST = p(f"{nm}_state", [P, NT, dv], 196)
    qe = p(f"{nm}_q_decayed", [P, T], 200)
    ke = p(f"{nm}_k_decayed", [P, T], 204)
    sq = p(f"{nm}_squares", [P, NT, 2 * dv], 160)
    dec = k.small[:, 80:88]
    ssq, ms, root, rstd = (k.small[:, c:c + 16] for c in (96, 112, 128, 144))
    nob = 2 * dv // P
    per = 512 // dv
    nper = NT // per
    nbk = 2 * nper
    sname = lambda n: k.sem(f"{nm}_{n}")
    diff, expd, level, score, picked = sname("diff"), sname("exp"), sname("level"), sname("score"), sname("picked")
    pre, eb, kd = sname("state_diff"), sname("state_exp"), sname("state_scaled")
    kt_mm, kt_st, u_mm, rec = sname("k_turned"), sname("k_stored"), sname("state_added"), sname("state_done")
    o_mm, o_st, turned, t_st = sname("o_product"), sname("o_stored"), sname("o_turned"), sname("oT_stored")
    pl, dn, an = Steps(k, f"{nm}_pool_norm"), Steps(k, f"{nm}_dve_norm"), Steps(k, f"{nm}_act_norm")
    bank = lambda b: k.banks[:, b, :]

    def halves(ap2d, h):
        return ap2d.rearrange("p (n two h) -> p n two h", two=2, h=h)

    def store_turned(b, g, act):
        fb, half = b // 2, b % 2
        src = bank((4 if g == 0 else 0) + b)
        nc.scalar.activation(k.oT[:, first_block + nob * g + fb, half * 512:(half + 1) * 512], src, ACT.Copy).then_inc(t_st, 1)

    with nc.Block() as block:
        @block.gpsimd
        def _(pool):
            gv = m.g[:, :, :].rearrange("p i (h v) -> p (i h) v", v=dv)
            pl.mark(pool.tensor_tensor(gv, gv, m.gain[:, :].unsqueeze(1).to_broadcast([P, 4 * NT, dv]), ALU.mult))
            for g in range(2):
                pool.wait_ge(eb, 3 * g + 1)
                if g:
                    pool.wait_ge(o_mm, nbk)
                pool.wait_ge(pre, 3 * g + 3)
                pool.tensor_tensor(qe[:, :], qe[:, :], m.qT[:, g, :], ALU.mult).then_inc(kd, 1)
                pool.wait_ge(eb, 3 * g + 2)
                pool.tensor_tensor(ke[:, :], ke[:, :], m.kT[:, g, :], ALU.mult).then_inc(kd, 1)
                for l in range(7):
                    s, h = 7 * g + l, 1 << l
                    pool.wait_ge(expd, s + 1)
                    if s >= 2:
                        pool.wait_ge(score, 4 * (8 * ((s - 2) // 7) + (s - 2) % 7 + 2))
                    e, c = halves(E[:, s % 2, :], h), halves(C[:, s % 2, :], h)
                    q, kk = halves(m.qT[:, g, :], h), halves(m.kT[:, g, :], h)
                    pool.tensor_tensor(c[:, :, 0, :], e[:, :, 0, :], kk[:, :, 0, :], ALU.mult).then_inc(level, 1)
                    pool.tensor_tensor(c[:, :, 1, :], e[:, :, 1, :], q[:, :, 1, :], ALU.mult).then_inc(level, 1)
                pool.wait_ge(o_st, nbk * (g + 1))
                pool.wait_ge(level, 14 * (g + 1))
                pl.mark(pool.tensor_tensor(sq[:, :, :], O[:, :, :], O[:, :, :], ALU.mult))

        @block.scalar
        def _(act):
            for g in range(2):
                if g:
                    act.wait_ge(o_mm, nbk)
                nc.scalar.activation(qe[:, :], m.bT[:, g, :], ACT.Exp).then_inc(eb, 1)
                act.wait_ge(pre, 3 * g + 1)
                nc.scalar.activation(ke[:, :], ke[:, :], ACT.Exp).then_inc(eb, 1)
                nc.scalar.activation(dec, m.bT[:, g, :].rearrange("p (i t) -> p i t", t=P)[:, :, P - 1], ACT.Exp).then_inc(eb, 1)
                for l in range(7):
                    s = 7 * g + l
                    act.wait_ge(diff, 2 * (s + 1))
                    nc.scalar.activation(E[:, s % 2, :], E[:, s % 2, :], ACT.Exp).then_inc(expd, 1)
                    if l == 0:
                        for h in range(2):
                            act.wait_ge(kt_mm, 2 * g + h + 1)
                            nc.scalar.activation(ktok[:, 4 * h:4 * h + 4, :], bank(h).rearrange("p (i t) -> p i t", t=P),
                                                 ACT.Copy).then_inc(kt_st, 1)
                if g:
                    for b in range(nob * 2):
                        act.wait_ge(turned, b + 1)
                        store_turned(b, 0, act)
                for b in range(nbk):
                    act.wait_ge(o_mm, nbk * g + b + 1)
                    if b == 0 and g:
                        act.wait_ge(turned, nob * 2)
                    ib, hh = b // 2, b % 2
                    nc.scalar.activation(O[:, ib * per:(ib + 1) * per, hh * dv:(hh + 1) * dv],
                                         bank(4 + hh * nper + ib).rearrange("p (i v) -> p i v", i=per),
                                         ACT.Copy).then_inc(o_st, 1)
                act.wait_ge(dn.sem, 5 * g + 2)
                an.mark(nc.scalar.activation(root, ms, ACT.Sqrt))
            for b in range(nob * 2):
                act.wait_ge(turned, nob * 2 + b + 1)
                store_turned(b, 1, act)

        @block.tensor
        def _(pe):
            def turn_out(g):
                pe.wait_ge(dn.sem, 5 * (g + 1))
                for b in range(nob * 2):
                    fb, half = b // 2, b % 2
                    for i in range(4):
                        ins = nc.tensor.transpose(bank((4 if g == 0 else 0) + b)[:, i * P:(i + 1) * P],
                                                  O[:, 4 * half + i, fb * P:(fb + 1) * P], k.ident[:, :])
                    ins.then_inc(turned, 1)

            for g in range(2):
                pe.wait_ge(kd, 2 * g + 2)
                if g:
                    pe.wait_ge(picked, 32)
                for i in range(NT):
                    ins = nc.tensor.transpose(bank(i // 4)[:, (i % 4) * P:(i % 4 + 1) * P], ke[:, i * P:(i + 1) * P], k.ident[:, :])
                    if i % 4 == 3:
                        ins.then_inc(kt_mm, 1)
                def add_state():
                    pe.wait_ge(kt_st, 2 * g + 2)
                    for i in range(NT):
                        for hh in range(2):
                            c = i * dv
                            ins = nc.tensor.matmul(bank(2 + c // 512)[64 * hh:64 * hh + 64, c % 512:c % 512 + dv],
                                                   ktok[:, i, 64 * hh:64 * hh + 64],
                                                   m.v[:, i, (2 * g + hh) * dv:(2 * g + hh + 1) * dv], start=True, stop=True)
                    ins.then_inc(u_mm, 1)
                for st in range(8):
                    s = 8 * g + st
                    base = 4 if s % 2 == 0 else 0
                    if st == 1:
                        pe.wait_ge(rec, NT * (g + 1))
                    if st > 0:
                        pe.wait_ge(level, 2 * (7 * g + st))
                    if st == 0 and g:
                        pe.wait_ge(o_st, nbk * g)
                    if st >= 2:
                        pe.wait_ge(picked, 4 * (s - 1))
                    for half in range(2):
                        for i in range(4 * half, 4 * half + 4):
                            for hh in range(2):
                                rows, tok = slice(64 * hh, 64 * hh + 64), slice(i * P, (i + 1) * P)
                                a = m.kT[rows, g, tok] if st == 0 else C[rows, (7 * g + st - 1) % 2, tok]
                                b = m.qT[rows, g, tok] if st == 0 else a
                                ins = nc.tensor.matmul(bank(base + 2 * hh + half)[:, (i % 4) * P:(i % 4 + 1) * P], a, b,
                                                       start=True, stop=True)
                                if i == 4 * half + 3:
                                    ins.then_inc(score, 1)
                    if st == 0:
                        add_state()
                if g:
                    pe.wait_ge(picked, 4 * 15)
                    turn_out(0)
                    pe.wait_ge(t_st, nob * 2)
                pe.wait_ge(picked, 32 * (g + 1))
                for i in range(NT):
                    for hh in range(2):
                        rows, tok = slice(64 * hh, 64 * hh + 64), slice(i * P, (i + 1) * P)
                        c = (i % per) * dv
                        out = bank(4 + hh * nper + i // per)[:, c:c + dv]
                        vv = m.v[:, i, (2 * g + hh) * dv:(2 * g + hh + 1) * dv]
                        ins = nc.tensor.matmul(out, S[:, hh, i, :], vv, start=True, stop=(i == 0))
                        if i:
                            ins = nc.tensor.matmul(out, qe[rows, tok], ST[rows, i, :], start=False, stop=True)
                        if i % per == per - 1:
                            ins.then_inc(o_mm, 1)
            turn_out(1)

        @block.vector
        def _(dve):
            for g in range(2):
                b3 = m.bT[:, g, :].rearrange("p (i t) -> p i t", t=P)
                if g:
                    dve.wait_ge(kt_mm, 2)
                nc.vector.tensor_tensor(ke[:, :].rearrange("p (i t) -> p i t", t=P),
                                        b3[:, :, P - 1:P].to_broadcast([P, NT, P]), b3, ALU.subtract).then_inc(pre, 1)

                def differences(l):
                    s, h = 7 * g + l, 1 << l
                    nb = T // (2 * h)
                    b4, e = halves(m.bT[:, g, :], h), halves(E[:, s % 2, :], h)
                    mid = b4[:, :, 0, h - 1:h].to_broadcast([P, nb, h])
                    if s >= 2:
                        dve.wait_ge(level, 2 * (s - 1))
                    nc.vector.tensor_tensor(e[:, :, 0, :], mid, b4[:, :, 0, :], ALU.subtract).then_inc(diff, 1)
                    nc.vector.tensor_tensor(e[:, :, 1, :], b4[:, :, 1, :], mid, ALU.subtract).then_inc(diff, 1)

                differences(0)
                differences(1)
                nc.vector.memset(ST[:, 0, :], 0.0).then_inc(pre, 1) if g == 0 else nc.vector.memset(k.small[:, 79:80], 0.0).then_inc(pre, 1)
                dve.wait_ge(eb, 3 * g + 3)
                nc.vector.tensor_copy(k.small[:, 88:96], dec).then_inc(pre, 1)
                for st in range(8):
                    s = 8 * g + st
                    base = 4 if s % 2 == 0 else 0
                    for half in range(2):
                        for hh in range(2):
                            n = 4 * s + 2 * half + hh
                            dve.wait_ge(score, n + 1)
                            src = bank(base + 2 * hh + half).rearrange("p (i t) -> p i t", t=P)
                            dst = S[:, hh, 4 * half:4 * half + 4, :]
                            if st == 0:
                                if g:
                                    dve.wait_ge(o_mm, nbk)
                                nc.vector.tensor_tensor(dst, src, k.ident[:, :].unsqueeze(1).to_broadcast([P, 4, P]),
                                                        ALU.mult).then_inc(picked, 1)
                            else:
                                dve.wait_ge(picked, n - 3)
                                mask = k.levels[:, st - 1, :].bitcast(U32).unsqueeze(1).to_broadcast([P, 4, P])
                                nc.vector.copy_predicated(dst, mask, src).then_inc(picked, 1)
                    if st == 0:
                        dve.wait_ge(u_mm, g + 1)
                        if g:
                            dve.wait_ge(o_mm, nbk)
                        n0 = NT * g
                        for i in range(NT - 1):
                            c = i * dv
                            u = bank(2 + c // 512)[:, c % 512:c % 512 + dv]
                            if i == 0:
                                nc.vector.tensor_copy(ST[:, 1, :], u).then_inc(rec, 1)
                            else:
                                dve.wait_ge(rec, n0 + i)
                                nc.vector.scalar_tensor_tensor(out=ST[:, i + 1, :], in0=ST[:, i, :],
                                                               scalar=k.small[:, 88 + i:89 + i], in1=u,
                                                               op0=ALU.mult, op1=ALU.add).then_inc(rec, 1)
                        nc.vector.memset(k.small[:, 78:79], 0.0).then_inc(rec, 1)
                    if 1 <= st <= 5:
                        differences(st + 1)
                dve.wait_ge(pl.sem, g + 2)
                v3 = lambda ap: ap.rearrange("p i (h v) -> p (i h) v", v=dv)
                dn.mark(nc.vector.tensor_reduce(ssq, v3(sq[:, :, :]), AX.X, ALU.add))
                dve.wait_ge(dn.sem, 5 * g + 1)
                dn.mark(nc.vector.tensor_scalar(ms, ssq, 1.0 / dv, EPS, ALU.mult, ALU.add))
                dve.wait_ge(an.sem, g + 1)
                dn.mark(nc.vector.reciprocal(rstd, root))
                dve.wait_ge(dn.sem, 5 * g + 3)
                dn.mark(nc.vector.tensor_tensor(v3(O[:, :, :]), v3(O[:, :, :]), rstd.unsqueeze(2).to_broadcast([P, 16, dv]), ALU.mult))
                dve.wait_ge(dn.sem, 5 * g + 4)
                dn.mark(nc.vector.tensor_tensor(O[:, :, :], O[:, :, :], m.g[:, :, 2 * g * dv:(2 * g + 2) * dv], ALU.mult))


def stage_stick_projection(nc, k):
    p = k.place
    k.sb_qT, k.sb_kT = p("sb_qT", [P, 2, T], 104), p("sb_kT", [P, 2, T], 112)
    k.sb_v, k.sb_gT = p("sb_v", [P, NT, 256], 120), p("sb_gT", [P, 2, T], 128)
    jobs = []
    for g in range(2):
        jobs += feature_jobs(k.c_qkc, g * P, k.sb_qT[:, g, :])
    for g in range(2):
        jobs += feature_jobs(k.c_qkc, 256 + g * P, k.sb_kT[:, g, :])
    jobs += token_jobs(k.c_vgc, 0, 256, lambda i: k.sb_v[:, i, :])
    for g in range(2):
        jobs += feature_jobs(k.c_vgc, 256 + g * P, k.sb_gT[:, g, :], "silu", "act")
    proj = Projection(nc, k, "stick_proj", jobs)
    with nc.Block() as block:
        @block.sync
        def _(sp):
            k.w.load_up_to(sp, k.c_out[1])

        @block.scalar
        def _(act):
            run_stores(nc, proj, act, "act")

        @block.tensor
        def _(pe):
            proj.pe_jobs(pe, 0, len(jobs))

        @block.vector
        def _(dve):
            run_stores(nc, proj, dve, "dve")


def stage_stick_attention(nc, k):
    p = k.place
    A = p("sb_softplus", [P, 2, T], 136)
    B = p("sb_weight", [P, 2, T], 144)
    WT = p("sb_weightT", [P, 2, NT, P], 152)
    neg = p("strict_bias", [P, P], 6.5)
    items = [(i, h) for i in range(NT) for h in range(4)]
    N = len(items)
    nb = [2 if i >= 4 else 1 for i, h in items]
    upto = [sum(nb[:n + 1]) for n in range(N)]
    two = [sum(b == 2 for b in nb[:n + 1]) for n in range(N)]
    s = lambda n: k.sem("sb_" + n)
    z_mm, e_done, capped, l_done, logit, w_done = s("z"), s("exp"), s("capped"), s("ln"), s("logit"), s("w")
    t_mm, wt_act, wt_dve, pv, o_done = s("turned"), s("wT_act"), s("wT_dve"), s("out"), s("out_stored")
    d = Steps(k, "sb_dve")
    x_in = k.kept_sem("x_again")
    k.x_again = x_in
    k.xres = p("x_residual", [P, NT, D], 160)
    sc = DK ** -0.5

    def width(n):
        return (items[n][0] + 1) * P

    def z(n):
        return k.banks[:, 2 * (n % 2):2 * (n % 2) + 2, :].rearrange("p b c -> p (b c)")[:, 0:width(n)]

    with nc.Block() as block:
        @block.sync
        def _(sp):
            sp.dma_start(k.xres[:, :, :], k.x[0].rearrange("(i p) d -> p i d", p=P)).then_inc(x_in, 16)

        @block.scalar
        def _(act):
            def exponentials(n):
                w = width(n)
                act.wait_ge(z_mm, n + 1)
                if n >= 2:
                    act.wait_ge(logit, n - 1)
                nc.scalar.activation(A[:, n % 2, 0:w], z(n), ACT.Exp, scale=sc).then_inc(e_done, 1)
                act.wait_ge(capped, n + 1)
                nc.scalar.activation(A[:, n % 2, 0:w], A[:, n % 2, 0:w], ACT.Ln, bias=1.0).then_inc(l_done, 1)

            exponentials(0)
            for n in range(N):
                w = width(n)
                if n + 1 < N:
                    exponentials(n + 1)
                act.wait_ge(logit, n + 1)
                nc.scalar.activation(B[:, n % 2, 0:w], B[:, n % 2, 0:w], ACT.Exp).then_inc(w_done, 1)
                act.wait_ge(t_mm, (upto[n - 1] if n else 0) + 1)
                if n >= 2:
                    act.wait_ge(pv, n - 1)
                m = min(items[n][0] + 1, 4)
                nc.scalar.activation(WT[:, n % 2, 0:m, :], k.banks[:, 4, 0:m * P].rearrange("p (j t) -> p j t", t=P),
                                     ACT.Copy).then_inc(wt_act, 1)

        @block.tensor
        def _(pe):
            def scores(n):
                i, h = items[n]
                rows, w = slice(64 * (h % 2), 64 * (h % 2) + 64), width(n)
                if n >= 2:
                    pe.wait_ge(logit, n - 1)
                for c in range(0, w, 512):
                    e = min(w, c + 512)
                    ins = nc.tensor.matmul(z(n)[:, c:e], k.sb_qT[rows, h // 2, i * P:(i + 1) * P],
                                           k.sb_kT[rows, h // 2, c:e], start=True, stop=True)
                ins.then_inc(z_mm, 1)

            scores(0)
            scores(1)
            for n, (i, h) in enumerate(items):
                if n + 2 < N:
                    scores(n + 2)
                pe.wait_ge(w_done, n + 1)
                for j in range(i + 1):
                    if j == 0 and n:
                        pe.wait_ge(wt_act, n)
                    if j == 4 and two[n] > 1:
                        pe.wait_ge(wt_dve, two[n] - 1)
                    ins = nc.tensor.transpose(k.banks[:, 4 + j // 4, (j % 4) * P:(j % 4 + 1) * P],
                                              B[:, n % 2, j * P:(j + 1) * P], k.ident[:, :])
                    if j == min(i, 3) or j == i:
                        ins.then_inc(t_mm, 1)
                if n >= 2:
                    pe.wait_ge(o_done, n - 1)
                out = k.banks[64 * (h % 2):64 * (h % 2) + 64, 6 + n % 2, 0:P]
                for j in range(i + 1):
                    if j == 0:
                        pe.wait_ge(wt_act, n + 1)
                    if j == 4:
                        pe.wait_ge(wt_dve, two[n])
                    ins = nc.tensor.matmul(out, k.sb_v[:, j, h * 64:(h + 1) * 64], WT[:, n % 2, j, :],
                                           start=(j == 0), stop=(j == i))
                ins.then_inc(pv, 1)

        @block.vector
        def _(dve):
            c0 = d.mark(nc.vector.tensor_scalar(neg[:, :], k.strict[:, :], 1.0, -MASKED, ALU.subtract, ALU.mult))

            def cap(n):
                w = width(n)
                dve.wait_ge(e_done, n + 1)
                nc.vector.tensor_scalar(A[:, n % 2, 0:w], A[:, n % 2, 0:w], 1e35, None, ALU.min).then_inc(capped, 1)

            def store(n):
                i, h = items[n]
                if nb[n] == 2:
                    dve.wait_ge(t_mm, upto[n])
                    if two[n] > 2:
                        dve.wait_ge(pv, n - 1)
                    nc.vector.tensor_copy(WT[:, n % 2, 4:i + 1, :],
                                          k.banks[:, 5, 0:(i - 3) * P].rearrange("p (j t) -> p j t", t=P)).then_inc(wt_dve, 1)
                dve.wait_ge(pv, n + 1)
                rows = slice(64 * (h % 2), 64 * (h % 2) + 64)
                tok = slice(i * P, (i + 1) * P)
                nc.vector.tensor_tensor(k.oT[rows, 6 + h // 2, tok], k.banks[rows, 6 + n % 2, 0:P],
                                        k.sb_gT[rows, h // 2, tok], ALU.mult).then_inc(o_done, 1)

            cap(0)
            for n, (i, h) in enumerate(items):
                w = width(n)
                if n + 1 < N:
                    cap(n + 1)
                a, b = A[:, n % 2, 0:w], B[:, n % 2, 0:w]
                dve.wait_ge(l_done, n + 1)
                c = d.mark(nc.vector.scalar_tensor_tensor(out=a, in0=z(n), scalar=sc, in1=a, op0=ALU.mult, op1=ALU.max))
                dve.wait_ge(d.sem, c)
                c = d.mark(nc.vector.tensor_tensor(a[:, w - P:w], a[:, w - P:w], k.strict[:, :], ALU.mult))
                dve.wait_ge(d.sem, c)
                if n >= 2:
                    dve.wait_ge(t_mm, upto[n - 2])
                c = d.mark(nc.vector.tensor_tensor_scan(b[:, ::-1], a[:, ::-1], a[:, ::-1], 0.0, ALU.add, ALU.max))
                dve.wait_ge(d.sem, c)
                c = d.mark(nc.vector.scalar_tensor_tensor(out=b, in0=z(n), scalar=sc, in1=b, op0=ALU.mult, op1=ALU.subtract))
                dve.wait_ge(d.sem, c)
                nc.vector.tensor_tensor(b[:, w - P:w], b[:, w - P:w], neg[:, :], ALU.add).then_inc(logit, 1)
                if n:
                    store(n - 1)
            store(N - 1)


def stage_first_output(nc, k):
    p = k.place
    x = k.xres
    fnw = p("final_norm_row", [P, D], 104)
    tmp = p("gated_y", [P, 2, 512], 108)
    mixg = k.small[:, 160:168]
    sq1, ms1, rt1, rs1 = (k.small[:, c:c + 8] for c in (168, 176, 184, 192))
    jobs = [dict(chunk=k.c_out[h], kind="tokens", tile=i, col=0, width=512, by="dve", dest=h, how="gate")
            for i in range(NT) for h in range(2)]
    proj = Projection(nc, k, "first_out", jobs, banks=6, src=k.oT)
    norm = NormTranspose(nc, k, "norm2", x, k.hT, p("x1_normed", [P, NT, D], 112))
    s = lambda n: k.sem(n)
    vec_in, added, summed, gained, x1_done = s("fnw_in"), s("residual_added"), s("x1_summed"), s("hT_gained"), s("x1_done")
    x1_out = k.sem("x1_out")
    d = Steps(k, "first_out_dve")
    a = Steps(k, "first_out_act")
    with nc.Block() as block:
        @block.sync
        def _(sp):
            sp.wait_ge(x1_done, NT)
            sp.dma_start(k.x1_dram.rearrange("(i p) d -> p i d", p=P), x[:, :, :]).then_inc(x1_out, 16)
            k.w.load_up_to(sp, k.c_akv)
            sp.wait_ge(x1_out, 16)

        @block.gpsimd
        def _(pool):
            pool.wait_ge(k.x_again, 16)
            for j, job in enumerate(jobs):
                i, h = job["tile"], job["dest"]
                pool.wait_ge(proj.stored["dve"], j + 1)
                xs = x[:, i, h * 512:(h + 1) * 512]
                pool.tensor_tensor(xs, xs, tmp[:, j % 2, :], ALU.add).then_inc(added, 1)

        @block.scalar
        def _(act):
            act.dma_start(fnw[:, :], k.final_norm_w.partition_broadcast(P)).then_inc(vec_in, 16)
            act.dma_start(mixg, k.norm_mix_g_2[0].rearrange("(k p) -> p k", p=P), allow_slow_non_contiguous=True).then_inc(vec_in, 16)
            for i in range(NT):
                act.wait_ge(added, 2 * i + 2)
                nc.scalar.activation(k.hT[:, i, :], x[:, i, :], ACT.Square, accum_out=sq1[:, i:i + 1]).then_inc(summed, 1)
            act.wait_ge(d.sem, 1)
            a.mark(nc.scalar.activation(rt1, ms1, ACT.Sqrt))
            act.wait_ge(summed, NT)
            norm.act_stats(act, lambda e, i: e.wait_ge(x1_done, i + 1))
            norm.store(act, 0)

        @block.tensor
        def _(pe):
            proj.pe_jobs(pe, 0, len(jobs))
            pe.wait_ge(proj.stored["dve"], len(jobs))
            norm.pe_transpose(pe)

        @block.vector
        def _(dve):
            for j, job in enumerate(jobs):
                dve.wait_ge(proj.done, j + 1)
                if j >= 2:
                    dve.wait_ge(added, j - 1)
                h = job["dest"]
                nc.vector.tensor_tensor(tmp[:, j % 2, :], proj.bank(j), k.gate_row[:, h * 512:(h + 1) * 512],
                                        ALU.mult).then_inc(proj.stored["dve"], 1)
            dve.wait_ge(summed, NT)
            d.mark(nc.vector.tensor_scalar(ms1, sq1, 1.0 / D, EPS, ALU.mult, ALU.add))
            dve.wait_ge(a.sem, 1)
            n = d.mark(nc.vector.reciprocal(rs1, rt1))
            dve.wait_ge(d.sem, n)
            dve.wait_ge(vec_in, 32)
            dve.wait_ge(added, 16)
            for i in range(NT):
                nc.vector.scalar_tensor_tensor(out=x[:, i, :], in0=x[:, i, :], scalar=rs1[:, i:i + 1], in1=fnw[:, :],
                                               op0=ALU.mult, op1=ALU.mult).then_inc(x1_done, 1)
            norm.dve_stats(dve)
            norm.dve_divide(dve)
            norm.store(dve, 1)
            dve.wait_ge(norm.by_act, NT)
            dve.wait_ge(norm.by_dve, NT)
            for b in range(KB):
                nc.vector.tensor_scalar(k.hT[:, b, :], k.hT[:, b, :], mixg[:, b:b + 1], None, ALU.mult).then_inc(gained, 1)


def rope_dve(nc, dve, d, x1, x2, cos, sin, t):
    V = nc.vector
    d.mark(V.tensor_tensor(t[0], x1, cos, ALU.mult))
    d.mark(V.tensor_tensor(t[1], x2, sin, ALU.mult))
    d.mark(V.tensor_tensor(t[2], x1, sin, ALU.mult))
    n = d.mark(V.tensor_tensor(t[3], x2, cos, ALU.mult))
    dve.wait_ge(d.sem, n)
    d.mark(V.tensor_tensor(x1, t[0], t[1], ALU.subtract))
    return d.mark(V.tensor_tensor(x2, t[2], t[3], ALU.add))


def stage_second_projection(nc, k):
    p = k.place
    aq = p("aq_tok", [P, NT, 512], 72)
    k.akv = p("akv_tok", [P, NT, 256], 88)
    iq = p("iq_tok", [P, NT, 512], 96)
    mix = p("mix_tok", [P, NT, GTA - IK], 112)
    k.cos, k.sin = p("cos_table", [P, NT, 24], 0.5), p("sin_table", [P, NT, 24], 1.25)
    k.aqT, k.iqT = p("aqT", [P, 4, T], 129), p("iqT", [P, 4, T], 145)
    k.akT, k.ikT = p("akT", [P, 2, T], 161), p("ikT", [P, T], 169)
    k.cqT, k.ckvT, k.krT = p("cqT", [P, 2, T], 173), p("ckvT", [P, T], 181), p("krT", [P, T], 185)
    sq = p("mix_squares", [P, NT, 456], 189)
    t4 = p("rope_products", [P, 4, 512], 203.5)
    ik2 = p("ik_twice", [P, NT, P], 211.5)
    ak4 = p("ak_twice", [P, NT, 256], 189)
    sm = k.small
    k.posq, k.iw = p("pos_col", [P, NT], 7), p("iw", [P, NT, 8], 7.0625)
    posi = sm[:, 200:208].bitcast(I32)
    inv = p("inv_freq", [P, 24], 7.375)
    ikg = p("ik_gain", [P, 64], 7.5)
    qg, kvg = sm[:, 208:210], sm[:, 210:211]
    ms, rt, rs = p("mix_mean", [P, 3, NT], 7.875), p("mix_root", [P, 3, NT], 6.0), p("mix_rstd", [P, 3, NT], 6.125)
    r, turns, ab, angv = (t4[:, c, 0:192].rearrange("p (i f) -> p i f", i=NT) for c in range(4))
    c_ik, c_iw, c_cq, c_ckv, c_kr = 0, IW - IK, CQ - IK, CKV - IK, KR - IK
    jobs = token_jobs(k.c_aq, 0, 512, lambda i: aq[:, i, :], 64 ** -0.5)
    jobs += token_jobs(k.c_akv, 0, 256, lambda i: k.akv[:, i, :])
    jobs += token_jobs(k.c_iq, 0, 512, lambda i: iq[:, i, :], 64 ** -0.5)
    jobs += token_jobs(k.c_mix, 0, GTA - IK, lambda i: mix[:, i, :])
    proj = Projection(nc, k, "second_proj", jobs)
    s = lambda n: k.sem(n)
    vec_in, table, rooted, copies, turned = s("second_vec_in"), s("angles"), s("mix_rooted"), s("twice"), s("heads_turned")
    by_act, by_dve, ready = s("heads_act"), s("heads_dve"), s("heads_ready")
    d = Steps(k, "second_dve")
    pl = Steps(k, "second_pool")
    C1 = 6.28125
    C2 = float(np.float32(np.round((2 * math.pi - C1) * 2 ** 20) / 2 ** 20))
    C3 = float(np.float32(2 * math.pi - C1 - C2))
    MAGIC = 1.5 * 2 ** 23
    freq = [float(THETA ** (-np.float32(2 * j) / np.float32(16))) for j in range(8)]
    freq += [float(THETA ** (-np.float32(2 * j) / np.float32(32))) for j in range(16)]

    with nc.Block() as block:
        @block.sync
        def _(sp):
            k.w.load_up_to(sp, k.c_gate[1])

        @block.gpsimd
        def _(pool):
            for f, v in enumerate(freq):
                pool.memset(inv[:, f:f + 1], v).then_inc(pl.sem, 1)
            pool.wait_ge(ready, 1)
            pool.tensor_copy(ik2[:, :, :].rearrange("p i (two f) -> p i two f", two=2),
                             mix[:, :, 0:64].unsqueeze(2).to_broadcast([P, NT, 2, 64])).then_inc(copies, 1)
            pool.wait_ge(ready, 2)
            for g in range(2):
                pool.tensor_copy(ak4[:, :, g * P:(g + 1) * P].rearrange("p i (two f) -> p i two f", two=2),
                                 k.akv[:, :, g * 64:(g + 1) * 64].unsqueeze(2).to_broadcast([P, NT, 2, 64])).then_inc(copies, 1)

        @block.scalar
        def _(act):
            slow = dict(allow_slow_non_contiguous=True)
            act.dma_start(posi, k.positions_2[0].rearrange("(i p) -> p i", p=P), **slow).then_inc(vec_in, 16)
            act.dma_start(ikg[:, :], k.idx_k_norm_g_2[0].partition_broadcast(P)).then_inc(vec_in, 16)
            act.dma_start(qg, k.q_a_norm_g_2[0].rearrange("(k p) -> p k", p=P), **slow).then_inc(vec_in, 16)
            act.dma_start(kvg, k.kv_a_norm_g_2[0].rearrange("(k p) -> p k", p=P), **slow).then_inc(vec_in, 16)
            run_stores_range(nc, proj, act, "act", 0, 8)
            act.wait_ge(table, 1)
            nc.scalar.activation(k.sin[:, :, :], r, ACT.Sin).then_inc(rooted, 1)
            nc.scalar.activation(k.cos[:, :, :], ab, ACT.Sin).then_inc(rooted, 1)
            run_stores_range(nc, proj, act, "act", 8, len(jobs))
            act.wait_ge(table, 2)
            nc.scalar.activation(rt[:, :, :], ms[:, :, :], ACT.Sqrt).then_inc(rooted, 1)
            for i in range(NT):
                tok = slice(i * P, (i + 1) * P)
                act.wait_ge(turned, 4 * i + 1)
                nc.scalar.activation(k.aqT[:, :, tok], k.banks[:, 4 * (i % 2), :].rearrange("p (b t) -> p b t", t=P),
                                     ACT.Copy).then_inc(by_act, 1)
                act.wait_ge(turned, 4 * i + 3)
                bk = k.banks[:, 4 * (i % 2) + 2, :].rearrange("p (b t) -> p b t", t=P)
                nc.scalar.activation(k.akT[:, :, tok], bk[:, 0:2, :], ACT.Copy).then_inc(by_act, 1)
                for b in range(2):
                    nc.scalar.activation(k.cqT[:, b, tok], bk[:, 2 + b, :], ACT.Copy, scale=1.0).then_inc(by_act, 1)

        @block.tensor
        def _(pe):
            proj.pe_jobs(pe, 0, len(jobs))
            pe.wait_ge(proj.stored["act"], proj.count["act"])
            pe.wait_ge(proj.stored["dve"], proj.count["dve"])
            pe.wait_ge(ready, 4)
            pe.wait_ge(copies, 3)
            tr = lambda bank, slot, src, w=P: nc.tensor.transpose(k.banks[0:w, bank, slot * P:(slot + 1) * P], src, k.ident[:, :])
            for i in range(NT):
                base = 4 * (i % 2)
                if i >= 2:
                    pe.wait_ge(by_act, 4 * (i - 1))
                    pe.wait_ge(by_dve, 4 * (i - 1))
                for b in range(4):
                    ins = tr(base, b, aq[:, i, b * P:(b + 1) * P])
                ins.then_inc(turned, 1)
                for b in range(4):
                    ins = tr(base + 1, b, iq[:, i, b * P:(b + 1) * P])
                ins.then_inc(turned, 1)
                for b in range(2):
                    tr(base + 2, b, ak4[:, i, b * P:(b + 1) * P])
                for b in range(2):
                    ins = tr(base + 2, 2 + b, mix[:, i, c_cq + b * P:c_cq + (b + 1) * P])
                ins.then_inc(turned, 1)
                tr(base + 3, 0, ik2[:, i, :])
                tr(base + 3, 1, mix[:, i, c_ckv:c_ckv + P])
                ins = tr(base + 3, 2, mix[:, i, c_kr - 64:c_kr + 32], 96)
                ins.then_inc(turned, 1)

        @block.vector
        def _(dve):
            V = nc.vector
            run_stores_range(nc, proj, dve, "dve", 0, 8)
            dve.wait_ge(vec_in, 64)
            d.mark(V.tensor_copy(k.posq[:, :], posi))
            dve.wait_ge(d.sem, d.n)
            dve.wait_ge(pl.sem, 24)
            d.mark(V.tensor_tensor(angv, k.posq[:, :].unsqueeze(2).to_broadcast([P, NT, 24]),
                                   inv[:, :].unsqueeze(1).to_broadcast([P, NT, 24]), ALU.mult))
            dve.wait_ge(d.sem, d.n)
            d.mark(V.tensor_scalar(turns, angv, 1.0 / (2 * math.pi), None, ALU.mult))
            dve.wait_ge(d.sem, d.n)
            d.mark(V.tensor_scalar(turns, turns, MAGIC, None, ALU.add))
            dve.wait_ge(d.sem, d.n)
            d.mark(V.tensor_scalar(turns, turns, MAGIC, None, ALU.subtract))
            src = angv
            for c in (C1, C2, C3):
                dve.wait_ge(d.sem, d.n)
                d.mark(V.scalar_tensor_tensor(out=r, in0=turns, scalar=-c, in1=src, op0=ALU.mult, op1=ALU.add))
                src = r
            dve.wait_ge(d.sem, d.n)
            d.mark(V.tensor_scalar(r, r, 3.1415925, -3.1415925, ALU.min, ALU.max))
            dve.wait_ge(d.sem, d.n)
            d.mark(V.scalar_tensor_tensor(out=ab, in0=r, scalar=-1.0, in1=r, op0=ALU.mult, op1=ALU.min))
            dve.wait_ge(d.sem, d.n)
            V.tensor_scalar(ab, ab, math.pi / 2, None, ALU.add).then_inc(table, 1)
            run_stores_range(nc, proj, dve, "dve", 8, len(jobs))
            for e in ("act", "dve"):
                dve.wait_ge(proj.stored[e], proj.count[e])
            cols = [(c_ik, 64), (c_cq, 256), (c_ckv, P)]
            at = [0, 64, 320]
            for n, (c, w) in enumerate(cols):
                d.mark(V.tensor_tensor(sq[:, :, at[n]:at[n] + w], mix[:, :, c:c + w], mix[:, :, c:c + w], ALU.mult))
            dve.wait_ge(d.sem, d.n)
            for n, (c, w) in enumerate(cols):
                d.mark(V.tensor_reduce(ms[:, n, :], sq[:, :, at[n]:at[n] + w], AX.X, ALU.add))
            dve.wait_ge(d.sem, d.n)
            for n, (c, w) in enumerate(cols):
                ins = V.tensor_scalar(ms[:, n, :], ms[:, n, :], 1.0 / w, EPS, ALU.mult, ALU.add)
                d.mark(ins)
            dve.wait_ge(d.sem, d.n)
            V.memset(sm[:, 79:80], 0.0).then_inc(table, 1)
            dve.wait_ge(rooted, 3)
            d.mark(V.reciprocal(rs[:, :, :], rt[:, :, :]))
            dve.wait_ge(d.sem, d.n)
            for n, (c, w) in enumerate(cols):
                d.mark(V.tensor_tensor(mix[:, :, c:c + w], mix[:, :, c:c + w], rs[:, n, :].unsqueeze(2).to_broadcast([P, NT, w]),
                                       ALU.mult))
            dve.wait_ge(d.sem, d.n)
            d.mark(V.tensor_tensor(mix[:, :, 0:64], mix[:, :, 0:64], ikg[:, :].unsqueeze(1).to_broadcast([P, NT, 64]), ALU.mult))
            d.mark(V.tensor_scalar(k.iw[:, :, :], mix[:, :, c_iw:c_iw + 8], float(np.float32(8 ** -0.5)), None, ALU.mult))
            dve.wait_ge(d.sem, d.n)

            def rope(x, heads, half, f0):
                t = [t4[:, c, 0:NT * heads * half].rearrange("p (i h f) -> p i h f", i=NT, h=heads) for c in range(4)]
                tab = [a[:, :, f0:f0 + half].unsqueeze(2).to_broadcast([P, NT, heads, half]) for a in (k.cos, k.sin)]
                rope_dve(nc, dve, d, x[:, :, :, 0:half], x[:, :, :, half:2 * half], tab[0], tab[1], t)
                dve.wait_ge(d.sem, d.n)

            heads = lambda a, w: a.rearrange("p i (h f) -> p i h f", f=w)
            rope(heads(mix[:, :, 0:64], 64), 1, 8, 0)
            V.memset(sm[:, 79:80], 0.0).then_inc(ready, 1)
            dve.wait_ge(ready, 1)
            rope(heads(k.akv[:, :, 0:128], 64), 2, 8, 0)
            V.memset(sm[:, 79:80], 0.0).then_inc(ready, 1)
            rope(heads(mix[:, :, c_kr:c_kr + 32], 32), 1, 16, 8)
            rope(heads(iq[:, :, :], 64), 8, 8, 0)
            dve.wait_ge(ready, 2)
            V.memset(sm[:, 79:80], 0.0).then_inc(ready, 1)
            rope(heads(aq[:, :, :], 64), 8, 8, 0)
            dve.wait_ge(ready, 3)
            V.memset(sm[:, 79:80], 0.0).then_inc(ready, 1)
            for i in range(NT):
                tok = slice(i * P, (i + 1) * P)
                dve.wait_ge(turned, 4 * i + 2)
                V.tensor_copy(k.iqT[:, :, tok], k.banks[:, 4 * (i % 2) + 1, :].rearrange("p (b t) -> p b t", t=P)).then_inc(by_dve, 1)
                dve.wait_ge(turned, 4 * i + 4)
                bk = k.banks[:, 4 * (i % 2) + 3, :]
                V.tensor_copy(k.ikT[:, tok], bk[:, 0:P]).then_inc(by_dve, 1)
                V.tensor_scalar(k.ckvT[:, tok], bk[:, P:2 * P], kvg[:, 0:1], None, ALU.mult).then_inc(by_dve, 1)
                V.tensor_copy(k.krT[64:96, tok], bk[64:96, 2 * P:3 * P]).then_inc(by_dve, 1)
            dve.wait_ge(by_act, 4 * NT)
            for b in range(2):
                d.mark(V.tensor_scalar(k.cqT[:, b, :], k.cqT[:, b, :], qg[:, b:b + 1], None, ALU.mult))


def stage_index_scores(nc, k):
    p = k.place
    k.isc = p("index_scores", [P, NT, T], 189)
    k.posrow = p("pos_row", [P, T], 125)
    R = p("index_relu", [P, 3, T], 96)
    posi = p("pos_row_int", [P, T], 108, I32)
    s = lambda n: k.sem("idx_" + n)
    pos_in, mm, relu, base, acc = s("pos_in"), s("product"), s("relu"), s("base"), s("sum")
    items = [(i, h) for i in range(NT) for h in range(8)]
    pair = lambda n: k.banks[:, 2 * (n % 4):2 * (n % 4) + 2, :].rearrange("p b c -> p (b c)")
    with nc.Block() as block:
        @block.scalar
        def _(act):
            act.dma_start(posi[:, :], k.positions_2[0].partition_broadcast(P)).then_inc(pos_in, 16)
            for n, (i, h) in enumerate(items):
                act.wait_ge(mm, n + 1)
                if n >= 3:
                    act.wait_ge(acc, n - 2)
                nc.scalar.activation(R[:, n % 3, :], pair(n), ACT.Relu).then_inc(relu, 1)

        @block.tensor
        def _(pe):
            for n, (i, h) in enumerate(items):
                rows = slice(64 * (h % 2), 64 * (h % 2) + 64)
                if n >= 4:
                    pe.wait_ge(relu, n - 3)
                for c in range(2):
                    ins = nc.tensor.matmul(pair(n)[:, c * 512:(c + 1) * 512], k.iqT[rows, h // 2, i * P:(i + 1) * P],
                                           k.ikT[rows, c * 512:(c + 1) * 512], start=True, stop=True)
                ins.then_inc(mm, 1)

        @block.vector
        def _(dve):
            dve.wait_ge(pos_in, 16)
            nc.vector.tensor_copy(k.posrow[:, :], posi[:, :]).then_inc(base, 1)
            dve.wait_ge(base, 1)
            for i in range(NT):
                nc.vector.tensor_scalar(k.isc[:, i, :], k.posrow[:, :], k.posq[:, i:i + 1], MASKED, ALU.is_gt,
                                        ALU.mult).then_inc(base, 1)
            for n, (i, h) in enumerate(items):
                dve.wait_ge(relu, n + 1)
                if h == 0:
                    dve.wait_ge(base, i + 2)
                else:
                    dve.wait_ge(acc, n)
                nc.vector.scalar_tensor_tensor(out=k.isc[:, i, :], in0=R[:, n % 3, :], scalar=k.iw[:, i, h:h + 1],
                                               in1=k.isc[:, i, :], op0=ALU.mult, op1=ALU.add).then_inc(acc, 1)


def stage_select(nc, k):
    p = k.place
    V = nc.vector
    junk = p("count_scratch", [P, 2, T], 96)
    G, Q, RK = p("above", [P, T], 104), p("equal", [P, T], 108), p("rank", [P, T], 112)
    stage = p("gate_stage", [P, 4, 512], 116)
    ints = p("threshold_bits", [P, 6, NT], 6.25, I32)
    key, cand, sign, flip, took = (ints[:, c, :] for c in range(5))
    thr = ints[:, 5, :].bitcast(F32)
    cnt = k.small[:, 216:224]
    left = k.small[:, 224:232]
    jobs = []
    for c in range(16):
        jobs += feature_jobs(k.c_gate[c // 4], (c % 4) * P, None, "sigmoid", "act")
    proj = Projection(nc, k, "gates", jobs)
    d = Steps(k, "select_dve")
    cs = Steps(k, "select_count")
    gate_out = [k.sem(f"gate_out_{i}") for i in range(4)]
    with nc.Block() as block:
        @block.sync
        def _(sp):
            for j, job in enumerate(jobs):
                if j % 8 == 0:
                    k.w.load_up_to(sp, k.c_gate[0] + j // 8 + 1)
                sp.wait_ge(proj.stored["act"], j + 1)
                sp.dma_start(k.gate_dram[j // 2, :, (j % 2) * 512:(j % 2 + 1) * 512], stage[:, j % 4, :]).then_inc(gate_out[j % 4], 16)
            k.w.load_up_to(sp, k.c_bb)
            for g in gate_out:
                sp.wait_ge(g, 16 * len(jobs) // 4)

        @block.scalar
        def _(act):
            for j, job in enumerate(jobs):
                act.wait_ge(proj.done, j + 1)
                if j >= 4:
                    act.wait_ge(gate_out[j % 4], 16 * (j // 4))
                nc.scalar.activation(stage[:, j % 4, :], proj.bank(j), ACT.Sigmoid).then_inc(proj.stored["act"], 1)

        @block.tensor
        def _(pe):
            proj.pe_jobs(pe, 0, len(jobs))

        @block.vector
        def _(dve):
            d.mark(V.memset(key, 0))
            dve.wait_ge(d.sem, d.n)
            top = -2 ** 31

            def ordered_to_float():
                d.mark(V.tensor_scalar(sign, cand, 31, -1, ALU.arith_shift_right, ALU.bitwise_xor))
                dve.wait_ge(d.sem, d.n)
                d.mark(V.tensor_scalar(flip, sign, top, None, ALU.bitwise_or))
                dve.wait_ge(d.sem, d.n)
                d.mark(V.tensor_tensor(thr.bitcast(I32), cand, flip, ALU.bitwise_xor))
                dve.wait_ge(d.sem, d.n)

            for bit in range(31, -1, -1):
                d.mark(V.tensor_scalar(cand, key, top if bit == 31 else 1 << bit, None, ALU.bitwise_or))
                dve.wait_ge(d.sem, d.n)
                ordered_to_float()
                for i in range(NT):
                    if cs.n >= 2:
                        dve.wait_ge(cs.sem, cs.n - 1)
                    cs.mark(V.tensor_scalar(junk[:, i % 2, :], k.isc[:, i, :], thr[:, i:i + 1], 0.0, ALU.is_ge, ALU.add,
                                            accum_out=cnt[:, i:i + 1]))
                dve.wait_ge(cs.sem, cs.n)
                d.mark(V.tensor_scalar(took, cnt, float(TOPK), None, ALU.is_ge))
                dve.wait_ge(d.sem, d.n)
                if bit:
                    d.mark(V.tensor_scalar(took, took, bit, None, ALU.logical_shift_left))
                    dve.wait_ge(d.sem, d.n)
                d.mark(V.tensor_tensor(key, key, took, ALU.bitwise_or))
                dve.wait_ge(d.sem, d.n)
            d.mark(V.tensor_copy(cand, key))
            dve.wait_ge(d.sem, d.n)
            ordered_to_float()
            for i in range(NT):
                x, t = k.isc[:, i, :], thr[:, i:i + 1]
                d.mark(V.tensor_scalar(G[:, :], x, t, 0.0, ALU.is_gt, ALU.add, accum_out=cnt[:, i:i + 1]))
                d.mark(V.tensor_scalar(Q[:, :], x, t, None, ALU.is_equal))
                dve.wait_ge(d.sem, d.n)
                d.mark(V.tensor_scalar(left[:, i:i + 1], cnt[:, i:i + 1], -1.0, float(TOPK), ALU.mult, ALU.add))
                d.mark(V.tensor_tensor_scan(RK[:, :], Q[:, :], Q[:, :], 0.0, ALU.add, ALU.max))
                dve.wait_ge(d.sem, d.n)
                d.mark(V.scalar_tensor_tensor(out=Q[:, :], in0=RK[:, :], scalar=left[:, i:i + 1], in1=Q[:, :],
                                              op0=ALU.is_le, op1=ALU.mult))
                dve.wait_ge(d.sem, d.n)
                d.mark(V.tensor_tensor(G[:, :], G[:, :], Q[:, :], ALU.add))
                dve.wait_ge(d.sem, d.n)
                d.mark(V.scalar_tensor_tensor(out=G[:, :], in0=x, scalar=MASKED / 2, in1=G[:, :], op0=ALU.is_gt, op1=ALU.mult))
                dve.wait_ge(d.sem, d.n)
                d.mark(V.tensor_scalar(x, G[:, :], 1.0, -MASKED, ALU.subtract, ALU.mult))
                dve.wait_ge(d.sem, d.n)


def attention(nc, k, name, q, kk, v, bias, scale, oT, at):
    p = k.place
    L = p(f"{name}_logits", [P, 2, T], at)
    E = p(f"{name}_probs", [P, 2, T], at + 8)
    ET = p(f"{name}_probsT", [P, 2, NT, P], at + 16)
    otok = p(f"{name}_out_tok", [P, 2, 512], at + 24)
    low = p(f"{name}_minus_max", [P, NT * 8], at + 28)
    tot = p(f"{name}_total", [P, NT * 8], at + 28.25)
    inv = p(f"{name}_inverse", [P, NT * 8], at + 28.5)
    items = [(i, h) for i in range(NT) for h in range(8)]
    N = len(items)
    s = lambda n: k.sem(f"{name}_{n}")
    mm, logit, prob, turned = s("scores"), s("logits"), s("probs"), s("probs_turned")
    t_act, t_dve, pv, invd, otk, ot_mm, ot_st = s("pT_act"), s("pT_dve"), s("out"), s("inverse"), s("out_stored"), s("out_turned"), s("oT_stored")
    pair = lambda n: k.banks[:, 2 * (n % 2):2 * (n % 2) + 2, :].rearrange("p b c -> p (b c)")

    def act_program(act):
        def softmax(n):
            act.wait_ge(logit, n + 1)
            if n >= 2:
                act.wait_ge(turned, 2 * (n - 1))
            nc.scalar.activation(E[:, n % 2, :], L[:, n % 2, :], ACT.Exp, scale=-1.0, bias=low[:, n:n + 1],
                                 accum_out=tot[:, n:n + 1]).then_inc(prob, 1)
        softmax(0)
        for n, (i, h) in enumerate(items):
            if n + 1 < N:
                softmax(n + 1)
            act.wait_ge(turned, 2 * n + 1)
            if n >= 2:
                act.wait_ge(pv, n - 1)
            nc.scalar.activation(ET[:, n % 2, 0:4, :], k.banks[:, 4, :].rearrange("p (j t) -> p j t", t=P),
                                 ACT.Copy).then_inc(t_act, 1)
            if h == 1 and i:
                act.wait_ge(ot_mm, i)
                nc.scalar.activation(oT[:, :, (i - 1) * P:i * P], k.banks[:, 7, :].rearrange("p (b t) -> p b t", t=P),
                                     ACT.Copy).then_inc(ot_st, 1)
        act.wait_ge(ot_mm, NT)
        nc.scalar.activation(oT[:, :, T - P:T], k.banks[:, 7, :].rearrange("p (b t) -> p b t", t=P), ACT.Copy).then_inc(ot_st, 1)

    def pe_program(pe):
        def scores(n):
            i, h = items[n]
            if n >= 2:
                pe.wait_ge(logit, n - 1)
            for c in range(2):
                ins = nc.tensor.matmul(pair(n)[:, c * 512:(c + 1) * 512], q(h, i), kk(h, c), start=True, stop=True)
            ins.then_inc(mm, 1)

        def turn_out(i):
            pe.wait_ge(otk, i + 1)
            if i:
                pe.wait_ge(ot_st, i)
            for b in range(4):
                ins = nc.tensor.transpose(k.banks[:, 7, b * P:(b + 1) * P], otok[:, i % 2, b * P:(b + 1) * P], k.ident[:, :])
            ins.then_inc(ot_mm, 1)

        scores(0)
        scores(1)
        for n, (i, h) in enumerate(items):
            if n + 2 < N:
                scores(n + 2)
            pe.wait_ge(prob, n + 1)
            if n:
                pe.wait_ge(t_act, n)
                pe.wait_ge(t_dve, n)
            for j in range(NT):
                ins = nc.tensor.transpose(k.banks[:, 4 + j // 4, (j % 4) * P:(j % 4 + 1) * P],
                                          E[:, n % 2, j * P:(j + 1) * P], k.ident[:, :])
                if j % 4 == 3:
                    ins.then_inc(turned, 1)
            if h == 1 and i:
                turn_out(i - 1)
            pe.wait_ge(t_act, n + 1)
            if h == 0 and i:
                pe.wait_ge(otk, i)
            for j in range(NT):
                if j == 4:
                    pe.wait_ge(t_dve, n + 1)
                ins = nc.tensor.matmul(k.banks[:, 6, h * 64:(h + 1) * 64], ET[:, n % 2, j, :], v(h, j),
                                       start=(j == 0), stop=(j == NT - 1))
            ins.then_inc(pv, 1)
        turn_out(NT - 1)

    def dve_program(dve):
        def logits(n):
            i, h = items[n]
            dve.wait_ge(mm, n + 1)
            if n >= 2:
                dve.wait_ge(prob, n - 1)
            nc.vector.tensor_tensor_reduce(L[:, n % 2, :], pair(n), bias(dve, i), -scale, -MASKED, ALU.add, ALU.min,
                                           low[:, n:n + 1]).then_inc(logit, 1)
        logits(0)
        for n, (i, h) in enumerate(items):
            if n + 1 < N:
                logits(n + 1)
            dve.wait_ge(turned, 2 * n + 2)
            if n >= 2:
                dve.wait_ge(pv, n - 1)
            nc.vector.tensor_copy(ET[:, n % 2, 4:8, :], k.banks[:, 5, :].rearrange("p (j t) -> p j t", t=P)).then_inc(t_dve, 1)
            if h == 7:
                dve.wait_ge(prob, n + 1)
                nc.vector.reciprocal(inv[:, 8 * i:8 * i + 8], tot[:, 8 * i:8 * i + 8]).then_inc(invd, 1)
                dve.wait_ge(invd, i + 1)
                dve.wait_ge(pv, n + 1)
                if i >= 2:
                    dve.wait_ge(ot_mm, i - 1)
                nc.vector.tensor_tensor(otok[:, i % 2, :].rearrange("p (h f) -> p h f", f=64),
                                        k.banks[:, 6, :].rearrange("p (h f) -> p h f", f=64),
                                        inv[:, 8 * i:8 * i + 8].unsqueeze(2).to_broadcast([P, 8, 64]), ALU.mult).then_inc(otk, 1)

    return act_program, pe_program, dve_program, logit


def stage_sparse_attention(nc, k):
    k.oaT = k.place("sparse_oT", [P, 4, T], 72)
    rows = lambda h: slice(64 * (h % 2), 64 * (h % 2) + 64)
    act_p, pe_p, dve_p, _ = attention(
        nc, k, "sparse",
        lambda h, i: k.aqT[rows(h), h // 2, i * P:(i + 1) * P],
        lambda h, c: k.akT[rows(h), h // 4, c * 512:(c + 1) * 512],
        lambda h, j: k.akv[:, j, 128 + (h // 4) * 64:128 + (h // 4) * 64 + 64],
        lambda dve, i: k.isc[:, i, :], 1.0, k.oaT, 96)
    with nc.Block() as block:
        block.scalar(act_p)
        block.tensor(pe_p)
        block.vector(dve_p)


def stage_latent_projection(nc, k):
    p = k.place
    wuq, wuk, wuv = p("w_uq", [P, 2, 768], 209), p("w_uk", [P, 512], 215), p("w_uv", [P, 512], 217)
    k.qf = p("latent_qT", [P, 8, T], 129)
    k.kf = p("latent_kT", [P, 8, T], 40)
    k.vb = p("latent_v", [P, NT, 512], 161)
    qb = p("latent_q_tok", [P, NT, 768], 92)
    t4 = p("latent_rope", [P, 4, 512], 116)
    s = lambda n: k.sem("lat_" + n)
    w_in, mm, st_a, st_d, kr, ready, turned, q_a, q_d = (s(n) for n in ("w_in", "product", "act", "dve", "rope_keys", "ready", "turned", "q_act", "q_dve"))
    d = Steps(k, "lat_rotate")
    jobs = [("q", i, c) for i in range(NT) for c in range(2)] + [("v", i, 0) for i in range(NT)] + \
           [("k", h, c) for h in range(8) for c in range(2)]
    by = ["act" if n % 2 == 0 else "dve" for n in range(len(jobs))]
    with nc.Block() as block:
        @block.sync
        def _(sp):
            sp.dma_start(wuq[:, :, :], k.w_uq_2[0].rearrange("(k p) h f -> p k (h f)", p=P)).then_inc(w_in, 16)
            sp.dma_start(wuk[:, :], k.w_uk_2[0].rearrange("r h f -> r (h f)")).then_inc(w_in, 16)
            sp.dma_start(wuv[:, :], k.w_uv_2[0].rearrange("r h f -> r (h f)")).then_inc(w_in, 16)

        def dest(n):
            kind, a, c = jobs[n]
            if kind == "q":
                return qb[:, a, c * 384:(c + 1) * 384], k.banks[:, n % 8, 0:384]
            if kind == "v":
                return k.vb[:, a, :], k.banks[:, n % 8, :]
            return k.kf[0:64, a, c * 512:(c + 1) * 512], k.banks[0:64, n % 8, :]

        @block.gpsimd
        def _(pool):
            for h in range(8):
                pool.tensor_copy(k.kf[64:96, h, :], k.krT[64:96, :]).then_inc(kr, 1)

        @block.scalar
        def _(act):
            for n in range(0, len(jobs), 2):
                out, src = dest(n)
                act.wait_ge(mm, n + 1)
                nc.scalar.activation(out, src, ACT.Copy).then_inc(st_a, 1)
            for i in range(NT):
                for b in range(0, 2):
                    if b == 0:
                        act.wait_ge(turned, 2 * i + 1)
                        nc.scalar.activation(k.qf[0:96, 0:4, i * P:(i + 1) * P],
                                             k.banks[0:96, 2 * (i % 2), :].rearrange("p (h t) -> p h t", t=P), ACT.Copy).then_inc(q_a, 1)

        @block.tensor
        def _(pe):
            pe.wait_ge(w_in, 48)
            for n, (kind, a, c) in enumerate(jobs):
                out = dest(n)[1]
                if n >= 8:
                    pe.wait_ge(st_a if n % 2 == 0 else st_d, (n - 8) // 2 + 1)
                if kind == "q":
                    for b in range(2):
                        ins = nc.tensor.matmul(out, k.cqT[:, b, a * P:(a + 1) * P], wuq[:, b, c * 384:(c + 1) * 384],
                                               start=(b == 0), stop=(b == 1))
                elif kind == "v":
                    ins = nc.tensor.matmul(out, k.ckvT[:, a * P:(a + 1) * P], wuv[:, :], start=True, stop=True)
                else:
                    ins = nc.tensor.matmul(out, wuk[:, a * 64:(a + 1) * 64], k.ckvT[:, c * 512:(c + 1) * 512], start=True, stop=True)
                ins.then_inc(mm, 1)
            pe.wait_ge(st_a, len(jobs) // 2)
            pe.wait_ge(st_d, len(jobs) // 2)
            pe.wait_ge(ready, 1)
            for i in range(NT):
                if i >= 2:
                    pe.wait_ge(q_a, i - 1)
                    pe.wait_ge(q_d, i - 1)
                for h in range(8):
                    ins = nc.tensor.transpose(k.banks[0:96, 2 * (i % 2) + h // 4, (h % 4) * P:(h % 4 + 1) * P],
                                              qb[:, i, h * 96:(h + 1) * 96], k.ident[:, :])
                    if h % 4 == 3:
                        ins.then_inc(turned, 1)

        @block.vector
        def _(dve):
            for n in range(1, len(jobs), 2):
                out, src = dest(n)
                dve.wait_ge(mm, n + 1)
                nc.vector.tensor_copy(out, src).then_inc(st_d, 1)
                if n == 15:
                    dve.wait_ge(st_a, 8)
                    dve.wait_ge(st_d, 8)
                    for i0 in range(0, NT, 4):
                        x = qb[:, i0:i0 + 4, :].rearrange("p i (h f) -> p i h f", f=96)
                        t = [t4[:, c, :].rearrange("p (i h f) -> p i h f", i=4, h=8) for c in range(4)]
                        tab = [a[:, i0:i0 + 4, 8:24].unsqueeze(2).to_broadcast([P, 4, 8, 16]) for a in (k.cos, k.sin)]
                        rope_dve(nc, dve, d, x[:, :, :, 64:80], x[:, :, :, 80:96], tab[0], tab[1], t)
                        dve.wait_ge(d.sem, d.n)
                    nc.vector.memset(k.small[:, 79:80], 0.0).then_inc(ready, 1)
            for i in range(NT):
                dve.wait_ge(turned, 2 * i + 2)
                nc.vector.tensor_copy(k.qf[0:96, 4:8, i * P:(i + 1) * P],
                                      k.banks[0:96, 2 * (i % 2) + 1, :].rearrange("p (h t) -> p h t", t=P)).then_inc(q_d, 1)


def stage_latent_attention(nc, k):
    p = k.place
    k.obT = p("latent_oT", [P, 4, T], 193)
    pen = p("causal_bias", [P, 2, T], 177)
    made = k.sem("lat_bias")
    state = {"made": -1}
    hold = {}

    def bias(dve, i):
        if state["made"] < i:
            state["made"] = i
            dve.wait_ge(made, i + 1)
        return pen[:, i % 2, :]

    act_p, pe_p, dve_p, logit = attention(
        nc, k, "latent",
        lambda h, i: k.qf[0:96, h, i * P:(i + 1) * P],
        lambda h, c: k.kf[0:96, h, c * 512:(c + 1) * 512],
        lambda h, j: k.vb[:, j, h * 64:(h + 1) * 64],
        bias, float(np.float32(96 ** -0.5)), k.obT, 92)
    with nc.Block() as block:
        @block.gpsimd
        def _(pool):
            for i in range(NT):
                if i >= 2:
                    pool.wait_ge(logit, 8 * (i - 1))
                pool.tensor_scalar(pen[:, i % 2, :], k.posrow[:, :], k.posq[:, i:i + 1], MASKED, ALU.is_gt,
                                   ALU.mult).then_inc(made, 1)
        block.scalar(act_p)
        block.tensor(pe_p)
        block.vector(dve_p)


def stage_merge(nc, k):
    p = k.place
    mT = p("merged_T", [P, KB, T], 100)
    gates = p("gates_in", [P, 4, T], 132)
    pa, pb = p("part_a", [P, 2, 512], 148), p("part_b", [P, 2, 512], 152)
    k.h2 = p("h2", [P, NT, D], 160)
    ffng = k.small[:, 232:240]
    s = lambda n: k.sem("mrg_" + n)
    g_in = [s(f"gate_in_{c}") for c in range(2)]
    x1_in, vec_in, mm_a, mm_b, st_a, st_b, merged, gained, res = (s(n) for n in ("x1_in", "vec_in", "a", "b", "a_st", "b_st", "sum", "gained", "residual"))
    k.w.freed[k.c_ba] = (mm_a, 16)
    k.w.freed[k.c_bb] = (mm_b, 16)
    jobs = [dict(chunk=k.c_out2[h], kind="tokens", tile=i, col=0, width=512, by="dve", dest=h, how="add")
            for i in range(NT) for h in range(2)]
    proj = Projection(nc, k, "second_out", jobs, banks=8, src=mT)
    norm = NormTranspose(nc, k, "norm3", k.h2, k.hT, p("h2_normed", [P, NT, D], 100))
    ga = lambda n: k.gate_dram[n]
    with nc.Block() as block:
        @block.sync
        def _(sp):
            for n in range(KB):
                if n >= 2:
                    sp.wait_ge(st_a, 2 * (n - 1))
                    sp.wait_ge(st_b, 2 * (n - 1))
                for br in range(2):
                    sp.dma_start(gates[:, 2 * (n % 2) + br, :], ga(8 * br + n)).then_inc(g_in[n % 2], 16)
                if n == 0:
                    sp.dma_start(k.h2[:, :, :], k.x1_dram.rearrange("(i p) d -> p i d", p=P)).then_inc(x1_in, 16)
            k.w.load_up_to(sp, k.c_up[1])

        @block.gpsimd
        def _(pool):
            for n in range(16):
                pool.wait_ge(st_a, n + 1)
                pool.wait_ge(st_b, n + 1)
                pool.tensor_tensor(mT[:, n // 2, (n % 2) * 512:(n % 2 + 1) * 512], pa[:, n % 2, :], pb[:, n % 2, :],
                                   ALU.add).then_inc(merged, 1)

        @block.scalar
        def _(act):
            act.dma_start(ffng, k.norm_ffn_g_2[0].rearrange("(k p) -> p k", p=P), allow_slow_non_contiguous=True).then_inc(vec_in, 16)
            norm.act_stats(act, lambda e, i: e.wait_ge(proj.stored["dve"], 2 * i + 2))
            norm.store(act, 0)

        @block.tensor
        def _(pe):
            for n in range(16):
                f, c = n // 2, n % 2
                for br, (chunk, src, mm, st) in enumerate(((k.c_ba, k.oaT, mm_a, st_a), (k.c_bb, k.obT, mm_b, st_b))):
                    if n == 0:
                        k.w.wait(pe, chunk)
                    if n >= 4:
                        pe.wait_ge(st, n - 3)
                    wv = k.w.view(chunk)
                    for b in range(4):
                        ins = nc.tensor.matmul(k.banks[:, 2 * (n % 4) + br, :], wv[:, b, f * P:(f + 1) * P],
                                               src[:, b, c * 512:(c + 1) * 512], start=(b == 0), stop=(b == 3))
                    ins.then_inc(mm, 1)
            pe.wait_ge(merged, 16)
            proj.pe_jobs(pe, 0, len(jobs))
            pe.wait_ge(proj.stored["dve"], len(jobs))
            norm.pe_transpose(pe)

        @block.vector
        def _(dve):
            for n in range(16):
                f, c = n // 2, n % 2
                if c == 0:
                    dve.wait_ge(g_in[f % 2], 32 * (f // 2 + 1))
                for br, (buf, mm, st) in enumerate(((pa, mm_a, st_a), (pb, mm_b, st_b))):
                    dve.wait_ge(mm, n + 1)
                    if n >= 2:
                        dve.wait_ge(merged, n - 1)
                    nc.vector.tensor_tensor(buf[:, n % 2, :], k.banks[:, 2 * (n % 4) + br, :],
                                            gates[:, 2 * (f % 2) + br, c * 512:(c + 1) * 512], ALU.mult).then_inc(st, 1)
            dve.wait_ge(x1_in, 16)
            for j, job in enumerate(jobs):
                i, h = job["tile"], job["dest"]
                dve.wait_ge(proj.done, j + 1)
                xs = k.h2[:, i, h * 512:(h + 1) * 512]
                nc.vector.tensor_tensor(xs, proj.bank(j), xs, ALU.add).then_inc(proj.stored["dve"], 1)
            norm.dve_stats(dve)
            norm.dve_divide(dve)
            norm.store(dve, 1)
            dve.wait_ge(norm.by_act, NT)
            dve.wait_ge(norm.by_dve, NT)
            dve.wait_ge(vec_in, 16)
            for b in range(KB):
                nc.vector.tensor_scalar(k.hT[:, b, :], k.hT[:, b, :], ffng[:, b:b + 1], None, ALU.mult).then_inc(gained, 1)


def stage_ffn_up(nc, k):
    p = k.place
    k.act = p("ffn_act", [P, FBLK, T], 72)
    Y = p("ffn_conv", [P, 4, T], 192)
    cw = p("conv_taps", [P, 3, 2 * FBLK], 208)
    cb = p("conv_bias", [P, 2 * FBLK], 209)
    vec_in = k.sem("conv_in")
    s = lambda n: k.sem("ffn_" + n)
    mm, y0, y1, y2, gate, out = (s(n) for n in ("u", "tap2", "tap1", "tap0", "silu", "act"))
    for n, c in enumerate(k.c_up):
        k.w.freed[c] = (mm, 4 * n + 4)
    pair = lambda n: k.banks[:, 2 * (n % 4):2 * (n % 4) + 2, :].rearrange("p b c -> p (b c)")
    with nc.Block() as block:
        @block.sync
        def _(sp):
            k.w.load_up_to(sp, k.c_down[0][1])

        @block.gpsimd
        def _(pool):
            for f in range(FBLK):
                pool.wait_ge(gate, f + 1)
                pool.wait_ge(y2, 2 * f + 2)
                b = 2 * (f % 2)
                pool.tensor_tensor(k.act[:, f, :], Y[:, b, :], Y[:, b + 1, :], ALU.mult).then_inc(out, 1)

        @block.scalar
        def _(act):
            slow = dict(allow_slow_non_contiguous=True)
            for j in range(3):
                act.dma_start(cw[:, j, :], k.conv_w_2[0, j].rearrange("(f p) -> p f", p=P), **slow).then_inc(vec_in, 16)
            act.dma_start(cb[:, :], k.conv_b_2[0].rearrange("(f p) -> p f", p=P), **slow).then_inc(vec_in, 16)
            act.wait_ge(vec_in, 64)
            for n in range(2 * FBLK + 2):
                if n < 2 * FBLK:
                    f, v = n // 2, n % 2
                    c = f + v * FBLK
                    act.wait_ge(mm, n + 1)
                    if f >= 2:
                        act.wait_ge(out, f - 1)
                    nc.scalar.activation(Y[:, 2 * (f % 2) + v, :], pair(n), ACT.Identity, bias=cb[:, c:c + 1],
                                         scale=cw[:, 2, c:c + 1]).then_inc(y0, 1)
                if n >= 2 and n % 2 == 0:
                    f = n // 2 - 1
                    act.wait_ge(y2, 2 * f + 1)
                    nc.scalar.activation(Y[:, 2 * (f % 2), :], Y[:, 2 * (f % 2), :], ACT.Silu).then_inc(gate, 1)

        @block.tensor
        def _(pe):
            for n in range(2 * FBLK):
                f, v = n // 2, n % 2
                chunk = k.c_up[f // 2]
                if f % 2 == 0 and v == 0:
                    k.w.wait(pe, chunk)
                if n >= 4:
                    pe.wait_ge(y2, n - 3)
                wv = k.w.view(chunk)
                c0 = v * 256 + (f % 2) * P
                for h in range(2):
                    for b in range(KB):
                        ins = nc.tensor.matmul(pair(n)[:, h * 512:(h + 1) * 512], wv[:, b, c0:c0 + P],
                                               k.hT[:, b, h * 512:(h + 1) * 512], start=(b == 0), stop=(b == KB - 1))
                ins.then_inc(mm, 1)

        @block.vector
        def _(dve):
            dve.wait_ge(vec_in, 64)
            for n in range(2 * FBLK):
                f, v = n // 2, n % 2
                c, y = f + v * FBLK, Y[:, 2 * (f % 2) + v, :]
                dve.wait_ge(y0, n + 1)
                nc.vector.scalar_tensor_tensor(out=y[:, 1:T], in0=pair(n)[:, 0:T - 1], scalar=cw[:, 1, c:c + 1],
                                               in1=y[:, 1:T], op0=ALU.mult, op1=ALU.add).then_inc(y1, 1)
                dve.wait_ge(y1, n + 1)
                nc.vector.scalar_tensor_tensor(out=y[:, 2:T], in0=pair(n)[:, 0:T - 2], scalar=cw[:, 0, c:c + 1],
                                               in1=y[:, 2:T], op0=ALU.mult, op1=ALU.add).then_inc(y2, 1)


def stage_ffn_down(nc, k):
    p = k.place
    x = k.h2
    row = p("last_gain", [P, D], 192)
    s = lambda n: k.sem("down_" + n)
    vec_in, part, done, added, summed = (s(n) for n in ("vec_in", "part", "product", "added", "summed"))
    out = k.output_stored
    rstd_s, root_s, mean_s, fin = s("rstd"), s("root"), s("mean"), s("normed")
    sq, ms, rt, rs = (k.small[:, c:c + 8] for c in (168, 176, 184, 192))
    n = 0
    for h in range(2):
        for g in range(3):
            n += 1
            k.w.freed[k.c_down[h][g]] = (part, n)
    with nc.Block() as block:
        @block.sync
        def _(sp):
            k.w.load_up_to(sp, k.c_down[1][2])
            for i in range(NT):
                sp.wait_ge(fin, i + 1)
                sp.dma_start(k.out[0, i * P:(i + 1) * P, :], x[:, i, :]).then_inc(out, 16)
            sp.wait_ge(out, 16 * NT)

        @block.scalar
        def _(act):
            act.dma_start(row[:, :], k.norm_final_g_2.partition_broadcast(P)).then_inc(vec_in, 16)
            for i in range(NT):
                act.wait_ge(added, NT + i + 1)
                nc.scalar.activation(k.hT[:, i, :], x[:, i, :], ACT.Square, accum_out=sq[:, i:i + 1]).then_inc(summed, 1)
                act.wait_ge(mean_s, i + 1)
                nc.scalar.activation(rt[:, i:i + 1], ms[:, i:i + 1], ACT.Sqrt).then_inc(root_s, 1)

        @block.tensor
        def _(pe):
            for h in range(2):
                for g in range(3):
                    chunk = k.c_down[h][g]
                    k.w.wait(pe, chunk)
                    wv, blocks = k.w.view(chunk), k.w.chunks[chunk][1]
                    last = g == 2
                    for i in range(NT):
                        if h and g == 0:
                            pe.wait_ge(added, i + 1)
                        for b in range(blocks):
                            f = 8 * g + b
                            ins = nc.tensor.matmul(k.banks[:, i, :], k.act[:, f, i * P:(i + 1) * P], wv[:, b, :],
                                                   start=(f == 0), stop=(f == FBLK - 1))
                        if last:
                            ins.then_inc(done if i < NT - 1 else part, 1)
                    if not last:
                        ins.then_inc(part, 1)

        @block.vector
        def _(dve):
            def finish(i):
                dve.wait_ge(summed, i + 1)
                nc.vector.tensor_scalar(ms[:, i:i + 1], sq[:, i:i + 1], 1.0 / D, EPS, ALU.mult, ALU.add).then_inc(mean_s, 1)
                dve.wait_ge(root_s, i + 1)
                nc.vector.reciprocal(rs[:, i:i + 1], rt[:, i:i + 1]).then_inc(rstd_s, 1)
                dve.wait_ge(rstd_s, i + 1)
                nc.vector.scalar_tensor_tensor(out=x[:, i, :], in0=x[:, i, :], scalar=rs[:, i:i + 1], in1=row[:, :],
                                               op0=ALU.mult, op1=ALU.mult).then_inc(fin, 1)

            dve.wait_ge(vec_in, 16)
            for h in range(2):
                for i in range(NT):
                    if i < NT - 1:
                        dve.wait_ge(done, 7 * h + i + 1)
                    else:
                        dve.wait_ge(part, 3 * h + 3)
                    xs = x[:, i, h * 512:(h + 1) * 512]
                    nc.vector.tensor_tensor(xs, k.banks[:, i, :], xs, ALU.add).then_inc(added, 1)
                    if h and i:
                        finish(i - 1)
            finish(NT - 1)


def build(nc, views):
    k = Kernel(nc)
    k.x = views["x"]
    k.c = views["c"]
    k.w_ada = views["w_ada"]
    k.b_ada = views["b_ada"]
    k.w_in = views["w_in"]
    k.w_gla_gate2 = views["w_gla_gate2"]
    k.b_gla_gate = views["b_gla_gate"]
    k.gla_norm_w = views["gla_norm_w"]
    k.hgrn_lb_logits = views["hgrn_lb_logits"]
    k.hgrn_norm_w = views["hgrn_norm_w"]
    k.w_out = views["w_out"]
    k.final_norm_w = views["final_norm_w"]
    k.positions_2 = views["positions_2"]
    k.norm_mix_g_2 = views["norm_mix_g_2"]
    k.w_in_2 = views["w_in_2"]
    k.idx_k_norm_g_2 = views["idx_k_norm_g_2"]
    k.q_a_norm_g_2 = views["q_a_norm_g_2"]
    k.kv_a_norm_g_2 = views["kv_a_norm_g_2"]
    k.w_uq_2 = views["w_uq_2"]
    k.w_uk_2 = views["w_uk_2"]
    k.w_uv_2 = views["w_uv_2"]
    k.w_branch_a_2 = views["w_branch_a_2"]
    k.w_branch_b_2 = views["w_branch_b_2"]
    k.w_out_2 = views["w_out_2"]
    k.norm_ffn_g_2 = views["norm_ffn_g_2"]
    k.w_up_2 = views["w_up_2"]
    k.conv_w_2 = views["conv_w_2"]
    k.conv_b_2 = views["conv_b_2"]
    k.w_down_2 = views["w_down_2"]
    k.norm_final_g_2 = views["norm_final_g_2"]
    k.out = views["out"]
    k.x1_dram = nc.dram_tensor("x1_scratch", (T, D), F32, kind="Internal").ap()
    k.gate_dram = nc.dram_tensor("gate_scratch", (16, P, T), F32, kind="Internal").ap()
    plan(nc, k)
    stage_input(nc, k)
    k.end_stage()
    stage_gla_projection(nc, k)
    k.end_stage()
    stage_gated_attention(nc, k, k.gla, 0)
    k.end_stage()
    stage_hgrn_projection(nc, k)
    k.end_stage()
    stage_gated_attention(nc, k, k.hgrn, 4)
    k.end_stage()
    stage_stick_projection(nc, k)
    k.end_stage()
    stage_stick_attention(nc, k)
    k.end_stage()
    stage_first_output(nc, k)
    k.end_stage()
    stage_second_projection(nc, k)
    k.end_stage()
    stage_index_scores(nc, k)
    k.end_stage()
    stage_select(nc, k)
    k.end_stage()
    stage_sparse_attention(nc, k)
    k.end_stage()
    stage_latent_projection(nc, k)
    k.end_stage()
    stage_latent_attention(nc, k)
    k.end_stage()
    stage_merge(nc, k)
    k.end_stage()
    stage_ffn_up(nc, k)
    k.end_stage()
    stage_ffn_down(nc, k)


INPUTS = ['x', 'c', 'w_ada', 'b_ada', 'w_in', 'w_gla_gate2', 'b_gla_gate', 'gla_norm_w', 'hgrn_lb_logits',
          'hgrn_norm_w', 'w_out', 'final_norm_w', 'positions_2', 'norm_mix_g_2', 'w_in_2', 'idx_k_norm_g_2',
          'q_a_norm_g_2', 'kv_a_norm_g_2', 'w_uq_2', 'w_uk_2', 'w_uv_2', 'w_branch_a_2', 'w_branch_b_2',
          'w_out_2', 'norm_ffn_g_2', 'w_up_2', 'conv_w_2', 'conv_b_2', 'w_down_2', 'norm_final_g_2']


def kernel(**inputs):
    import numpy as _np
    import concourse.bacc as _bacc
    from concourse import mybir as _mybir
    from concourse.bass_utils import run_bass_kernel_spmd as _run

    nc = _bacc.Bacc("TRN2", target_bir_lowering=False, num_devices=1, dynamic_dma_scratch_size=1024)
    arrays, views = {}, {}
    for name in INPUTS:
        a = _np.ascontiguousarray(inputs[name])
        arrays[f"in_{name}"] = a
        views[name] = nc.dram_tensor(f"in_{name}", a.shape, _mybir.dt.from_np(a.dtype), kind="ExternalInput").ap()
    views["out"] = nc.dram_tensor("out_0", (1, T, D), _mybir.dt.float32, kind="ExternalOutput").ap()
    build(nc, views)
    r = _run(nc, [arrays], core_ids=[0])
    return r.results[0]["out_0"]
```

```python
import math
import numpy as np
import concourse.bass as bass
from concourse import mybir

F32 = mybir.dt.float32
U32 = mybir.dt.uint32
I32 = mybir.dt.int32
ALU = mybir.AluOpType
ACT = mybir.ActivationFunctionType
AX = mybir.AxisListType

P = 128
T = 1024
NT = T // P
D = 1024
KB = D // P
W512 = 512
EPS = 1e-6
MASKED = -1e30
SBUF_BASE = 1280

QA, KA, VA, LRA, GA, QB, FB, IB, GB, QC, KC, VC, GC = (
    0, 256, 512, 1024, 1040, 1552, 1808, 2064, 2320, 2576, 2832, 3088, 3344)
GLA_TAU = 16.0
RANK = 16
HEADS1 = 4
DK = 64
AQ, AK, AV, IQ, IK, IW, CQ, CKV, KR, GTA, GTB = (
    0, 512, 640, 768, 1280, 1344, 1352, 1608, 1736, 1768, 2792)
TOPK = 256
THETA = 500000.0
DFF = 2816
FBLK = DFF // P


class Steps:

    def __init__(self, k, name):
        self.sem, self.n = k.sem(name), 0

    def mark(self, ins):
        ins.then_inc(self.sem, 1)
        self.n += 1
        return self.n


class Weights:

    RING = 2

    def __init__(self, nc, place):
        self.slot = [place(f"weights_{i}", [P, KB * W512], 8 + 16 * i) for i in range(self.RING)]
        self.landed = [nc.alloc_semaphore(name=f"weights_landed_{i}") for i in range(self.RING)]
        self.freed = {}
        self.chunks = []
        self.issued = 0
        self.count = [0] * self.RING
        self.need = []

    def add(self, pieces, blocks, width):
        self.chunks.append((pieces, blocks, width))
        return len(self.chunks) - 1

    def view(self, n):
        _, blocks, width = self.chunks[n]
        return self.slot[n % self.RING][:, 0:blocks * width].rearrange("p (k n) -> p k n", n=width)

    def load(self, sp, n):
        if n >= self.RING:
            sp.wait_ge(*self.freed[n - self.RING])
        v, i = self.view(n), n % self.RING
        for at, src, width in self.chunks[n][0]:
            sp.dma_start(v[:, :, at:at + width], src.rearrange("(k p) n -> p k n", p=P)).then_inc(self.landed[i], 16)
            self.count[i] += 16
        self.need.append(self.count[i])

    def load_up_to(self, sp, n):
        while self.issued <= min(n, len(self.chunks) - 1):
            self.load(sp, self.issued)
            self.issued += 1

    def wait(self, pe, n):
        pe.wait_ge(self.landed[n % self.RING], self.need[n])


class Kernel:

    def __init__(self, nc):
        self.nc, self.own, self.cleared = nc, [], []

    def sem(self, name):
        self.own.append(self.nc.alloc_semaphore(name=name))
        return self.own[-1]

    def kept_sem(self, name):
        return self.nc.alloc_semaphore(name=name)

    def end_stage(self):
        for sem in self.cleared:
            self.nc.release_semaphore(sem)
        for sem in self.own:
            self.nc.gpsimd.sem_clear(sem)
        self.own, self.cleared = [], self.own


def plan(nc, k):

    def place(name, shape, kb, dt=F32):
        return nc.alloc_sbuf_tensor_at(name, shape, dt, offset=SBUF_BASE + int(kb * 1024))

    k.place = place
    k.ident = place("ident", [P, P], 0)
    k.levels = place("level_masks", [P, 7, P], 0.5)
    k.strict = place("strict_mask", [P, P], 4)
    k.shiftcol = place("shift_col", [P, KB], 4.5)
    k.scalecol = place("scale_col", [P, KB], 4.5625)
    k.small = place("small", [P, 256], 5)
    k.w = Weights(nc, place)
    k.output_stored = k.kept_sem("output_stored")
    k.hT = place("hT", [P, KB, T], 40)
    k.keep = place("keep", [P, T], 208)
    k.oT = place("mixed_outT", [P, KB, T], 72)
    k.banks = nc.alloc_psum_tensor("banks", [P, 8, W512], F32)
    w = k.w
    cols = lambda a, lo, hi: a[:, lo:hi]
    w_in, w_in2 = k.w_in[0], k.w_in_2[0]
    k.c_qka = w.add([(0, cols(w_in, QA, VA), 512)], KB, 512)
    k.c_va = w.add([(0, cols(w_in, VA, LRA), 512)], KB, 512)
    k.c_ga = w.add([(0, cols(w_in, GA, QB), 512)], KB, 512)
    k.c_qfb = w.add([(0, cols(w_in, QB, IB), 512)], KB, 512)
    k.c_igb = w.add([(0, cols(w_in, IB, QC), 512)], KB, 512)
    k.c_qkc = w.add([(0, cols(w_in, QC, VC), 512)], KB, 512)
    k.c_vgc = w.add([(0, cols(w_in, VC, 3600), 512)], KB, 512)
    k.c_out = [w.add([(0, cols(k.w_out[0], h * 512, h * 512 + 512), 512)], KB, 512) for h in range(2)]
    k.c_aq = w.add([(0, cols(w_in2, AQ, AK), 512)], KB, 512)
    k.c_akv = w.add([(0, cols(w_in2, AK, IQ), 256)], KB, 256)
    k.c_iq = w.add([(0, cols(w_in2, IQ, IK), 512)], KB, 512)
    k.c_mix = w.add([(0, cols(w_in2, IK, GTA), GTA - IK)], KB, GTA - IK)
    k.c_gate = [w.add([(0, cols(w_in2, GTA + h * 512, GTA + h * 512 + 512), 512)], KB, 512) for h in range(4)]
    k.c_ba = w.add([(0, k.w_branch_a_2[0], D)], 4, D)
    k.c_bb = w.add([(0, k.w_branch_b_2[0], D)], 4, D)
    k.c_out2 = [w.add([(0, cols(k.w_out_2[0], h * 512, h * 512 + 512), 512)], KB, 512) for h in range(2)]
    up = k.w_up_2[0]
    k.c_up = [w.add([(0, cols(up, f * 256, f * 256 + 256), 256),
                     (256, cols(up, DFF + f * 256, DFF + f * 256 + 256), 256)], KB, 512) for f in range(FBLK // 2)]
    down = k.w_down_2[0]
    k.c_down = [[w.add([(0, down[b * P:min(b + 8, FBLK) * P, h * 512:h * 512 + 512], 512)], min(8, FBLK - b), 512)
                 for b in range(0, FBLK, 8)] for h in range(2)]


class NormTranspose:

    def __init__(self, nc, k, name, x, scratch, out=None):
        self.nc, self.k, self.x, self.scratch, self.bank0 = nc, k, x, scratch, 0
        self.out = x if out is None else out
        self.squares = k.small[:, 0:8]
        self.rms = k.small[:, 8:16]
        self.rstd = k.small[:, 16:24]
        self.root = k.small[:, 24:32]
        s = lambda n: k.sem(f"{name}_{n}")
        self.summed, self.mean, self.rooted, self.inverted = s("summed"), s("mean"), s("rooted"), s("inverted")
        self.divided, self.turned, self.by_act, self.by_dve = s("divided"), s("turned"), s("stored_act"), s("stored_dve")

    def act_stats(self, act, ready):
        for i in range(NT):
            ready(act, i)
            self.nc.scalar.activation(self.scratch[:, i, :], self.x[:, i, :], ACT.Square,
                                      accum_out=self.squares[:, i:i + 1]).then_inc(self.summed, 1)
        act.wait_ge(self.mean, 1)
        self.nc.scalar.activation(self.root, self.rms, ACT.Sqrt).then_inc(self.rooted, 1)

    def dve_stats(self, dve):
        dve.wait_ge(self.summed, NT)
        self.nc.vector.tensor_scalar(self.rms, self.squares, 1.0 / D, EPS, ALU.mult, ALU.add).then_inc(self.mean, 1)
        dve.wait_ge(self.rooted, 1)
        self.nc.vector.reciprocal(self.rstd, self.root).then_inc(self.inverted, 1)
        dve.wait_ge(self.inverted, 1)

    def dve_divide(self, dve):
        for i in range(NT):
            self.nc.vector.tensor_scalar(self.out[:, i, :], self.x[:, i, :], self.rstd[:, i:i + 1], None,
                                         ALU.mult).then_inc(self.divided, 1)

    def pe_transpose(self, pe):
        for i in range(NT):
            pe.wait_ge(self.divided, i + 1)
            for g in range(2):
                j = 2 * i + g
                if j >= 4:
                    pe.wait_ge(self.by_dve if g else self.by_act, (j - 4) // 2 + 1)
                for b in range(4):
                    ins = self.nc.tensor.transpose(self.k.banks[:, self.bank0 + j % 4, b * P:(b + 1) * P],
                                                   self.out[:, i, (4 * g + b) * P:(4 * g + b + 1) * P], self.k.ident[:, :])
                ins.then_inc(self.turned, 1)

    def store(self, eng, g):
        for i in range(NT):
            j = 2 * i + g
            eng.wait_ge(self.turned, j + 1)
            src = self.k.banks[:, self.bank0 + j % 4, :].rearrange("p (b t) -> p b t", t=P)
            dst = self.k.hT[:, 4 * g:4 * g + 4, i * P:(i + 1) * P]
            if g:
                self.nc.vector.tensor_copy(dst, src).then_inc(self.by_dve, 1)
            else:
                self.nc.scalar.activation(dst, src, ACT.Copy).then_inc(self.by_act, 1)


def stage_input(nc, k):
    x = k.place("x_tiles", [P, NT, D], 72)
    ada = k.place("ada_weights", [P, 6, KB, 512], 104)
    gate_bias = k.place("gate_bias", [P, D], 216)
    k.gate_row = k.place("gate_row", [P, D], 212)
    crow = k.place("c_broadcast", [P, KB, P], 204)
    ccol, cact, bcol = k.small[:, 32:40], k.small[:, 40:48], k.small[:, 48:64]
    norm = NormTranspose(nc, k, "norm1", x, k.hT)
    s = lambda n: k.sem(n)
    x_in = [s(f"x_in_{i}") for i in range(2)]
    vec_in, ada_in = s("c_in"), [s(f"ada_in_{i}") for i in range(6)]
    built, silu_done, spread = s("constants_built"), s("c_silu"), s("c_spread")
    ada_mm, gate_mm, cols_done, hmod = s("ada_cols"), s("ada_gate"), s("mod_cols_done"), s("h_modulated")
    pool_step = Steps(k, "pool_step1")
    xd = k.x[0].rearrange("(i p) d -> i p d", p=P)
    wd = k.w_ada[0]
    with nc.Block() as block:
        @block.sync
        def _(sp):
            for h in range(2):
                sp.dma_start(x[:, 4 * h:4 * h + 4, :], xd[4 * h:4 * h + 4].rearrange("i p d -> p i d")).then_inc(x_in[h], 16)
            for n in range(4):
                sp.dma_start(ada[:, n, :, :], wd[:, n * 512:(n + 1) * 512].rearrange("(k p) n -> p k n", p=P)).then_inc(ada_in[n], 16)
            k.w.load_up_to(sp, 0)
            for n in range(4, 6):
                sp.dma_start(ada[:, n, :, :], wd[:, n * 512:(n + 1) * 512].rearrange("(k p) n -> p k n", p=P)).then_inc(ada_in[n], 16)
            k.w.load_up_to(sp, 1)

        @block.gpsimd
        def _(pool):
            pool.memset(k.ident[:, :], 0.0).then_inc(pool_step.sem, 1)
            pool.memset(k.strict[:, :], 1.0).then_inc(pool_step.sem, 1)
            pool.memset(k.levels[:, :, :], 0.0).then_inc(pool_step.sem, 1)
            n = 3
            pool.wait_ge(pool_step.sem, n)
            pool.affine_select(out=k.ident[:, :], in_=k.ident[:, :], compare_op=ALU.not_equal, fill=1.0, base=0,
                               pattern=[[-1, P]], channel_multiplier=1).then_inc(built, 1)
            pool.affine_select(out=k.strict[:, :], in_=k.strict[:, :], compare_op=ALU.is_gt, fill=0.0, base=0,
                               pattern=[[-1, P]], channel_multiplier=1).then_inc(built, 1)
            for l in range(7):
                h = 1 << l
                v = k.levels[:, l, :].rearrange("p (b two h) -> p b two h", two=2, h=h)[:, :, 1, :]
                nb = P // (2 * h)
                pool.memset(v, 1.0).then_inc(pool_step.sem, 1)
                n += 1
                pool.wait_ge(pool_step.sem, n)
                pool.affine_select(out=v, in_=v, compare_op=ALU.is_ge, fill=0.0, base=0,
                                   pattern=[[-2 * h, nb], [0, h]], channel_multiplier=1).then_inc(pool_step.sem, 1)
                n += 1
                pool.wait_ge(pool_step.sem, n)
                pool.affine_select(out=v, in_=v, compare_op=ALU.is_ge, fill=0.0, base=h - 1,
                                   pattern=[[2 * h, nb], [0, h]], channel_multiplier=-1).then_inc(built, 1)

        @block.scalar
        def _(act):
            act.dma_start(ccol, k.c.rearrange("o (k p) -> p (o k)", p=P), allow_slow_non_contiguous=True).then_inc(vec_in, 16)
            act.dma_start(bcol, k.b_ada[0, 0:2 * D].rearrange("(k p) -> p k", p=P), allow_slow_non_contiguous=True).then_inc(vec_in, 16)
            act.dma_start(gate_bias[:, :], k.b_ada[0, 2 * D:3 * D].partition_broadcast(P)).then_inc(vec_in, 16)
            norm.act_stats(act, lambda e, i: e.wait_ge(x_in[i // 4], 16))
            act.wait_ge(vec_in, 48)
            nc.scalar.activation(cact, ccol, ACT.Silu).then_inc(silu_done, 1)
            norm.store(act, 0)
            act.wait_ge(cols_done, 2)
            act.wait_ge(norm.by_dve, NT)
            act.wait_ge(norm.by_act, NT)
            for b in range(0, KB, 2):
                nc.scalar.activation(k.hT[:, b, :], k.hT[:, b, :], ACT.Identity, bias=k.shiftcol[:, b:b + 1],
                                     scale=k.scalecol[:, b:b + 1]).then_inc(hmod, 1)

        @block.tensor
        def _(pe):
            pe.wait_ge(built, 1)
            norm.pe_transpose(pe)
            pe.wait_ge(silu_done, 1)
            for n in range(4):
                pe.wait_ge(ada_in[n], 16)
                for j in range(4):
                    for b in range(KB):
                        ins = nc.tensor.matmul(k.banks[:, 4, 4 * n + j:4 * n + j + 1], ada[:, n, b, j * P:(j + 1) * P],
                                               cact[:, b:b + 1], start=(b == 0), stop=(b == KB - 1))
                ins.then_inc(ada_mm, 1)
            pe.wait_ge(spread, 1)
            for n in range(4, 6):
                pe.wait_ge(ada_in[n], 16)
                for b in range(KB):
                    ins = nc.tensor.matmul(k.banks[:, n + 1, :], crow[:, b, :], ada[:, n, b, :],
                                           start=(b == 0), stop=(b == KB - 1))
                ins.then_inc(gate_mm, 1)

        @block.vector
        def _(dve):
            norm.dve_stats(dve)
            norm.dve_divide(dve)
            dve.wait_ge(silu_done, 1)
            nc.vector.tensor_copy(crow[:, :, :], cact.unsqueeze(2).to_broadcast([P, KB, P])).then_inc(spread, 1)
            norm.store(dve, 1)
            dve.wait_ge(vec_in, 48)
            dve.wait_ge(ada_mm, 4)
            nc.vector.tensor_tensor(k.shiftcol[:, :], k.banks[:, 4, 0:8], bcol[:, 0:8], ALU.add).then_inc(cols_done, 1)
            nc.vector.scalar_tensor_tensor(out=k.scalecol[:, :], in0=k.banks[:, 4, 8:16], scalar=1.0, in1=bcol[:, 8:16],
                                           op0=ALU.add, op1=ALU.add).then_inc(cols_done, 1)
            dve.wait_ge(cols_done, 2)
            dve.wait_ge(norm.by_act, NT)
            dve.wait_ge(norm.by_dve, NT)
            for b in range(1, KB, 2):
                nc.vector.tensor_scalar(k.hT[:, b, :], k.hT[:, b, :], k.scalecol[:, b:b + 1], k.shiftcol[:, b:b + 1],
                                        ALU.mult, ALU.add).then_inc(hmod, 1)
            for h in range(2):
                dve.wait_ge(gate_mm, h + 1)
                nc.vector.tensor_tensor(k.gate_row[:, h * 512:(h + 1) * 512], k.banks[:, 5 + h, :],
                                        gate_bias[:, h * 512:(h + 1) * 512], ALU.add).then_inc(hmod, 1)


class Projection:

    def __init__(self, nc, k, name, jobs, banks=8, src=None):
        self.nc, self.k, self.jobs, self.nb, self.src = nc, k, jobs, banks, src
        self.done = k.sem(f"{name}_product")
        self.stored = {e: k.sem(f"{name}_stored_{e}") for e in ("act", "dve")}
        self.nth = []
        count = {"act": 0, "dve": 0}
        for job in jobs:
            count[job["by"]] += 1
            self.nth.append(count[job["by"]])
            k.w.freed[job["chunk"]] = (self.done, len(self.nth))
        self.count = count

    def bank(self, j):
        return self.k.banks[:, j % self.nb, :]

    def pe_jobs(self, pe, lo, hi):
        k, w = self.k, self.k.w
        src = self.src if self.src is not None else k.hT
        for j in range(lo, hi):
            job = self.jobs[j]
            if j == 0 or self.jobs[j - 1]["chunk"] != job["chunk"]:
                w.wait(pe, job["chunk"])
            if j >= self.nb:
                o = j - self.nb
                pe.wait_ge(self.stored[self.jobs[o]["by"]], self.nth[o])
            wv = w.view(job["chunk"])
            for b in range(KB):
                if job["kind"] == "tokens":
                    i, c0, width = job["tile"], job["col"], job["width"]
                    ins = self.nc.tensor.matmul(self.bank(j)[:, 0:width], src[:, b, i * P:(i + 1) * P],
                                                wv[:, b, c0:c0 + width], start=(b == 0), stop=(b == KB - 1))
                else:
                    c, h = job["col"], job["half"]
                    ins = self.nc.tensor.matmul(self.bank(j), wv[:, b, c:c + P], src[:, b, h * 512:(h + 1) * 512],
                                                start=(b == 0), stop=(b == KB - 1))
            ins.then_inc(self.done, 1)


def feature_jobs(chunk, col, dest, how="copy", by=None):
    return [dict(chunk=chunk, kind="features", col=col, half=h, dest=dest, how=how,
                 by=by or ("act" if h == 0 else "dve")) for h in range(2)]


def token_jobs(chunk, col, width, dest, how="copy", by=None):
    return [dict(chunk=chunk, kind="tokens", tile=i, col=col, width=width, dest=dest, how=how,
                 by=by or ("act" if i % 2 == 0 else "dve")) for i in range(NT)]


def store_act(nc, out, src, how):
    if how == "copy":
        return nc.scalar.activation(out, src, ACT.Copy)
    if how == "silu":
        return nc.scalar.activation(out, src, ACT.Silu)
    if how == "sigmoid":
        return nc.scalar.activation(out, src, ACT.Sigmoid)
    return nc.scalar.activation(out, src, ACT.Copy, scale=float(how))


def store_dve(nc, out, src, how):
    if how == "copy":
        return nc.vector.tensor_copy(out, src)
    return nc.vector.tensor_scalar(out, src, float(how), None, ALU.mult)


def job_out(job):
    if job["kind"] == "tokens":
        return job["dest"](job["tile"])
    return job["dest"][:, job["half"] * 512:(job["half"] + 1) * 512]


def run_stores(nc, proj, eng, who):
    for j, job in enumerate(proj.jobs):
        if job["by"] != who:
            continue
        width = job["width"] if job["kind"] == "tokens" else 512
        eng.wait_ge(proj.done, j + 1)
        store = store_act if who == "act" else store_dve
        store(nc, job_out(job), proj.bank(j)[:, 0:width], job["how"]).then_inc(proj.stored[who], 1)


class Mixer:

    def __init__(self, k, name, dv):
        p = k.place
        self.name, self.dv = name, dv
        self.qT = p(f"{name}_qT", [P, 2, T], 104)
        self.kT = p(f"{name}_kT", [P, 2, T], 112)
        self.bT = p(f"{name}_bT", [P, 2, T], 120)
        self.v = p(f"{name}_v", [P, NT, 4 * dv], 128)
        self.g = p(f"{name}_g", [P, NT, 4 * dv], 144)
        self.t0 = p(f"{name}_t0", [P, 2, T], 160)
        self.t1 = p(f"{name}_t1", [P, 2, T], 168)
        self.t2 = p(f"{name}_t2", [P, 2, T], 176)
        self.keep = k.keep
        self.gain = p(f"{name}_gain", [P, dv], 6)


def softplus_act(nc, act, m, chain, ready):
    ready(act)
    n = chain.mark(nc.scalar.activation(m.t1[:, :, :], m.t0[:, :, :], ACT.Abs))
    act.wait_ge(chain.sem, n)
    n = chain.mark(nc.scalar.activation(m.t1[:, :, :], m.t1[:, :, :], ACT.Exp, scale=-1.0))
    act.wait_ge(chain.sem, n)
    return chain.mark(nc.scalar.activation(m.t1[:, :, :], m.t1[:, :, :], ACT.Ln, bias=1.0))


def summed_decay_dve(nc, dve, m, chain):
    for g in range(2):
        n = chain.mark(nc.vector.tensor_tensor_scan(m.bT[:, g, :], m.keep[:, :], m.t1[:, g, :], 0.0, ALU.mult, ALU.add))
    return n


def stage_gla_projection(nc, k):
    m = k.gla = Mixer(k, "gla", 128)
    p = k.place
    lra_w = p("lra_w", [P, KB, RANK], 184)
    gate2 = p("gate2_w", [RANK, 256], 185)
    lraT = p("lraT", [RANK, T], 188)
    bias = k.small[:, 64:66]
    jobs = []
    for g in range(2):
        jobs += feature_jobs(k.c_qka, g * P, m.qT[:, g, :], DK ** -0.5)
    for g in range(2):
        jobs += feature_jobs(k.c_qka, 256 + g * P, m.kT[:, g, :])
    jobs += token_jobs(k.c_va, 0, 512, lambda i: m.v[:, i, :])
    jobs += token_jobs(k.c_ga, 0, 512, lambda i: m.g[:, i, :], "silu", "act")
    proj = Projection(nc, k, "gla_proj", jobs, banks=6)
    s = lambda n: k.sem(n)
    vec_in, lra_mm, lra_st, z_mm, z_st = s("gla_vec_in"), s("lra_mm"), s("lra_stored"), s("gate_z"), s("gate_z_stored")
    a, d = Steps(k, "gla_gate_act"), Steps(k, "gla_gate_dve")
    with nc.Block() as block:
        @block.sync
        def _(sp):
            k.w.load_up_to(sp, k.c_qfb + 1)

        @block.gpsimd
        def _(pool):
            n = Steps(k, "pool_step2")
            c = n.mark(pool.memset(m.keep[:, :], 1.0))
            pool.wait_ge(n.sem, c)
            pool.memset(m.keep[:, :].rearrange("p (i t) -> p i t", t=P)[:, :, 0:1], 0.0).then_inc(d.sem, 1)

        d.n += 1

        @block.scalar
        def _(act):
            act.dma_start(lra_w[:, :, :], k.w_in[0][:, LRA:GA].rearrange("(k p) n -> p k n", p=P)).then_inc(vec_in, 16)
            act.dma_start(gate2[:, :], k.w_gla_gate2[0]).then_inc(vec_in, 16)
            act.dma_start(bias, k.b_gla_gate[0].rearrange("(k p) -> p k", p=P), allow_slow_non_contiguous=True).then_inc(vec_in, 16)
            act.dma_start(m.gain[:, :], k.gla_norm_w[0].partition_broadcast(P)).then_inc(vec_in, 16)
            for h in range(2):
                act.wait_ge(lra_mm, h + 1)
                nc.scalar.activation(lraT[:, h * 512:(h + 1) * 512], k.banks[0:RANK, 6 + h, :], ACT.Copy).then_inc(lra_st, 1)
            run_stores(nc, proj, act, "act")
            softplus_act(nc, act, m, a, lambda e: e.wait_ge(z_st, 4))

        @block.tensor
        def _(pe):
            pe.wait_ge(vec_in, 64)
            for h in range(2):
                for b in range(KB):
                    ins = nc.tensor.matmul(k.banks[0:RANK, 6 + h, :], lra_w[:, b, :], k.hT[:, b, h * 512:(h + 1) * 512],
                                           start=(b == 0), stop=(b == KB - 1))
                ins.then_inc(lra_mm, 1)
            proj.pe_jobs(pe, 0, 8)
            pe.wait_ge(lra_st, 2)
            for g in range(2):
                if g:
                    proj.pe_jobs(pe, 8, 16)
                    pe.wait_ge(z_st, 2)
                for h in range(2):
                    nc.tensor.matmul(k.banks[:, 6 + h, :], gate2[:, g * P:(g + 1) * P], lraT[:, h * 512:(h + 1) * 512],
                                     start=True, stop=True).then_inc(z_mm, 1)
            proj.pe_jobs(pe, 16, 24)

        @block.vector
        def _(dve):
            def negated(g):
                for h in range(2):
                    dve.wait_ge(z_mm, 2 * g + h + 1)
                    nc.vector.tensor_scalar(m.t0[:, g, h * 512:(h + 1) * 512], k.banks[:, 6 + h, :], bias[:, g:g + 1], -1.0,
                                            ALU.add, ALU.mult).then_inc(z_st, 1)
            dve.wait_ge(vec_in, 64)
            run_stores_range(nc, proj, dve, "dve", 0, 8)
            negated(0)
            run_stores_range(nc, proj, dve, "dve", 8, 16)
            negated(1)
            dve.wait_ge(a.sem, 3)
            dve.wait_ge(z_st, 4)
            n = d.mark(nc.vector.scalar_tensor_tensor(out=m.t1[:, :, :], in0=m.t0[:, :, :], scalar=0.0, in1=m.t1[:, :, :],
                                                      op0=ALU.max, op1=ALU.add))
            dve.wait_ge(d.sem, n)
            n = d.mark(nc.vector.tensor_scalar(m.t1[:, :, :], m.t1[:, :, :], -1.0 / GLA_TAU, None, ALU.mult))
            dve.wait_ge(d.sem, n)
            summed_decay_dve(nc, dve, m, d)


def run_stores_range(nc, proj, eng, who, lo, hi):
    for j in range(lo, hi):
        job = proj.jobs[j]
        if job["by"] != who:
            continue
        width = job["width"] if job["kind"] == "tokens" else 512
        eng.wait_ge(proj.done, j + 1)
        store = store_act if who == "act" else store_dve
        store(nc, job_out(job), proj.bank(j)[:, 0:width], job["how"]).then_inc(proj.stored[who], 1)


def stage_hgrn_projection(nc, k):
    m = k.hgrn = Mixer(k, "hgrn", 64)
    lg, ex, tot, pr, lb, om = (k.small[:, c:c + 2] for c in (66, 68, 70, 72, 74, 76))
    jobs = []
    for g in range(2):
        jobs += feature_jobs(k.c_qfb, g * P, m.qT[:, g, :], "silu", "act")
    for g in range(2):
        jobs += feature_jobs(k.c_qfb, 256 + g * P, m.t2[:, g, :], "copy", "dve")
    jobs += token_jobs(k.c_igb, 0, 256, lambda i: m.v[:, i, :])
    jobs += token_jobs(k.c_igb, 256, 256, lambda i: m.g[:, i, :], "silu", "act")
    proj = Projection(nc, k, "hgrn_proj", jobs)
    vec_in = k.sem("hgrn_vec_in")
    a, d = Steps(k, "hgrn_act"), Steps(k, "hgrn_dve")
    with nc.Block() as block:
        @block.sync
        def _(sp):
            k.w.load_up_to(sp, k.c_qkc + 1)

        @block.scalar
        def _(act):
            act.dma_start(lg, k.hgrn_lb_logits[0].rearrange("(k p) -> p k", p=P), allow_slow_non_contiguous=True).then_inc(vec_in, 16)
            act.dma_start(m.gain[:, :], k.hgrn_norm_w[0].partition_broadcast(P)).then_inc(vec_in, 16)
            run_stores_range(nc, proj, act, "act", 0, 4)
            act.wait_ge(proj.stored["dve"], 4)
            a.mark(nc.scalar.activation(m.kT[:, :, :], m.t2[:, :, :], ACT.Sigmoid, scale=-1.0))
            a.mark(nc.scalar.activation(m.t1[:, :, :], m.t2[:, :, :], ACT.Abs))
            act.wait_ge(d.sem, 1)
            a.mark(nc.scalar.activation(ex, tot, ACT.Exp))
            act.wait_ge(a.sem, 2)
            a.mark(nc.scalar.activation(m.t1[:, :, :], m.t1[:, :, :], ACT.Exp, scale=-1.0))
            act.wait_ge(a.sem, 4)
            a.mark(nc.scalar.activation(m.t1[:, :, :], m.t1[:, :, :], ACT.Ln, bias=1.0))
            act.wait_ge(a.sem, 5)
            a.mark(nc.scalar.activation(m.t0[:, :, :], m.t2[:, :, :], ACT.Exp, scale=-1.0))
            act.wait_ge(d.sem, 8)
            a.mark(nc.scalar.activation(m.t0[:, :, :], m.t0[:, :, :], ACT.Ln))
            run_stores_range(nc, proj, act, "act", 4, len(jobs))

        @block.tensor
        def _(pe):
            proj.pe_jobs(pe, 0, len(jobs))

        @block.vector
        def _(dve):
            run_stores_range(nc, proj, dve, "dve", 0, 8)
            dve.wait_ge(vec_in, 32)
            d.mark(nc.vector.tensor_tensor(tot, lg, lg, ALU.subtract))
            dve.wait_ge(a.sem, 3)
            d.mark(nc.vector.reciprocal(tot, ex))
            dve.wait_ge(d.sem, 2)
            d.mark(nc.vector.tensor_tensor(pr, ex, tot, ALU.mult))
            dve.wait_ge(d.sem, 3)
            d.mark(nc.vector.tensor_tensor(lb, pr, pr, ALU.subtract))
            dve.wait_ge(d.sem, 4)
            d.mark(nc.vector.tensor_scalar(om, lb, -1.0, 1.0, ALU.mult, ALU.add))
            dve.wait_ge(a.sem, 6)
            for g in range(2):
                d.mark(nc.vector.tensor_scalar(m.t0[:, g, :], m.t0[:, g, :], 3e38, lb[:, g:g + 1], ALU.min, ALU.mult))
            dve.wait_ge(d.sem, 7)
            n = d.mark(nc.vector.tensor_scalar(m.t0[:, :, :], m.t0[:, :, :], 1.0, 1.0, ALU.add, ALU.mult))
            for g in range(2):
                d.mark(nc.vector.tensor_scalar(m.kT[:, g, :], m.kT[:, g, :], om[:, g:g + 1], None, ALU.mult))
            n = d.mark(nc.vector.scalar_tensor_tensor(out=m.t1[:, :, :], in0=m.t2[:, :, :], scalar=0.0, in1=m.t1[:, :, :],
                                                      op0=ALU.min, op1=ALU.subtract))
            dve.wait_ge(a.sem, 7)
            dve.wait_ge(d.sem, n)
            n = d.mark(nc.vector.tensor_tensor(m.t1[:, :, :], m.t1[:, :, :], m.t0[:, :, :], ALU.add))
            dve.wait_ge(d.sem, n)
            summed_decay_dve(nc, dve, m, d)
            run_stores_range(nc, proj, dve, "dve", 8, len(jobs))


def stage_gated_attention(nc, k, m, first_block):
    dv, nm = m.dv, m.name
    p = k.place
    E = p(f"{nm}_decay", [P, 2, T], 160)
    C = p(f"{nm}_level_keys", [P, 2, T], 168)
    S = p(f"{nm}_scores", [P, 2, NT, P], 176)
    O = p(f"{nm}_out", [P, NT, 2 * dv], 184)
    slot = 1 if dv == P else 3
    ST = p(f"{nm}_state", [P, NT, slot + 1, dv], 192)
    qe = p(f"{nm}_q_decayed", [P, T], 200)
    ke = p(f"{nm}_k_decayed", [P, T], 204)
    ktok = p(f"{nm}_k_tokens", [P, NT, P], 216)
    junk = p(f"{nm}_square_scratch", [P, 2, P], 220)
    qpad = p(f"{nm}_q_padded", [P, 2, T], 88 if dv == P else 136)
    Q = p(f"{nm}_level_queries", [P, 2, 2, T // 2], 96)
    own = k.small[:, 248:250]
    dec = k.small[:, 80:88]
    ssq, ms, root, rstd = (k.small[:, c:c + 16] for c in (96, 112, 128, 144))
    nob = 2 * dv // P
    sname = lambda n: k.sem(f"{nm}_{n}")
    diff, expd, level_k, level_q = sname("diff"), sname("exp"), sname("level_keys"), sname("level_queries")
    score, picked, prod, diag = sname("score"), sname("picked"), sname("qk"), sname("diagonal")
    pre, eb, kd, qd, padq = sname("state_diff"), sname("state_exp"), sname("k_decayed"), sname("q_decayed"), sname("q_padded")
    kt_mm, kt_st, u_mm, rec, zeroed = sname("k_turned"), sname("k_stored"), sname("state_added"), sname("state_done"), sname("zeroed")
    o_mm, o_st, turned, t_st = sname("o_product"), sname("o_stored"), sname("o_turned"), sname("oT_stored")
    squares, gained, rec0 = sname("squares"), sname("gate_gained"), sname("state_head0")
    dn, an, an_o = Steps(k, f"{nm}_dve_norm"), Steps(k, f"{nm}_act_norm"), Steps(k, f"{nm}_act_out")
    bank = lambda b: k.banks[:, b, :]
    base = lambda s: 4 + 2 * (s % 2)
    PICKS = 1 + 4 * 7
    picks = lambda s: PICKS * (s // 8) + 1 + 4 * (s % 8)

    def halves(ap2d, h):
        return ap2d.rearrange("p (n two h) -> p n two h", two=2, h=h)

    def out_of(i, hh):
        c = (i % 2) * 256 + hh * P
        return bank(i // 2), c, c + (hh * dv if dv < P else 0)

    with nc.Block() as block:
        @block.gpsimd
        def _(pool):
            for g in range(2):
                if g:
                    pool.wait_ge(o_mm, 4)
                pool.tensor_tensor(qe[:, :], m.qT[:, g, :], m.kT[:, g, :], ALU.mult).then_inc(prod, 1)
                for l in range(7):
                    s, h = 7 * g + l, 1 << l
                    pool.wait_ge(expd, s + 1)
                    pool.wait_ge(padq, 2 * g + 2)
                    if s >= 2:
                        pool.wait_ge(score, 2 * (s - 1))
                    for hh in range(2):
                        q4 = halves(qpad[:, hh, :], h)[:, :, 1, :]
                        pool.tensor_tensor(Q[:, s % 2, hh, :].rearrange("p (n h) -> p n h", h=h),
                                           halves(E[:, s % 2, :], h)[:, :, 1, :], q4, ALU.mult).then_inc(level_q, 1)
                    if l == 4:
                        pool.wait_ge(eb, 3 * g + 3)
                        pool.tensor_tensor(qe[:, :], qe[:, :], m.qT[:, g, :], ALU.mult).then_inc(qd, 1)
                if g == 0:
                    gv = m.g[:, :, :].rearrange("p i (h v) -> p (i h) v", v=dv)
                    pool.tensor_tensor(gv, gv, m.gain[:, :].unsqueeze(1).to_broadcast([P, 4 * NT, dv]), ALU.mult).then_inc(gained, 1)

        @block.scalar
        def _(act):
            def exponential(s):
                act.wait_ge(diff, 2 * (s + 1))
                nc.scalar.activation(E[:, s % 2, :], E[:, s % 2, :], ACT.Exp).then_inc(expd, 1)

            def store_out(g):
                for b in range(4):
                    act.wait_ge(o_mm, 4 * g + b + 1)
                    if b == 0 and g:
                        act.wait_ge(turned, nob * 2)
                    for i in (2 * b, 2 * b + 1):
                        for hh in range(2):
                            c, n = out_of(i, hh)[2], 2 * i + hh + 16 * g
                            if n >= 2:
                                act.wait_ge(squares, n - 1)
                            nc.scalar.activation(junk[:, n % 2, 0:dv], bank(b)[:, c:c + dv], ACT.Square,
                                                 accum_out=ssq[:, 2 * i + hh:2 * i + hh + 1]).then_inc(squares, 1)
                    if dv == P:
                        dst, src = O[:, 2 * b:2 * b + 2, :], bank(b).rearrange("p (i v) -> p i v", i=2)
                        nc.scalar.activation(dst, src, ACT.Copy).then_inc(o_st, 1)
                    else:
                        for i in (0, 1):
                            src = bank(b)[:, i * 256:(i + 1) * 256].rearrange("p (four f) -> p four f", f=dv)[:, 0::3, :]
                            ins = nc.scalar.activation(O[:, 2 * b + i, :].rearrange("p (h f) -> p h f", f=dv), src, ACT.Copy)
                            if i:
                                ins.then_inc(o_st, 1)
                            else:
                                an_o.mark(ins)

            def take_root(g):
                act.wait_ge(dn.sem, 4 * g + 1)
                an.mark(nc.scalar.activation(root, ms, ACT.Sqrt))

            def store_turned(g):
                for b in range(nob * 2):
                    act.wait_ge(turned, nob * 2 * g + b + 1)
                    fb, half = b // 2, b % 2
                    nc.scalar.activation(k.oT[:, first_block + nob * g + fb, half * 512:(half + 1) * 512], bank(4 + b),
                                         ACT.Copy).then_inc(t_st, 1)

            for g in range(2):
                act.wait_ge(pre, g + 1)
                nc.scalar.activation(ke[:, :], ke[:, :], ACT.Exp).then_inc(eb, 1)
                if g:
                    act.wait_ge(rec, NT)
                nc.scalar.activation(dec, m.bT[:, g, :].rearrange("p (i t) -> p i t", t=P)[:, :, P - 1], ACT.Exp).then_inc(eb, 1)
                exponential(7 * g)
                act.wait_ge(zeroed, 5)
                if g:
                    act.wait_ge(level_q, 14)
                for hh in range(2):
                    nc.scalar.activation(qpad[:, hh, :], m.qT[:, g, :], ACT.Copy, scale=own[:, hh:hh + 1]).then_inc(padq, 1)
                exponential(7 * g + 1)
                for h in range(2):
                    act.wait_ge(kt_mm, 2 * g + h + 1)
                    nc.scalar.activation(ktok[:, 4 * h:4 * h + 4, :], bank(h).rearrange("p (i t) -> p i t", t=P),
                                         ACT.Copy).then_inc(kt_st, 1)
                act.wait_ge(diag, g + 1)
                nc.scalar.activation(qe[:, :], m.bT[:, g, :], ACT.Exp).then_inc(eb, 1)
                for l in range(2, 7):
                    exponential(7 * g + l)
                if g:
                    take_root(0)
                    store_turned(0)
                store_out(g)
            take_root(1)
            store_turned(1)

        @block.tensor
        def _(pe):
            def turn_out(g):
                pe.wait_ge(dn.sem, 4 * (g + 1))
                if g:
                    pe.wait_ge(t_st, nob * 2)
                for b in range(nob * 2):
                    fb, half = b // 2, b % 2
                    for i in range(4):
                        ins = nc.tensor.transpose(bank(4 + b)[:, i * P:(i + 1) * P], O[:, 4 * half + i, fb * P:(fb + 1) * P],
                                                  k.ident[:, :])
                    ins.then_inc(turned, 1)

            pe.wait_ge(zeroed, 5)
            for g in range(2):
                pe.wait_ge(kd, g + 1)
                if g:
                    pe.wait_ge(o_st, 4)
                for i in range(NT):
                    ins = nc.tensor.transpose(bank(i // 4)[:, (i % 4) * P:(i % 4 + 1) * P], ke[:, i * P:(i + 1) * P], k.ident[:, :])
                    if i % 4 == 3:
                        ins.then_inc(kt_mm, 1)
                pe.wait_ge(prod, g + 1)
                if g:
                    pe.wait_ge(picked, picks(8 * g - 2))
                d16 = bank(base(8 * g))[:, 0:16].rearrange("p (h i) -> p h i", i=NT)
                for i in range(NT):
                    ins = nc.tensor.matmul(d16[:, :, i], qe[:, i * P:(i + 1) * P], own, start=True, stop=True)
                ins.then_inc(diag, 1)
                for st in range(1, 8):
                    s, l = 8 * g + st, 7 * g + st - 1
                    pe.wait_ge(level_k, l + 1)
                    pe.wait_ge(level_q, 2 * (l + 1))
                    if s >= 2:
                        pe.wait_ge(picked, picks(s - 2))
                    for i in range(NT):
                        out = bank(base(s) + i // 4).rearrange("p (h i t) -> p h i t", h=2, i=4)[:, :, i % 4, :]
                        ins = nc.tensor.matmul(out, C[:, l % 2, i * P:(i + 1) * P], Q[:, l % 2, :, i * 64:(i + 1) * 64],
                                               start=True, stop=True)
                        if i % 4 == 3:
                            ins.then_inc(score, 1)
                    if st == 1:
                        pe.wait_ge(kt_st, 2 * g + 2)
                        for i in range(NT):
                            for hh in range(2):
                                c = i * dv
                                ins = nc.tensor.matmul(bank(2 + c // 512)[64 * hh:64 * hh + 64, c % 512:c % 512 + dv],
                                                       ktok[:, i, 64 * hh:64 * hh + 64],
                                                       m.v[:, i, (2 * g + hh) * dv:(2 * g + hh + 1) * dv], start=True, stop=True)
                        ins.then_inc(u_mm, 1)
                pe.wait_ge(picked, PICKS * (g + 1))
                if g:
                    turn_out(0)
                pe.wait_ge(rec, NT * (g + 1))
                pe.wait_ge(qd, g + 1)
                for i in range(NT):
                    if i:
                        c = (i % 2) * 256
                        nc.tensor.matmul(bank(i // 2)[:, c:c + 256], qe[:, i * P:(i + 1) * P], ST[:, i, :, :], start=True, stop=False)
                    for hh in range(2):
                        bk, c, _ = out_of(i, hh)
                        lo = (2 * g + hh) * dv if dv == P else 2 * g * dv
                        ins = nc.tensor.matmul(bk[:, c:c + P], S[:, hh, i, :], m.v[:, i, lo:lo + P], start=(i == 0),
                                               stop=(i == 0 or hh == 1))
                    if i % 2:
                        ins.then_inc(o_mm, 1)
            turn_out(1)

        @block.vector
        def _(dve):
            V = nc.vector

            def norm(g):
                v3 = lambda ap: ap.rearrange("p i (h v) -> p (i h) v", v=dv)
                dve.wait_ge(squares, 16 * (g + 1))
                dn.mark(V.tensor_scalar(ms, ssq, 1.0 / dv, EPS, ALU.mult, ALU.add))
                dve.wait_ge(an.sem, g + 1)
                dn.mark(V.reciprocal(rstd, root))
                dve.wait_ge(dn.sem, 4 * g + 2)
                dve.wait_ge(o_st, 4 * (g + 1))
                dn.mark(V.tensor_tensor(v3(O[:, :, :]), v3(O[:, :, :]), rstd.unsqueeze(2).to_broadcast([P, 16, dv]), ALU.mult))
                dve.wait_ge(dn.sem, 4 * g + 3)
                dve.wait_ge(gained, 1)
                dn.mark(V.tensor_tensor(O[:, :, :], O[:, :, :], m.g[:, :, 2 * g * dv:(2 * g + 2) * dv], ALU.mult))

            for g in range(2):
                b3 = m.bT[:, g, :].rearrange("p (i t) -> p i t", t=P)
                V.tensor_tensor(ke[:, :].rearrange("p (i t) -> p i t", t=P),
                                b3[:, :, P - 1:P].to_broadcast([P, NT, P]), b3, ALU.subtract).then_inc(pre, 1)

                def differences(l):
                    s, h = 7 * g + l, 1 << l
                    b4, e = halves(m.bT[:, g, :], h), halves(E[:, s % 2, :], h)
                    mid = b4[:, :, 0, h - 1:h].to_broadcast([P, T // (2 * h), h])
                    if s >= 2:
                        dve.wait_ge(level_q, 2 * (s - 1))
                        dve.wait_ge(level_k, s - 1)
                    V.tensor_tensor(e[:, :, 0, :], mid, b4[:, :, 0, :], ALU.subtract).then_inc(diff, 1)
                    V.tensor_tensor(e[:, :, 1, :], b4[:, :, 1, :], mid, ALU.subtract).then_inc(diff, 1)

                def keys(l):
                    s, h = 7 * g + l, 1 << l
                    dve.wait_ge(expd, s + 1)
                    if s >= 2:
                        dve.wait_ge(score, 2 * (s - 1))
                    V.tensor_tensor(halves(C[:, s % 2, :], h)[:, :, 0, :], halves(E[:, s % 2, :], h)[:, :, 0, :],
                                    halves(m.kT[:, g, :], h)[:, :, 0, :], ALU.mult).then_inc(level_k, 1)

                def pick(l):
                    h = 1 << l
                    s = 8 * g + l + 1
                    mask = halves(k.levels[:, l, :], h)[:, :, 1, :].bitcast(U32).unsqueeze(1).to_broadcast([P, 4, 64 // h, h])
                    dve.wait_ge(picked, picks(s - 1))
                    for half in range(2):
                        dve.wait_ge(score, 2 * (7 * g + l) + half + 1)
                        src = bank(base(s) + half).rearrange("p (hh i b h) -> p hh i b h", hh=2, i=4, h=h)
                        for hh in range(2):
                            dst = S[:, hh, 4 * half:4 * half + 4, :].rearrange("p i (b two h) -> p i b two h", two=2, h=h)
                            V.copy_predicated(dst[:, :, :, 1, :], mask, src[:, hh, :, :, :]).then_inc(picked, 1)

                def diagonal():
                    dve.wait_ge(diag, g + 1)
                    if g:
                        dve.wait_ge(o_mm, 4)
                    d16 = bank(base(8 * g))[:, 0:16].rearrange("p (h i) -> p h i", i=NT)
                    V.tensor_tensor(S[:, :, :, :], k.ident[:, :].unsqueeze(1).unsqueeze(1).to_broadcast([P, 2, NT, P]),
                                    d16.unsqueeze(3).to_broadcast([P, 2, NT, P]), ALU.mult).then_inc(picked, 1)

                def states():
                    dve.wait_ge(u_mm, g + 1)
                    dve.wait_ge(eb, 3 * g + 2)
                    for i in range(NT - 1):
                        c = i * dv
                        if i:
                            dve.wait_ge(rec, NT * g + i)
                        for hh in range(2):
                            rows = slice(64 * hh, 64 * hh + 64)
                            u = k.banks[rows, 2 + c // 512, c % 512:c % 512 + dv]
                            if i == 0:
                                ins = V.tensor_copy(ST[rows, 1, slot * hh, :], u)
                            else:
                                ins = V.scalar_tensor_tensor(out=ST[rows, i + 1, slot * hh, :], in0=ST[rows, i, slot * hh, :],
                                                             scalar=dec[rows, i:i + 1], in1=u, op0=ALU.mult, op1=ALU.add)
                            if hh:
                                ins.then_inc(rec, 1)
                            else:
                                ins.then_inc(rec0, 1)
                        dve.wait_ge(rec0, (NT - 1) * g + i + 1)
                    V.memset(k.small[:, 78:79], 0.0).then_inc(rec, 1)

                differences(0)
                if g == 0:
                    for hh in range(2):
                        for rows in range(2):
                            V.memset(own[64 * rows:64 * rows + 64, hh:hh + 1], float(hh == rows)).then_inc(zeroed, 1)
                    V.memset(C[:, :, :], 0.0).then_inc(zeroed, 1)
                    V.memset(ST[:, :, :, :], 0.0).then_inc(zeroed, 1)
                dve.wait_ge(eb, 3 * g + 1)
                V.tensor_tensor(ke[:, :], ke[:, :], m.kT[:, g, :], ALU.mult).then_inc(kd, 1)
                differences(1)
                dve.wait_ge(zeroed, 6)
                keys(0)
                differences(2)
                diagonal()
                for l in range(1, 7):
                    keys(l)
                    if l <= 4:
                        differences(l + 2)
                    pick(l - 1)
                    if l == 2:
                        states()
                    if l == 4 and g:
                        norm(0)
                pick(6)
            norm(1)


def stage_stick_projection(nc, k):
    p = k.place
    k.sb_qT, k.sb_kT = p("sb_qT", [P, 2, T], 104), p("sb_kT", [P, 2, T], 112)
    k.sb_v, k.sb_gT = p("sb_v", [P, NT, 256], 120), p("sb_gT", [P, 2, T], 128)
    k.sb_k = p("sb_keys_padded", [P, 4, T], 192)
    padded = Steps(k, "sb_keys_padded")
    jobs = []
    for g in range(2):
        jobs += feature_jobs(k.c_qkc, g * P, k.sb_qT[:, g, :])
    for g in range(2):
        jobs += feature_jobs(k.c_qkc, 256 + g * P, k.sb_kT[:, g, :])
    jobs += token_jobs(k.c_vgc, 0, 256, lambda i: k.sb_v[:, i, :])
    for g in range(2):
        jobs += feature_jobs(k.c_vgc, 256 + g * P, k.sb_gT[:, g, :], "silu", "act")
    proj = Projection(nc, k, "stick_proj", jobs)
    with nc.Block() as block:
        @block.sync
        def _(sp):
            k.w.load_up_to(sp, k.c_out[1])

        @block.gpsimd
        def _(pool):
            pool.wait_ge(proj.stored["act"], 4)
            pool.wait_ge(proj.stored["dve"], 4)
            for g in range(2):
                pad_keys(pool, k.sb_k[:, 2 * g:2 * g + 2, :], lambda rows: k.sb_kT[rows, g, :], padded)

        @block.scalar
        def _(act):
            run_stores(nc, proj, act, "act")

        @block.tensor
        def _(pe):
            proj.pe_jobs(pe, 0, len(jobs))

        @block.vector
        def _(dve):
            run_stores(nc, proj, dve, "dve")


def stage_stick_attention(nc, k):
    p = k.place
    A = p("sb_rest", [P, 2, T], 136)
    B = p("sb_weight", [P, 2, T], 144)
    WT = p("sb_weightT", [P, 2, NT, P], 152)
    R = p("sb_rest_product", [P, T], 216)
    other = p("not_strict", [P, P], 6.5)
    ones = p("ones", [P, P], 220)
    items = [(i, h) for i in range(NT) for h in range(4)]
    N = len(items)
    nb = [2 if i >= 4 else 1 for i, h in items]
    upto = [sum(nb[:n + 1]) for n in range(N)]
    two = [sum(b == 2 for b in nb[:n + 1]) for n in range(N)]
    s = lambda n: k.sem("sb_" + n)
    z_mm, rest, taken, w_done = s("z"), s("rest"), s("taken"), s("w")
    t_mm, wt_act, wt_dve, pv, o_done = s("turned"), s("wT_act"), s("wT_dve"), s("out"), s("out_stored")
    d = Steps(k, "sb_dve")
    x_in = k.kept_sem("x_again")
    k.x_again = x_in
    k.xres = p("x_residual", [P, NT, D], 160)
    sc = DK ** -0.5

    def width(n):
        return (items[n][0] + 1) * P

    def z(n):
        return k.banks[:, 2 * (n % 2):2 * (n % 2) + 2, :].rearrange("p b c -> p (b c)")[:, 0:width(n)]

    with nc.Block() as block:
        @block.sync
        def _(sp):
            sp.dma_start(k.xres[:, :, :], k.x[0].rearrange("(i p) d -> p i d", p=P)).then_inc(x_in, 16)

        @block.scalar
        def _(act):
            def sigmoids(n):
                w = width(n)
                act.wait_ge(z_mm, n + 1)
                if n >= 2:
                    act.wait_ge(w_done, n - 1)
                    act.wait_ge(t_mm, upto[n - 2])
                nc.scalar.activation(A[:, n % 2, 0:w], z(n), ACT.Sigmoid, scale=-sc).then_inc(rest, 1)
                nc.scalar.activation(B[:, n % 2, 0:w], z(n), ACT.Sigmoid, scale=sc).then_inc(taken, 1)

            sigmoids(0)
            for n in range(N):
                if n + 1 < N:
                    sigmoids(n + 1)
                act.wait_ge(t_mm, (upto[n - 1] if n else 0) + 1)
                if n >= 2:
                    act.wait_ge(pv, n - 1)
                m = min(items[n][0] + 1, 4)
                nc.scalar.activation(WT[:, n % 2, 0:m, :], k.banks[:, 4, 0:m * P].rearrange("p (j t) -> p j t", t=P),
                                     ACT.Copy).then_inc(wt_act, 1)

        @block.tensor
        def _(pe):
            def scores(n):
                i, h = items[n]
                w = width(n)
                if n >= 2:
                    pe.wait_ge(taken, n - 1)
                for c in range(0, w, 512):
                    e = min(w, c + 512)
                    ins = nc.tensor.matmul(z(n)[:, c:e], k.sb_qT[:, h // 2, i * P:(i + 1) * P],
                                           k.sb_k[:, h, c:e], start=True, stop=True)
                ins.then_inc(z_mm, 1)

            def values(n):
                i, h = items[n]
                if n >= 2:
                    pe.wait_ge(o_done, n - 1)
                out = k.banks[64 * (h % 2):64 * (h % 2) + 64, 6 + n % 2, 0:P]
                for j in range(i + 1):
                    if j == 0:
                        pe.wait_ge(wt_act, n + 1)
                    if j == 4:
                        pe.wait_ge(wt_dve, two[n])
                    ins = nc.tensor.matmul(out, k.sb_v[:, j, h * 64:(h + 1) * 64], WT[:, n % 2, j, :],
                                           start=(j == 0), stop=(j == i))
                ins.then_inc(pv, 1)

            scores(0)
            scores(1)
            for n, (i, h) in enumerate(items):
                pe.wait_ge(w_done, n + 1)
                for j in range(i + 1):
                    if j == 0 and n:
                        pe.wait_ge(wt_act, n)
                    if j == 4 and two[n] > 1:
                        pe.wait_ge(wt_dve, two[n] - 1)
                    ins = nc.tensor.transpose(k.banks[:, 4 + j // 4, (j % 4) * P:(j % 4 + 1) * P],
                                              B[:, n % 2, j * P:(j + 1) * P], k.ident[:, :])
                    if j == min(i, 3) or j == i:
                        ins.then_inc(t_mm, 1)
                if n:
                    values(n - 1)
                if n + 2 < N:
                    scores(n + 2)
            values(N - 1)

        @block.vector
        def _(dve):
            d.mark(nc.vector.memset(ones[:, :], 1.0))
            c0 = d.mark(nc.vector.tensor_scalar(other[:, :], k.strict[:, :], -1.0, 1.0, ALU.mult, ALU.add))
            dve.wait_ge(d.sem, c0)

            def weights(n):
                w = width(n)
                a, b, r = A[:, n % 2, 0:w], B[:, n % 2, 0:w], R[:, 0:w]
                dve.wait_ge(rest, n + 1)
                c = d.mark(nc.vector.copy_predicated(a[:, w - P:w], other[:, :].bitcast(U32), ones[:, :]))
                dve.wait_ge(taken, n + 1)
                d.mark(nc.vector.tensor_tensor(b[:, w - P:w], b[:, w - P:w], k.strict[:, :], ALU.mult))
                dve.wait_ge(d.sem, c)
                d.mark(nc.vector.tensor_tensor_scan(r[:, ::-1], a[:, ::-1], a[:, ::-1], 1.0, ALU.mult, ALU.min))
                dve.wait_ge(d.sem, d.n)
                nc.vector.tensor_tensor(b[:, 0:w - 1], b[:, 0:w - 1], r[:, 1:w], ALU.mult).then_inc(w_done, 1)
                dve.wait_ge(w_done, n + 1)

            def turned_weights(n):
                if nb[n] == 2:
                    dve.wait_ge(t_mm, upto[n])
                    if two[n] > 2:
                        dve.wait_ge(pv, n - 1)
                    nc.vector.tensor_copy(WT[:, n % 2, 4:items[n][0] + 1, :],
                                          k.banks[:, 5, 0:(items[n][0] - 3) * P].rearrange("p (j t) -> p j t", t=P)).then_inc(wt_dve, 1)

            def store(n):
                i, h = items[n]
                dve.wait_ge(pv, n + 1)
                rows = slice(64 * (h % 2), 64 * (h % 2) + 64)
                tok = slice(i * P, (i + 1) * P)
                nc.vector.tensor_tensor(k.oT[rows, 6 + h // 2, tok], k.banks[rows, 6 + n % 2, 0:P],
                                        k.sb_gT[rows, h // 2, tok], ALU.mult).then_inc(o_done, 1)

            weights(0)
            for n, (i, h) in enumerate(items):
                if n + 1 < N:
                    weights(n + 1)
                turned_weights(n)
                if n:
                    store(n - 1)
            store(N - 1)


def stage_first_output(nc, k):
    p = k.place
    x = k.xres
    fnw = p("final_norm_row", [P, D], 104)
    tmp = p("gated_y", [P, 2, 512], 108)
    mixg = k.small[:, 160:168]
    sq1, ms1, rt1, rs1 = (k.small[:, c:c + 8] for c in (168, 176, 184, 192))
    jobs = [dict(chunk=k.c_out[h], kind="tokens", tile=i, col=0, width=512, by="dve", dest=h, how="gate")
            for i in range(NT) for h in range(2)]
    proj = Projection(nc, k, "first_out", jobs, banks=6, src=k.oT)
    norm = NormTranspose(nc, k, "norm2", x, k.hT, p("x1_normed", [P, NT, D], 112))
    s = lambda n: k.sem(n)
    vec_in, added, summed, gained, x1_done = s("fnw_in"), s("residual_added"), s("x1_summed"), s("hT_gained"), s("x1_done")
    x1_out = k.sem("x1_out")
    d = Steps(k, "first_out_dve")
    a = Steps(k, "first_out_act")
    with nc.Block() as block:
        @block.sync
        def _(sp):
            sp.wait_ge(x1_done, NT)
            sp.dma_start(k.x1_dram.rearrange("(i p) d -> p i d", p=P), x[:, :, :]).then_inc(x1_out, 16)
            k.w.load_up_to(sp, k.c_akv)
            sp.wait_ge(x1_out, 16)

        @block.gpsimd
        def _(pool):
            pool.wait_ge(k.x_again, 16)
            for j, job in enumerate(jobs):
                i, h = job["tile"], job["dest"]
                pool.wait_ge(proj.stored["dve"], j + 1)
                xs = x[:, i, h * 512:(h + 1) * 512]
                pool.tensor_tensor(xs, xs, tmp[:, j % 2, :], ALU.add).then_inc(added, 1)

        @block.scalar
        def _(act):
            act.dma_start(fnw[:, :], k.final_norm_w.partition_broadcast(P)).then_inc(vec_in, 16)
            act.dma_start(mixg, k.norm_mix_g_2[0].rearrange("(k p) -> p k", p=P), allow_slow_non_contiguous=True).then_inc(vec_in, 16)
            for i in range(NT):
                act.wait_ge(added, 2 * i + 2)
                nc.scalar.activation(k.hT[:, i, :], x[:, i, :], ACT.Square, accum_out=sq1[:, i:i + 1]).then_inc(summed, 1)
            act.wait_ge(d.sem, 1)
            a.mark(nc.scalar.activation(rt1, ms1, ACT.Sqrt))
            act.wait_ge(summed, NT)
            norm.act_stats(act, lambda e, i: e.wait_ge(x1_done, i + 1))
            norm.store(act, 0)

        @block.tensor
        def _(pe):
            proj.pe_jobs(pe, 0, len(jobs))
            pe.wait_ge(proj.stored["dve"], len(jobs))
            norm.pe_transpose(pe)

        @block.vector
        def _(dve):
            for j, job in enumerate(jobs):
                dve.wait_ge(proj.done, j + 1)
                if j >= 2:
                    dve.wait_ge(added, j - 1)
                h = job["dest"]
                nc.vector.tensor_tensor(tmp[:, j % 2, :], proj.bank(j), k.gate_row[:, h * 512:(h + 1) * 512],
                                        ALU.mult).then_inc(proj.stored["dve"], 1)
            dve.wait_ge(summed, NT)
            d.mark(nc.vector.tensor_scalar(ms1, sq1, 1.0 / D, EPS, ALU.mult, ALU.add))
            dve.wait_ge(a.sem, 1)
            n = d.mark(nc.vector.reciprocal(rs1, rt1))
            dve.wait_ge(d.sem, n)
            dve.wait_ge(vec_in, 32)
            dve.wait_ge(added, 16)
            for i in range(NT):
                nc.vector.scalar_tensor_tensor(out=x[:, i, :], in0=x[:, i, :], scalar=rs1[:, i:i + 1], in1=fnw[:, :],
                                               op0=ALU.mult, op1=ALU.mult).then_inc(x1_done, 1)
            norm.dve_stats(dve)
            norm.dve_divide(dve)
            norm.store(dve, 1)
            dve.wait_ge(norm.by_act, NT)
            dve.wait_ge(norm.by_dve, NT)
            for b in range(KB):
                nc.vector.tensor_scalar(k.hT[:, b, :], k.hT[:, b, :], mixg[:, b:b + 1], None, ALU.mult).then_inc(gained, 1)


def rope_dve(nc, dve, d, x1, x2, cos, sin, t):
    V = nc.vector
    d.mark(V.tensor_tensor(t[0], x1, cos, ALU.mult))
    d.mark(V.tensor_tensor(t[1], x2, sin, ALU.mult))
    d.mark(V.tensor_tensor(t[2], x1, sin, ALU.mult))
    n = d.mark(V.tensor_tensor(t[3], x2, cos, ALU.mult))
    dve.wait_ge(d.sem, n)
    d.mark(V.tensor_tensor(x1, t[0], t[1], ALU.subtract))
    return d.mark(V.tensor_tensor(x2, t[2], t[3], ALU.add))


def stage_second_projection(nc, k):
    p = k.place
    aq = p("aq_tok", [P, NT, 512], 72)
    k.akv = p("akv_tok", [P, NT, 256], 88)
    iq = p("iq_tok", [P, NT, 512], 96)
    mix = p("mix_tok", [P, NT, GTA - IK], 112)
    k.cos, k.sin = p("cos_table", [P, NT, 24], 0.5), p("sin_table", [P, NT, 24], 1.25)
    k.aqT, k.iqT = p("aqT", [P, 4, T], 129), p("iqT", [P, 4, T], 145)
    k.akT, k.ikT = p("akT", [P, 2, T], 161), p("ikT", [P, T], 169)
    k.cqT, k.ckvT, k.krT = p("cqT", [P, 2, T], 173), p("ckvT", [P, T], 181), p("krT", [P, T], 185)
    sq = p("mix_squares", [P, NT, 456], 189)
    t4 = p("rope_products", [P, 4, 512], 203.5)
    ik2 = p("ik_twice", [P, NT, P], 211.5)
    ak4 = p("ak_twice", [P, NT, 256], 189)
    sm = k.small
    k.posq, k.iw = p("pos_col", [P, NT], 7), p("iw", [P, NT, 8], 7.0625)
    posi = sm[:, 200:208].bitcast(I32)
    inv = p("inv_freq", [P, 24], 7.375)
    ikg = p("ik_gain", [P, 64], 7.5)
    qg, kvg = sm[:, 208:210], sm[:, 210:211]
    ms, rt, rs = p("mix_mean", [P, 3, NT], 7.875), p("mix_root", [P, 3, NT], 6.0), p("mix_rstd", [P, 3, NT], 6.125)
    r, turns, ab, angv = (t4[:, c, 0:192].rearrange("p (i f) -> p i f", i=NT) for c in range(4))
    c_ik, c_iw, c_cq, c_ckv, c_kr = 0, IW - IK, CQ - IK, CKV - IK, KR - IK
    jobs = token_jobs(k.c_aq, 0, 512, lambda i: aq[:, i, :], 64 ** -0.5)
    jobs += token_jobs(k.c_akv, 0, 256, lambda i: k.akv[:, i, :])
    jobs += token_jobs(k.c_iq, 0, 512, lambda i: iq[:, i, :], 64 ** -0.5)
    jobs += token_jobs(k.c_mix, 0, GTA - IK, lambda i: mix[:, i, :])
    proj = Projection(nc, k, "second_proj", jobs)
    s = lambda n: k.sem(n)
    vec_in, table, rooted, copies, turned = s("second_vec_in"), s("angles"), s("mix_rooted"), s("twice"), s("heads_turned")
    by_act, by_dve, ready = s("heads_act"), s("heads_dve"), s("heads_ready")
    d = Steps(k, "second_dve")
    pl = Steps(k, "second_pool")
    C1 = 6.28125
    C2 = float(np.float32(np.round((2 * math.pi - C1) * 2 ** 20) / 2 ** 20))
    C3 = float(np.float32(2 * math.pi - C1 - C2))
    MAGIC = 1.5 * 2 ** 23
    freq = [float(THETA ** (-np.float32(2 * j) / np.float32(16))) for j in range(8)]
    freq += [float(THETA ** (-np.float32(2 * j) / np.float32(32))) for j in range(16)]

    with nc.Block() as block:
        @block.sync
        def _(sp):
            k.w.load_up_to(sp, k.c_gate[1])

        @block.gpsimd
        def _(pool):
            for f, v in enumerate(freq):
                pool.memset(inv[:, f:f + 1], v).then_inc(pl.sem, 1)
            pool.wait_ge(ready, 1)
            pool.tensor_copy(ik2[:, :, :].rearrange("p i (two f) -> p i two f", two=2),
                             mix[:, :, 0:64].unsqueeze(2).to_broadcast([P, NT, 2, 64])).then_inc(copies, 1)
            pool.wait_ge(ready, 2)
            for g in range(2):
                pool.tensor_copy(ak4[:, :, g * P:(g + 1) * P].rearrange("p i (two f) -> p i two f", two=2),
                                 k.akv[:, :, g * 64:(g + 1) * 64].unsqueeze(2).to_broadcast([P, NT, 2, 64])).then_inc(copies, 1)

        @block.scalar
        def _(act):
            slow = dict(allow_slow_non_contiguous=True)
            act.dma_start(posi, k.positions_2[0].rearrange("(i p) -> p i", p=P), **slow).then_inc(vec_in, 16)
            act.dma_start(ikg[:, :], k.idx_k_norm_g_2[0].partition_broadcast(P)).then_inc(vec_in, 16)
            act.dma_start(qg, k.q_a_norm_g_2[0].rearrange("(k p) -> p k", p=P), **slow).then_inc(vec_in, 16)
            act.dma_start(kvg, k.kv_a_norm_g_2[0].rearrange("(k p) -> p k", p=P), **slow).then_inc(vec_in, 16)
            run_stores_range(nc, proj, act, "act", 0, 8)
            act.wait_ge(table, 1)
            nc.scalar.activation(k.sin[:, :, :], r, ACT.Sin).then_inc(rooted, 1)
            nc.scalar.activation(k.cos[:, :, :], ab, ACT.Sin).then_inc(rooted, 1)
            run_stores_range(nc, proj, act, "act", 8, len(jobs))
            act.wait_ge(table, 2)
            nc.scalar.activation(rt[:, :, :], ms[:, :, :], ACT.Sqrt).then_inc(rooted, 1)
            for i in range(NT):
                tok = slice(i * P, (i + 1) * P)
                act.wait_ge(turned, 4 * i + 1)
                nc.scalar.activation(k.aqT[:, :, tok], k.banks[:, 4 * (i % 2), :].rearrange("p (b t) -> p b t", t=P),
                                     ACT.Copy).then_inc(by_act, 1)
                act.wait_ge(turned, 4 * i + 3)
                bk = k.banks[:, 4 * (i % 2) + 2, :].rearrange("p (b t) -> p b t", t=P)
                nc.scalar.activation(k.akT[:, :, tok], bk[:, 0:2, :], ACT.Copy).then_inc(by_act, 1)
                for b in range(2):
                    nc.scalar.activation(k.cqT[:, b, tok], bk[:, 2 + b, :], ACT.Copy, scale=1.0).then_inc(by_act, 1)

        @block.tensor
        def _(pe):
            proj.pe_jobs(pe, 0, len(jobs))
            pe.wait_ge(proj.stored["act"], proj.count["act"])
            pe.wait_ge(proj.stored["dve"], proj.count["dve"])
            pe.wait_ge(ready, 4)
            pe.wait_ge(copies, 3)
            tr = lambda bank, slot, src, w=P: nc.tensor.transpose(k.banks[0:w, bank, slot * P:(slot + 1) * P], src, k.ident[:, :])
            for i in range(NT):
                base = 4 * (i % 2)
                if i >= 2:
                    pe.wait_ge(by_act, 4 * (i - 1))
                    pe.wait_ge(by_dve, 4 * (i - 1))
                for b in range(4):
                    ins = tr(base, b, aq[:, i, b * P:(b + 1) * P])
                ins.then_inc(turned, 1)
                for b in range(4):
                    ins = tr(base + 1, b, iq[:, i, b * P:(b + 1) * P])
                ins.then_inc(turned, 1)
                for b in range(2):
                    tr(base + 2, b, ak4[:, i, b * P:(b + 1) * P])
                for b in range(2):
                    ins = tr(base + 2, 2 + b, mix[:, i, c_cq + b * P:c_cq + (b + 1) * P])
                ins.then_inc(turned, 1)
                tr(base + 3, 0, ik2[:, i, :])
                tr(base + 3, 1, mix[:, i, c_ckv:c_ckv + P])
                ins = tr(base + 3, 2, mix[:, i, c_kr - 64:c_kr + 32], 96)
                ins.then_inc(turned, 1)

        @block.vector
        def _(dve):
            V = nc.vector
            run_stores_range(nc, proj, dve, "dve", 0, 8)
            dve.wait_ge(vec_in, 64)
            d.mark(V.tensor_copy(k.posq[:, :], posi))
            dve.wait_ge(d.sem, d.n)
            dve.wait_ge(pl.sem, 24)
            d.mark(V.tensor_tensor(angv, k.posq[:, :].unsqueeze(2).to_broadcast([P, NT, 24]),
                                   inv[:, :].unsqueeze(1).to_broadcast([P, NT, 24]), ALU.mult))
            dve.wait_ge(d.sem, d.n)
            d.mark(V.tensor_scalar(turns, angv, 1.0 / (2 * math.pi), None, ALU.mult))
            dve.wait_ge(d.sem, d.n)
            d.mark(V.tensor_scalar(turns, turns, MAGIC, None, ALU.add))
            dve.wait_ge(d.sem, d.n)
            d.mark(V.tensor_scalar(turns, turns, MAGIC, None, ALU.subtract))
            src = angv
            for c in (C1, C2, C3):
                dve.wait_ge(d.sem, d.n)
                d.mark(V.scalar_tensor_tensor(out=r, in0=turns, scalar=-c, in1=src, op0=ALU.mult, op1=ALU.add))
                src = r
            dve.wait_ge(d.sem, d.n)
            d.mark(V.tensor_scalar(r, r, 3.1415925, -3.1415925, ALU.min, ALU.max))
            dve.wait_ge(d.sem, d.n)
            d.mark(V.scalar_tensor_tensor(out=ab, in0=r, scalar=-1.0, in1=r, op0=ALU.mult, op1=ALU.min))
            dve.wait_ge(d.sem, d.n)
            V.tensor_scalar(ab, ab, math.pi / 2, None, ALU.add).then_inc(table, 1)
            run_stores_range(nc, proj, dve, "dve", 8, len(jobs))
            for e in ("act", "dve"):
                dve.wait_ge(proj.stored[e], proj.count[e])
            cols = [(c_ik, 64), (c_cq, 256), (c_ckv, P)]
            at = [0, 64, 320]
            for n, (c, w) in enumerate(cols):
                d.mark(V.tensor_tensor(sq[:, :, at[n]:at[n] + w], mix[:, :, c:c + w], mix[:, :, c:c + w], ALU.mult))
            dve.wait_ge(d.sem, d.n)
            for n, (c, w) in enumerate(cols):
                d.mark(V.tensor_reduce(ms[:, n, :], sq[:, :, at[n]:at[n] + w], AX.X, ALU.add))
            dve.wait_ge(d.sem, d.n)
            for n, (c, w) in enumerate(cols):
                ins = V.tensor_scalar(ms[:, n, :], ms[:, n, :], 1.0 / w, EPS, ALU.mult, ALU.add)
                d.mark(ins)
            dve.wait_ge(d.sem, d.n)
            V.memset(sm[:, 79:80], 0.0).then_inc(table, 1)
            dve.wait_ge(rooted, 3)
            d.mark(V.reciprocal(rs[:, :, :], rt[:, :, :]))
            dve.wait_ge(d.sem, d.n)
            for n, (c, w) in enumerate(cols):
                d.mark(V.tensor_tensor(mix[:, :, c:c + w], mix[:, :, c:c + w], rs[:, n, :].unsqueeze(2).to_broadcast([P, NT, w]),
                                       ALU.mult))
            dve.wait_ge(d.sem, d.n)
            d.mark(V.tensor_tensor(mix[:, :, 0:64], mix[:, :, 0:64], ikg[:, :].unsqueeze(1).to_broadcast([P, NT, 64]), ALU.mult))
            d.mark(V.tensor_scalar(k.iw[:, :, :], mix[:, :, c_iw:c_iw + 8], float(np.float32(8 ** -0.5)), None, ALU.mult))
            dve.wait_ge(d.sem, d.n)

            def rope(x, heads, half, f0):
                t = [t4[:, c, 0:NT * heads * half].rearrange("p (i h f) -> p i h f", i=NT, h=heads) for c in range(4)]
                tab = [a[:, :, f0:f0 + half].unsqueeze(2).to_broadcast([P, NT, heads, half]) for a in (k.cos, k.sin)]
                rope_dve(nc, dve, d, x[:, :, :, 0:half], x[:, :, :, half:2 * half], tab[0], tab[1], t)
                dve.wait_ge(d.sem, d.n)

            heads = lambda a, w: a.rearrange("p i (h f) -> p i h f", f=w)
            rope(heads(mix[:, :, 0:64], 64), 1, 8, 0)
            V.memset(sm[:, 79:80], 0.0).then_inc(ready, 1)
            dve.wait_ge(ready, 1)
            rope(heads(k.akv[:, :, 0:128], 64), 2, 8, 0)
            V.memset(sm[:, 79:80], 0.0).then_inc(ready, 1)
            rope(heads(mix[:, :, c_kr:c_kr + 32], 32), 1, 16, 8)
            rope(heads(iq[:, :, :], 64), 8, 8, 0)
            dve.wait_ge(ready, 2)
            V.memset(sm[:, 79:80], 0.0).then_inc(ready, 1)
            rope(heads(aq[:, :, :], 64), 8, 8, 0)
            dve.wait_ge(ready, 3)
            V.memset(sm[:, 79:80], 0.0).then_inc(ready, 1)
            for i in range(NT):
                tok = slice(i * P, (i + 1) * P)
                dve.wait_ge(turned, 4 * i + 2)
                V.tensor_copy(k.iqT[:, :, tok], k.banks[:, 4 * (i % 2) + 1, :].rearrange("p (b t) -> p b t", t=P)).then_inc(by_dve, 1)
                dve.wait_ge(turned, 4 * i + 4)
                bk = k.banks[:, 4 * (i % 2) + 3, :]
                V.tensor_copy(k.ikT[:, tok], bk[:, 0:P]).then_inc(by_dve, 1)
                V.tensor_scalar(k.ckvT[:, tok], bk[:, P:2 * P], kvg[:, 0:1], None, ALU.mult).then_inc(by_dve, 1)
                V.tensor_copy(k.krT[64:96, tok], bk[64:96, 2 * P:3 * P]).then_inc(by_dve, 1)
            dve.wait_ge(by_act, 4 * NT)
            for b in range(2):
                d.mark(V.tensor_scalar(k.cqT[:, b, :], k.cqT[:, b, :], qg[:, b:b + 1], None, ALU.mult))


def pad_keys(pool, out, keys, padded):
    for half in range(2):
        own, other = slice(64 * half, 64 * half + 64), slice(64 - 64 * half, 128 - 64 * half)
        pool.wait_ge(padded.sem, padded.mark(pool.memset(out[other, half, :], 0.0)))
        pool.wait_ge(padded.sem, padded.mark(pool.tensor_copy(out[own, half, :], keys(own))))


def stage_index_scores(nc, k):
    p = k.place
    k.isc = p("index_scores", [P, NT, T], 189)
    k.posrow = p("pos_row", [P, T], 125)
    R = p("index_relu", [P, 3, T], 96)
    posi = p("pos_row_int", [P, T], 108, I32)
    keys = p("index_keys_padded", [P, 2, T], 112)
    s = lambda n: k.sem("idx_" + n)
    padded = Steps(k, "idx_padded")
    pos_in, mm, relu, base, acc = s("pos_in"), s("product"), s("relu"), s("base"), s("sum")
    items = [(i, h) for i in range(NT) for h in range(8)]
    pair = lambda n: k.banks[:, 2 * (n % 4):2 * (n % 4) + 2, :].rearrange("p b c -> p (b c)")
    with nc.Block() as block:
        @block.gpsimd
        def _(pool):
            pad_keys(pool, keys, lambda rows: k.ikT[rows, :], padded)

        @block.scalar
        def _(act):
            act.dma_start(posi[:, :], k.positions_2[0].partition_broadcast(P)).then_inc(pos_in, 16)
            for n, (i, h) in enumerate(items):
                act.wait_ge(mm, n + 1)
                if n >= 3:
                    act.wait_ge(acc, n - 2)
                nc.scalar.activation(R[:, n % 3, :], pair(n), ACT.Relu).then_inc(relu, 1)

        @block.tensor
        def _(pe):
            pe.wait_ge(padded.sem, 4)
            for n, (i, h) in enumerate(items):
                if n >= 4:
                    pe.wait_ge(relu, n - 3)
                for c in range(2):
                    ins = nc.tensor.matmul(pair(n)[:, c * 512:(c + 1) * 512], k.iqT[:, h // 2, i * P:(i + 1) * P],
                                           keys[:, h % 2, c * 512:(c + 1) * 512], start=True, stop=True)
                ins.then_inc(mm, 1)

        @block.vector
        def _(dve):
            dve.wait_ge(pos_in, 16)
            nc.vector.tensor_copy(k.posrow[:, :], posi[:, :]).then_inc(base, 1)
            dve.wait_ge(base, 1)
            for i in range(NT):
                nc.vector.tensor_scalar(k.isc[:, i, :], k.posrow[:, :], k.posq[:, i:i + 1], MASKED, ALU.is_gt,
                                        ALU.mult).then_inc(base, 1)
            for n, (i, h) in enumerate(items):
                dve.wait_ge(relu, n + 1)
                if h == 0:
                    dve.wait_ge(base, i + 2)
                else:
                    dve.wait_ge(acc, n)
                nc.vector.scalar_tensor_tensor(out=k.isc[:, i, :], in0=R[:, n % 3, :], scalar=k.iw[:, i, h:h + 1],
                                               in1=k.isc[:, i, :], op0=ALU.mult, op1=ALU.add).then_inc(acc, 1)


def stage_select(nc, k):
    p = k.place
    V = nc.vector
    SPLIT = 4
    BIG = 3e38
    junk = p("count_scratch", [P, 2, T], 96)
    junk_act = p("sign_scratch", [P, T], 104)
    Q, RK, B = (p(n, [P, T], at) for n, at in (("equal", 108), ("rank", 112), ("below", 100)))
    G = p("excluded", [P, 2, T], 161)
    stage = p("gate_stage", [P, 4, 512], 116)
    ints = p("threshold_bits", [P, 4, NT], 6.25, I32)
    best, cand, took = (ints[:, c, :] for c in range(3))
    thr = best.bitcast(F32)
    cnt = k.small[:, 216:224]
    left = k.small[:, 224:232]
    least = k.small[:, 240:248]
    jobs = []
    for c in range(16):
        jobs += feature_jobs(k.c_gate[c // 4], (c % 4) * P, None, "sigmoid", "act")
    proj = Projection(nc, k, "gates", jobs)
    d = Steps(k, "select_dve")
    cs = Steps(k, "select_count")
    tried, signs = k.sem("candidate"), k.sem("signs_summed")
    padded = Steps(k, "sparse_keys_padded")
    k.ak_pad = p("sparse_keys_padded", [P, 4, T], 145)
    selq, below = k.sem("excluded_equal"), k.sem("below_threshold")
    cut, biased = k.sem("threshold_done"), k.sem("bias_done")
    gate_out = [k.sem(f"gate_out_{i}") for i in range(4)]
    with nc.Block() as block:
        @block.sync
        def _(sp):
            for j, job in enumerate(jobs):
                if j % 8 == 0:
                    k.w.load_up_to(sp, k.c_gate[0] + j // 8 + 1)
                sp.wait_ge(proj.stored["act"], j + 1)
                sp.dma_start(k.gate_dram[j // 2, :, (j % 2) * 512:(j % 2 + 1) * 512], stage[:, j % 4, :]).then_inc(gate_out[j % 4], 16)
            k.w.load_up_to(sp, k.c_bb)
            for g in gate_out:
                sp.wait_ge(g, 16 * len(jobs) // 4)

        @block.gpsimd
        def _(pool):
            for g in range(2):
                pad_keys(pool, k.ak_pad[:, 2 * g:2 * g + 2, :], lambda rows: k.akT[rows, g, :], padded)
            pool.wait_ge(cut, 1)
            for i in range(NT):
                if i:
                    pool.wait_ge(biased, i)
                pool.tensor_scalar(B[:, :], k.isc[:, i, :], thr[:, i:i + 1], MASKED, ALU.is_lt, ALU.mult).then_inc(below, 1)
                pool.wait_ge(selq, i + 1)
                pool.wait_ge(below, i + 1)
                pool.tensor_tensor(k.isc[:, i, :], B[:, :], G[:, i % 2, :], ALU.add).then_inc(biased, 1)

        @block.scalar
        def _(act):
            def gate(j):
                act.wait_ge(proj.done, j + 1)
                if j >= 4:
                    act.wait_ge(gate_out[j % 4], 16 * (j // 4))
                nc.scalar.activation(stage[:, j % 4, :], proj.bank(j), ACT.Sigmoid).then_inc(proj.stored["act"], 1)

            for bit in range(32):
                act.wait_ge(tried, bit + 1)
                for i in range(SPLIT, NT):
                    if bit or i > SPLIT:
                        act.wait_ge(signs, (NT - SPLIT) * bit + i - SPLIT)
                    nc.scalar.activation(junk_act[:, :], k.isc[:, i, :], ACT.Sign, scale=-1.0, bias=cand.bitcast(F32)[:, i:i + 1],
                                         accum_out=cnt[:, i:i + 1]).then_inc(signs, 1)
                for j in range(4 * bit // 5, 4 * (bit + 1) // 5):
                    gate(j)
            for j in range(4 * 32 // 5, len(jobs)):
                gate(j)

        @block.tensor
        def _(pe):
            proj.pe_jobs(pe, 0, len(jobs))

        @block.vector
        def _(dve):
            def step(ins):
                d.mark(ins)
                dve.wait_ge(d.sem, d.n)

            top = -2 ** 31
            for n, bit in enumerate(range(31, -1, -1)):
                if n == 0:
                    V.memset(cand, 0).then_inc(tried, 1)
                else:
                    V.tensor_scalar(cand, best, 1 << bit, None, ALU.bitwise_xor).then_inc(tried, 1)
                dve.wait_ge(tried, n + 1)
                for i in range(SPLIT):
                    if cs.n >= 2:
                        dve.wait_ge(cs.sem, cs.n - 1)
                    cs.mark(V.tensor_scalar(junk[:, i % 2, :], k.isc[:, i, :], cand.bitcast(F32)[:, i:i + 1], 0.0, ALU.is_ge, ALU.add,
                                            accum_out=cnt[:, i:i + 1]))
                dve.wait_ge(cs.sem, cs.n)
                dve.wait_ge(signs, (NT - SPLIT) * (n + 1))
                d.mark(V.tensor_scalar(took[:, 0:SPLIT], cnt[:, 0:SPLIT], float(TOPK), None, ALU.is_ge))
                step(V.tensor_scalar(took[:, SPLIT:NT], cnt[:, SPLIT:NT], float(T - 2 * TOPK), None, ALU.is_le))
                if n == 0:
                    step(V.tensor_scalar(best, took, 1.0, None, ALU.subtract))
                else:
                    step(V.copy_predicated(best, took.bitcast(U32), cand))
            for i in range(SPLIT, NT):
                x, t = k.isc[:, i, :], thr[:, i:i + 1]
                step(V.tensor_scalar(junk[:, 0, :], x, t, 0.0, ALU.is_gt, ALU.add, accum_out=cnt[:, i:i + 1]))
                step(V.tensor_scalar(junk[:, 0, :], x, t, BIG, ALU.is_le, ALU.mult))
                step(V.tensor_tensor_reduce(junk[:, 1, :], junk[:, 0, :], x, 1.0, BIG, ALU.add, ALU.min, least[:, i:i + 1]))
            step(V.tensor_scalar(took[:, SPLIT:NT], cnt[:, SPLIT:NT], float(TOPK), None, ALU.is_ge))
            step(V.copy_predicated(best[:, SPLIT:NT], took[:, SPLIT:NT].bitcast(U32), least[:, SPLIT:NT].bitcast(I32)))
            step(V.tensor_scalar(thr, thr, MASKED / 2, None, ALU.max))
            V.memset(k.small[:, 79:80], 0.0).then_inc(cut, 1)
            dve.wait_ge(padded.sem, 8)
            for i in range(NT):
                x, t, c = k.isc[:, i, :], thr[:, i:i + 1], i % 2
                d.mark(V.tensor_scalar(junk[:, 0, :], x, t, 0.0, ALU.is_gt, ALU.add, accum_out=cnt[:, i:i + 1]))
                if i:
                    dve.wait_ge(selq, i)
                step(V.tensor_scalar(Q[:, :], x, t, None, ALU.is_equal))
                d.mark(V.tensor_scalar(left[:, i:i + 1], cnt[:, i:i + 1], -1.0, float(TOPK), ALU.mult, ALU.add))
                step(V.tensor_tensor_scan(RK[:, :], Q[:, :], Q[:, :], 0.0, ALU.add, ALU.max))
                step(V.tensor_scalar(RK[:, :], RK[:, :], left[:, i:i + 1], MASKED, ALU.is_gt, ALU.mult))
                if i >= 2:
                    dve.wait_ge(biased, i - 1)
                V.tensor_tensor(G[:, c, :], RK[:, :], Q[:, :], ALU.mult).then_inc(selq, 1)
            dve.wait_ge(biased, NT)


def attention(nc, k, name, q, kk, v, bias, scale, oT, at, at_turned):
    p = k.place
    L = p(f"{name}_logits", [P, 2, T], at)
    E = p(f"{name}_probs", [P, 2, T], at + 8)
    ET = [p(f"{name}_probsT_{c}", [P, 2, NT, P], at_turned[c]) for c in range(2)]
    wide = p(f"{name}_inverse_wide", [P, 2, 512], at + 16)
    spread = p(f"{name}_inverse_spread", [P, 2, 512], at + 20)
    low = p(f"{name}_minus_max", [P, NT * 8], at + 28)
    tot = p(f"{name}_total", [P, NT * 8], at + 28.25)
    inv = p(f"{name}_inverse", [P, NT * 8], at + 28.5)
    items = [(i, h) for i in range(NT) for h in range(8)]
    N = len(items)
    s = lambda n: k.sem(f"{name}_{n}")
    mm, logit, prob, turned = s("scores"), s("logits"), s("probs"), s("probs_turned")
    t_act, t_dve, pv, invd, wided = s("pT_act"), s("pT_dve"), s("out"), s("inverse"), s("inverse_wide")
    sp_mm, sp_st, o_done = s("inverse_product"), s("inverse_spread"), s("oT_stored")
    pair = lambda n: k.banks[:, 2 * (n % 2):2 * (n % 2) + 2, :].rearrange("p b c -> p (b c)")
    turned_at = lambda n: ET[(n // 2) % 2][:, n % 2, :, :]

    def act_program(act):
        def softmax(n):
            act.wait_ge(logit, n + 1)
            if n >= 2:
                act.wait_ge(turned, 2 * (n - 1))
            nc.scalar.activation(E[:, n % 2, :], L[:, n % 2, :], ACT.Exp, scale=-1.0, bias=low[:, n:n + 1],
                                 accum_out=tot[:, n:n + 1]).then_inc(prob, 1)

        def store_spread(i):
            act.wait_ge(sp_mm, i + 1)
            if i >= 2:
                act.wait_ge(o_done, i - 1)
            nc.scalar.activation(spread[:, i % 2, :], k.banks[:, 7, :], ACT.Copy).then_inc(sp_st, 1)

        softmax(0)
        for n, (i, h) in enumerate(items):
            if n + 1 < N:
                softmax(n + 1)
            act.wait_ge(turned, 2 * n + 1)
            if n >= 4:
                act.wait_ge(pv, n // 2 - 1)
            nc.scalar.activation(turned_at(n)[:, 0:4, :], k.banks[:, 4, :].rearrange("p (j t) -> p j t", t=P),
                                 ACT.Copy).then_inc(t_act, 1)
            if h == 1 and i:
                store_spread(i - 1)
        store_spread(NT - 1)

    def pe_program(pe):
        def scores(n):
            i, h = items[n]
            if n >= 2:
                pe.wait_ge(logit, n - 1)
            for c in range(2):
                ins = nc.tensor.matmul(pair(n)[:, c * 512:(c + 1) * 512], q(h, i), kk(h, c), start=True, stop=True)
            ins.then_inc(mm, 1)

        def spread_inverse(i):
            pe.wait_ge(wided, i + 1)
            if i:
                pe.wait_ge(sp_st, i)
            for b in range(4):
                ins = nc.tensor.matmul(k.banks[:, 7, b * P:(b + 1) * P], wide[:, i % 2, b * P:(b + 1) * P], k.ident[:, :],
                                       start=True, stop=True)
            ins.then_inc(sp_mm, 1)

        def values(m, second):
            i, b = m // 4, m % 4
            if b == 0 and not second and i:
                pe.wait_ge(o_done, i)
            if not second:
                pe.wait_ge(t_act, 2 * m + 2)
                pe.wait_ge(t_dve, 2 * m + 2)
            for j in range(4 * second, 4 * second + 4):
                for c in range(2):
                    ins = nc.tensor.matmul(k.banks[64 * c:64 * c + 64, 6, b * P:(b + 1) * P], v(2 * b + c, j),
                                           ET[m % 2][:, c, j, :], start=(j == 0), stop=(j == NT - 1))
            if second:
                ins.then_inc(pv, 1)

        scores(0)
        scores(1)
        for n, (i, h) in enumerate(items):
            pe.wait_ge(prob, n + 1)
            for j in range(NT):
                if n and j % 4 == 0:
                    pe.wait_ge(t_dve if j else t_act, n)
                ins = nc.tensor.transpose(k.banks[:, 4 + j // 4, (j % 4) * P:(j % 4 + 1) * P],
                                          E[:, n % 2, j * P:(j + 1) * P], k.ident[:, :])
                if j % 4 == 3:
                    ins.then_inc(turned, 1)
            if n >= 2:
                values(n // 2 - 1, n % 2)
            if n + 2 < N:
                scores(n + 2)
            if h == 0 and i:
                spread_inverse(i - 1)
        values(N // 2 - 1, 0)
        values(N // 2 - 1, 1)
        spread_inverse(NT - 1)

    def dve_program(dve):
        def logits(n):
            i, h = items[n]
            dve.wait_ge(mm, n + 1)
            if n >= 2:
                dve.wait_ge(prob, n - 1)
            nc.vector.tensor_tensor_reduce(L[:, n % 2, :], pair(n), bias(dve, i), -scale, -MASKED, ALU.add, ALU.min,
                                           low[:, n:n + 1]).then_inc(logit, 1)

        def invert(i):
            dve.wait_ge(prob, 8 * i + 8)
            nc.vector.reciprocal(inv[:, 8 * i:8 * i + 8], tot[:, 8 * i:8 * i + 8]).then_inc(invd, 1)
            dve.wait_ge(invd, i + 1)
            if i >= 2:
                dve.wait_ge(sp_mm, i - 1)
            nc.vector.tensor_copy(wide[:, i % 2, :].rearrange("p (h f) -> p h f", f=64),
                                  inv[:, 8 * i:8 * i + 8].unsqueeze(2).to_broadcast([P, 8, 64])).then_inc(wided, 1)

        def store_out(i):
            dve.wait_ge(sp_st, i + 1)
            dve.wait_ge(pv, 4 * i + 4)
            nc.vector.tensor_tensor(oT[:, :, i * P:(i + 1) * P], k.banks[:, 6, :].rearrange("p (b t) -> p b t", t=P),
                                    spread[:, i % 2, :].rearrange("p (b t) -> p b t", t=P), ALU.mult).then_inc(o_done, 1)

        logits(0)
        for n, (i, h) in enumerate(items):
            if n + 1 < N:
                logits(n + 1)
            dve.wait_ge(turned, 2 * n + 2)
            if n >= 4:
                dve.wait_ge(pv, n // 2 - 1)
            nc.vector.tensor_copy(turned_at(n)[:, 4:8, :], k.banks[:, 5, :].rearrange("p (j t) -> p j t", t=P)).then_inc(t_dve, 1)
            if h == 7:
                invert(i)
            if h == 1 and i:
                store_out(i - 1)
        store_out(NT - 1)

    return act_program, pe_program, dve_program, logit


def stage_sparse_attention(nc, k):
    k.oaT = k.place("sparse_oT", [P, 4, T], 72)
    act_p, pe_p, dve_p, _ = attention(
        nc, k, "sparse",
        lambda h, i: k.aqT[:, h // 2, i * P:(i + 1) * P],
        lambda h, c: k.ak_pad[:, 2 * (h // 4) + h % 2, c * 512:(c + 1) * 512],
        lambda h, j: k.akv[:, j, 128 + (h // 4) * 64:128 + (h // 4) * 64 + 64],
        lambda dve, i: k.isc[:, i, :], 1.0, k.oaT, 96, (40, 48))
    with nc.Block() as block:
        block.scalar(act_p)
        block.tensor(pe_p)
        block.vector(dve_p)


def stage_latent_projection(nc, k):
    p = k.place
    wuq, wuk, wuv = p("w_uq", [P, 2, 768], 209), p("w_uk", [P, 512], 215), p("w_uv", [P, 512], 217)
    k.qf = p("latent_qT", [P, 8, T], 129)
    k.kf = p("latent_kT", [P, 8, T], 40)
    k.vb = p("latent_v", [P, NT, 512], 161)
    qb = p("latent_q_tok", [P, NT, 768], 92)
    t4 = p("latent_rope", [P, 4, 512], 116)
    s = lambda n: k.sem("lat_" + n)
    w_in, mm, st_a, st_d, kr, ready, turned, q_a, q_d = (s(n) for n in ("w_in", "product", "act", "dve", "rope_keys", "ready", "turned", "q_act", "q_dve"))
    d = Steps(k, "lat_rotate")
    jobs = [("q", i, c) for i in range(NT) for c in range(2)] + [("v", i, 0) for i in range(NT)] + \
           [("k", h, c) for h in range(8) for c in range(2)]
    by = ["act" if n % 2 == 0 else "dve" for n in range(len(jobs))]
    with nc.Block() as block:
        @block.sync
        def _(sp):
            sp.dma_start(wuq[:, :, :], k.w_uq_2[0].rearrange("(k p) h f -> p k (h f)", p=P)).then_inc(w_in, 16)
            sp.dma_start(wuk[:, :], k.w_uk_2[0].rearrange("r h f -> r (h f)")).then_inc(w_in, 16)
            sp.dma_start(wuv[:, :], k.w_uv_2[0].rearrange("r h f -> r (h f)")).then_inc(w_in, 16)

        def dest(n):
            kind, a, c = jobs[n]
            if kind == "q":
                return qb[:, a, c * 384:(c + 1) * 384], k.banks[:, n % 8, 0:384]
            if kind == "v":
                return k.vb[:, a, :], k.banks[:, n % 8, :]
            return k.kf[0:64, a, c * 512:(c + 1) * 512], k.banks[0:64, n % 8, :]

        @block.gpsimd
        def _(pool):
            for h in range(8):
                pool.tensor_copy(k.kf[64:96, h, :], k.krT[64:96, :]).then_inc(kr, 1)

        @block.scalar
        def _(act):
            for n in range(0, len(jobs), 2):
                out, src = dest(n)
                act.wait_ge(mm, n + 1)
                nc.scalar.activation(out, src, ACT.Copy).then_inc(st_a, 1)
            for i in range(NT):
                for b in range(0, 2):
                    if b == 0:
                        act.wait_ge(turned, 2 * i + 1)
                        nc.scalar.activation(k.qf[0:96, 0:4, i * P:(i + 1) * P],
                                             k.banks[0:96, 2 * (i % 2), :].rearrange("p (h t) -> p h t", t=P), ACT.Copy).then_inc(q_a, 1)

        @block.tensor
        def _(pe):
            pe.wait_ge(w_in, 48)
            for n, (kind, a, c) in enumerate(jobs):
                out = dest(n)[1]
                if n >= 8:
                    pe.wait_ge(st_a if n % 2 == 0 else st_d, (n - 8) // 2 + 1)
                if kind == "q":
                    for b in range(2):
                        ins = nc.tensor.matmul(out, k.cqT[:, b, a * P:(a + 1) * P], wuq[:, b, c * 384:(c + 1) * 384],
                                               start=(b == 0), stop=(b == 1))
                elif kind == "v":
                    ins = nc.tensor.matmul(out, k.ckvT[:, a * P:(a + 1) * P], wuv[:, :], start=True, stop=True)
                else:
                    ins = nc.tensor.matmul(out, wuk[:, a * 64:(a + 1) * 64], k.ckvT[:, c * 512:(c + 1) * 512], start=True, stop=True)
                ins.then_inc(mm, 1)
            pe.wait_ge(st_a, len(jobs) // 2)
            pe.wait_ge(st_d, len(jobs) // 2)
            pe.wait_ge(ready, 1)
            for i in range(NT):
                if i >= 2:
                    pe.wait_ge(q_a, i - 1)
                    pe.wait_ge(q_d, i - 1)
                for h in range(8):
                    ins = nc.tensor.transpose(k.banks[0:96, 2 * (i % 2) + h // 4, (h % 4) * P:(h % 4 + 1) * P],
                                              qb[:, i, h * 96:(h + 1) * 96], k.ident[:, :])
                    if h % 4 == 3:
                        ins.then_inc(turned, 1)

        @block.vector
        def _(dve):
            for n in range(1, len(jobs), 2):
                out, src = dest(n)
                dve.wait_ge(mm, n + 1)
                nc.vector.tensor_copy(out, src).then_inc(st_d, 1)
                if n == 15:
                    dve.wait_ge(st_a, 8)
                    dve.wait_ge(st_d, 8)
                    for i0 in range(0, NT, 4):
                        x = qb[:, i0:i0 + 4, :].rearrange("p i (h f) -> p i h f", f=96)
                        t = [t4[:, c, :].rearrange("p (i h f) -> p i h f", i=4, h=8) for c in range(4)]
                        tab = [a[:, i0:i0 + 4, 8:24].unsqueeze(2).to_broadcast([P, 4, 8, 16]) for a in (k.cos, k.sin)]
                        rope_dve(nc, dve, d, x[:, :, :, 64:80], x[:, :, :, 80:96], tab[0], tab[1], t)
                        dve.wait_ge(d.sem, d.n)
                    nc.vector.memset(k.small[:, 79:80], 0.0).then_inc(ready, 1)
            for i in range(NT):
                dve.wait_ge(turned, 2 * i + 2)
                nc.vector.tensor_copy(k.qf[0:96, 4:8, i * P:(i + 1) * P],
                                      k.banks[0:96, 2 * (i % 2) + 1, :].rearrange("p (h t) -> p h t", t=P)).then_inc(q_d, 1)


def stage_latent_attention(nc, k):
    p = k.place
    k.obT = p("latent_oT", [P, 4, T], 193)
    pen = p("causal_bias", [P, 2, T], 177)
    made = k.sem("lat_bias")
    state = {"made": -1}
    hold = {}

    def bias(dve, i):
        if state["made"] < i:
            state["made"] = i
            dve.wait_ge(made, i + 1)
        return pen[:, i % 2, :]

    act_p, pe_p, dve_p, logit = attention(
        nc, k, "latent",
        lambda h, i: k.qf[0:96, h, i * P:(i + 1) * P],
        lambda h, c: k.kf[0:96, h, c * 512:(c + 1) * 512],
        lambda h, j: k.vb[:, j, h * 64:(h + 1) * 64],
        bias, float(np.float32(96 ** -0.5)), k.obT, 92, (185, 209))
    with nc.Block() as block:
        @block.gpsimd
        def _(pool):
            for i in range(NT):
                if i >= 2:
                    pool.wait_ge(logit, 8 * (i - 1))
                pool.tensor_scalar(pen[:, i % 2, :], k.posrow[:, :], k.posq[:, i:i + 1], MASKED, ALU.is_gt,
                                   ALU.mult).then_inc(made, 1)
        block.scalar(act_p)
        block.tensor(pe_p)
        block.vector(dve_p)


def stage_merge(nc, k):
    p = k.place
    mT = p("merged_T", [P, KB, T], 100)
    gates = p("gates_in", [P, 4, T], 132)
    pa, pb = p("part_a", [P, 2, 512], 148), p("part_b", [P, 2, 512], 152)
    k.h2 = p("h2", [P, NT, D], 160)
    ffng = k.small[:, 232:240]
    s = lambda n: k.sem("mrg_" + n)
    g_in = [s(f"gate_in_{c}") for c in range(2)]
    x1_in, vec_in, mm_a, mm_b, st_a, st_b, merged, gained, res = (s(n) for n in ("x1_in", "vec_in", "a", "b", "a_st", "b_st", "sum", "gained", "residual"))
    k.w.freed[k.c_ba] = (mm_a, 16)
    k.w.freed[k.c_bb] = (mm_b, 16)
    jobs = [dict(chunk=k.c_out2[h], kind="tokens", tile=i, col=0, width=512, by="dve", dest=h, how="add")
            for i in range(NT) for h in range(2)]
    proj = Projection(nc, k, "second_out", jobs, banks=8, src=mT)
    norm = NormTranspose(nc, k, "norm3", k.h2, k.hT, p("h2_normed", [P, NT, D], 100))
    ga = lambda n: k.gate_dram[n]
    with nc.Block() as block:
        @block.sync
        def _(sp):
            for n in range(KB):
                if n >= 2:
                    sp.wait_ge(st_a, 2 * (n - 1))
                    sp.wait_ge(st_b, 2 * (n - 1))
                for br in range(2):
                    sp.dma_start(gates[:, 2 * (n % 2) + br, :], ga(8 * br + n)).then_inc(g_in[n % 2], 16)
                if n == 0:
                    sp.dma_start(k.h2[:, :, :], k.x1_dram.rearrange("(i p) d -> p i d", p=P)).then_inc(x1_in, 16)
            k.w.load_up_to(sp, k.c_up[1])

        @block.gpsimd
        def _(pool):
            for n in range(16):
                pool.wait_ge(st_a, n + 1)
                pool.wait_ge(st_b, n + 1)
                pool.tensor_tensor(mT[:, n // 2, (n % 2) * 512:(n % 2 + 1) * 512], pa[:, n % 2, :], pb[:, n % 2, :],
                                   ALU.add).then_inc(merged, 1)

        @block.scalar
        def _(act):
            act.dma_start(ffng, k.norm_ffn_g_2[0].rearrange("(k p) -> p k", p=P), allow_slow_non_contiguous=True).then_inc(vec_in, 16)
            norm.act_stats(act, lambda e, i: e.wait_ge(proj.stored["dve"], 2 * i + 2))
            norm.store(act, 0)

        @block.tensor
        def _(pe):
            for n in range(16):
                f, c = n // 2, n % 2
                for br, (chunk, src, mm, st) in enumerate(((k.c_ba, k.oaT, mm_a, st_a), (k.c_bb, k.obT, mm_b, st_b))):
                    if n == 0:
                        k.w.wait(pe, chunk)
                    if n >= 4:
                        pe.wait_ge(st, n - 3)
                    wv = k.w.view(chunk)
                    for b in range(4):
                        ins = nc.tensor.matmul(k.banks[:, 2 * (n % 4) + br, :], wv[:, b, f * P:(f + 1) * P],
                                               src[:, b, c * 512:(c + 1) * 512], start=(b == 0), stop=(b == 3))
                    ins.then_inc(mm, 1)
            pe.wait_ge(merged, 16)
            proj.pe_jobs(pe, 0, len(jobs))
            pe.wait_ge(proj.stored["dve"], len(jobs))
            norm.pe_transpose(pe)

        @block.vector
        def _(dve):
            for n in range(16):
                f, c = n // 2, n % 2
                if c == 0:
                    dve.wait_ge(g_in[f % 2], 32 * (f // 2 + 1))
                for br, (buf, mm, st) in enumerate(((pa, mm_a, st_a), (pb, mm_b, st_b))):
                    dve.wait_ge(mm, n + 1)
                    if n >= 2:
                        dve.wait_ge(merged, n - 1)
                    nc.vector.tensor_tensor(buf[:, n % 2, :], k.banks[:, 2 * (n % 4) + br, :],
                                            gates[:, 2 * (f % 2) + br, c * 512:(c + 1) * 512], ALU.mult).then_inc(st, 1)
            dve.wait_ge(x1_in, 16)
            for j, job in enumerate(jobs):
                i, h = job["tile"], job["dest"]
                dve.wait_ge(proj.done, j + 1)
                xs = k.h2[:, i, h * 512:(h + 1) * 512]
                nc.vector.tensor_tensor(xs, proj.bank(j), xs, ALU.add).then_inc(proj.stored["dve"], 1)
            norm.dve_stats(dve)
            norm.dve_divide(dve)
            norm.store(dve, 1)
            dve.wait_ge(norm.by_act, NT)
            dve.wait_ge(norm.by_dve, NT)
            dve.wait_ge(vec_in, 16)
            for b in range(KB):
                nc.vector.tensor_scalar(k.hT[:, b, :], k.hT[:, b, :], ffng[:, b:b + 1], None, ALU.mult).then_inc(gained, 1)


def stage_ffn_up(nc, k):
    p = k.place
    k.act = p("ffn_act", [P, FBLK, T], 72)
    Y = p("ffn_conv", [P, 4, T], 192)
    cw = p("conv_taps", [P, 3, 2 * FBLK], 208)
    cb = p("conv_bias", [P, 2 * FBLK], 209)
    vec_in = k.sem("conv_in")
    s = lambda n: k.sem("ffn_" + n)
    mm, y0, y1, y2, gate, out = (s(n) for n in ("u", "tap2", "tap1", "tap0", "silu", "act"))
    for n, c in enumerate(k.c_up):
        k.w.freed[c] = (mm, 4 * n + 4)
    pair = lambda n: k.banks[:, 2 * (n % 4):2 * (n % 4) + 2, :].rearrange("p b c -> p (b c)")
    with nc.Block() as block:
        @block.sync
        def _(sp):
            k.w.load_up_to(sp, k.c_down[0][1])

        @block.gpsimd
        def _(pool):
            for f in range(FBLK):
                pool.wait_ge(gate, f + 1)
                pool.wait_ge(y2, 2 * f + 2)
                b = 2 * (f % 2)
                pool.tensor_tensor(k.act[:, f, :], Y[:, b, :], Y[:, b + 1, :], ALU.mult).then_inc(out, 1)

        @block.scalar
        def _(act):
            slow = dict(allow_slow_non_contiguous=True)
            for j in range(3):
                act.dma_start(cw[:, j, :], k.conv_w_2[0, j].rearrange("(f p) -> p f", p=P), **slow).then_inc(vec_in, 16)
            act.dma_start(cb[:, :], k.conv_b_2[0].rearrange("(f p) -> p f", p=P), **slow).then_inc(vec_in, 16)
            act.wait_ge(vec_in, 64)
            for n in range(2 * FBLK + 2):
                if n < 2 * FBLK:
                    f, v = n // 2, n % 2
                    c = f + v * FBLK
                    act.wait_ge(mm, n + 1)
                    if f >= 2:
                        act.wait_ge(out, f - 1)
                    nc.scalar.activation(Y[:, 2 * (f % 2) + v, :], pair(n), ACT.Identity, bias=cb[:, c:c + 1],
                                         scale=cw[:, 2, c:c + 1]).then_inc(y0, 1)
                if n >= 2 and n % 2 == 0:
                    f = n // 2 - 1
                    act.wait_ge(y2, 2 * f + 1)
                    nc.scalar.activation(Y[:, 2 * (f % 2), :], Y[:, 2 * (f % 2), :], ACT.Silu).then_inc(gate, 1)

        @block.tensor
        def _(pe):
            for n in range(2 * FBLK):
                f, v = n // 2, n % 2
                chunk = k.c_up[f // 2]
                if f % 2 == 0 and v == 0:
                    k.w.wait(pe, chunk)
                if n >= 4:
                    pe.wait_ge(y2, n - 3)
                wv = k.w.view(chunk)
                c0 = v * 256 + (f % 2) * P
                for h in range(2):
                    for b in range(KB):
                        ins = nc.tensor.matmul(pair(n)[:, h * 512:(h + 1) * 512], wv[:, b, c0:c0 + P],
                                               k.hT[:, b, h * 512:(h + 1) * 512], start=(b == 0), stop=(b == KB - 1))
                ins.then_inc(mm, 1)

        @block.vector
        def _(dve):
            dve.wait_ge(vec_in, 64)
            for n in range(2 * FBLK):
                f, v = n // 2, n % 2
                c, y = f + v * FBLK, Y[:, 2 * (f % 2) + v, :]
                dve.wait_ge(y0, n + 1)
                nc.vector.scalar_tensor_tensor(out=y[:, 1:T], in0=pair(n)[:, 0:T - 1], scalar=cw[:, 1, c:c + 1],
                                               in1=y[:, 1:T], op0=ALU.mult, op1=ALU.add).then_inc(y1, 1)
                dve.wait_ge(y1, n + 1)
                nc.vector.scalar_tensor_tensor(out=y[:, 2:T], in0=pair(n)[:, 0:T - 2], scalar=cw[:, 0, c:c + 1],
                                               in1=y[:, 2:T], op0=ALU.mult, op1=ALU.add).then_inc(y2, 1)


def stage_ffn_down(nc, k):
    p = k.place
    x = k.h2
    row = p("last_gain", [P, D], 192)
    s = lambda n: k.sem("down_" + n)
    vec_in, part, done, added, summed = (s(n) for n in ("vec_in", "part", "product", "added", "summed"))
    out = k.output_stored
    rstd_s, root_s, mean_s, fin = s("rstd"), s("root"), s("mean"), s("normed")
    sq, ms, rt, rs = (k.small[:, c:c + 8] for c in (168, 176, 184, 192))
    n = 0
    for h in range(2):
        for g in range(3):
            n += 1
            k.w.freed[k.c_down[h][g]] = (part, n)
    with nc.Block() as block:
        @block.sync
        def _(sp):
            k.w.load_up_to(sp, k.c_down[1][2])
            for i in range(NT):
                sp.wait_ge(fin, i + 1)
                sp.dma_start(k.out[0, i * P:(i + 1) * P, :], x[:, i, :]).then_inc(out, 16)
            sp.wait_ge(out, 16 * NT)

        @block.scalar
        def _(act):
            act.dma_start(row[:, :], k.norm_final_g_2.partition_broadcast(P)).then_inc(vec_in, 16)
            for i in range(NT):
                act.wait_ge(added, NT + i + 1)
                nc.scalar.activation(k.hT[:, i, :], x[:, i, :], ACT.Square, accum_out=sq[:, i:i + 1]).then_inc(summed, 1)
                act.wait_ge(mean_s, i + 1)
                nc.scalar.activation(rt[:, i:i + 1], ms[:, i:i + 1], ACT.Sqrt).then_inc(root_s, 1)

        @block.tensor
        def _(pe):
            for h in range(2):
                for g in range(3):
                    chunk = k.c_down[h][g]
                    k.w.wait(pe, chunk)
                    wv, blocks = k.w.view(chunk), k.w.chunks[chunk][1]
                    last = g == 2
                    for i in range(NT):
                        if h and g == 0:
                            pe.wait_ge(added, i + 1)
                        for b in range(blocks):
                            f = 8 * g + b
                            ins = nc.tensor.matmul(k.banks[:, i, :], k.act[:, f, i * P:(i + 1) * P], wv[:, b, :],
                                                   start=(f == 0), stop=(f == FBLK - 1))
                        if last:
                            ins.then_inc(done if i < NT - 1 else part, 1)
                    if not last:
                        ins.then_inc(part, 1)

        @block.vector
        def _(dve):
            def finish(i):
                dve.wait_ge(summed, i + 1)
                nc.vector.tensor_scalar(ms[:, i:i + 1], sq[:, i:i + 1], 1.0 / D, EPS, ALU.mult, ALU.add).then_inc(mean_s, 1)
                dve.wait_ge(root_s, i + 1)
                nc.vector.reciprocal(rs[:, i:i + 1], rt[:, i:i + 1]).then_inc(rstd_s, 1)
                dve.wait_ge(rstd_s, i + 1)
                nc.vector.scalar_tensor_tensor(out=x[:, i, :], in0=x[:, i, :], scalar=rs[:, i:i + 1], in1=row[:, :],
                                               op0=ALU.mult, op1=ALU.mult).then_inc(fin, 1)

            dve.wait_ge(vec_in, 16)
            for h in range(2):
                for i in range(NT):
                    if i < NT - 1:
                        dve.wait_ge(done, 7 * h + i + 1)
                    else:
                        dve.wait_ge(part, 3 * h + 3)
                    xs = x[:, i, h * 512:(h + 1) * 512]
                    nc.vector.tensor_tensor(xs, k.banks[:, i, :], xs, ALU.add).then_inc(added, 1)
                    if h and i:
                        finish(i - 1)
            finish(NT - 1)


def build(nc, views):
    k = Kernel(nc)
    k.x = views["x"]
    k.c = views["c"]
    k.w_ada = views["w_ada"]
    k.b_ada = views["b_ada"]
    k.w_in = views["w_in"]
    k.w_gla_gate2 = views["w_gla_gate2"]
    k.b_gla_gate = views["b_gla_gate"]
    k.gla_norm_w = views["gla_norm_w"]
    k.hgrn_lb_logits = views["hgrn_lb_logits"]
    k.hgrn_norm_w = views["hgrn_norm_w"]
    k.w_out = views["w_out"]
    k.final_norm_w = views["final_norm_w"]
    k.positions_2 = views["positions_2"]
    k.norm_mix_g_2 = views["norm_mix_g_2"]
    k.w_in_2 = views["w_in_2"]
    k.idx_k_norm_g_2 = views["idx_k_norm_g_2"]
    k.q_a_norm_g_2 = views["q_a_norm_g_2"]
    k.kv_a_norm_g_2 = views["kv_a_norm_g_2"]
    k.w_uq_2 = views["w_uq_2"]
    k.w_uk_2 = views["w_uk_2"]
    k.w_uv_2 = views["w_uv_2"]
    k.w_branch_a_2 = views["w_branch_a_2"]
    k.w_branch_b_2 = views["w_branch_b_2"]
    k.w_out_2 = views["w_out_2"]
    k.norm_ffn_g_2 = views["norm_ffn_g_2"]
    k.w_up_2 = views["w_up_2"]
    k.conv_w_2 = views["conv_w_2"]
    k.conv_b_2 = views["conv_b_2"]
    k.w_down_2 = views["w_down_2"]
    k.norm_final_g_2 = views["norm_final_g_2"]
    k.out = views["out"]
    k.x1_dram = nc.dram_tensor("x1_scratch", (T, D), F32, kind="Internal").ap()
    k.gate_dram = nc.dram_tensor("gate_scratch", (16, P, T), F32, kind="Internal").ap()
    plan(nc, k)
    stage_input(nc, k)
    k.end_stage()
    stage_gla_projection(nc, k)
    k.end_stage()
    stage_gated_attention(nc, k, k.gla, 0)
    k.end_stage()
    stage_hgrn_projection(nc, k)
    k.end_stage()
    stage_gated_attention(nc, k, k.hgrn, 4)
    k.end_stage()
    stage_stick_projection(nc, k)
    k.end_stage()
    stage_stick_attention(nc, k)
    k.end_stage()
    stage_first_output(nc, k)
    k.end_stage()
    stage_second_projection(nc, k)
    k.end_stage()
    stage_index_scores(nc, k)
    k.end_stage()
    stage_select(nc, k)
    k.end_stage()
    stage_sparse_attention(nc, k)
    k.end_stage()
    stage_latent_projection(nc, k)
    k.end_stage()
    stage_latent_attention(nc, k)
    k.end_stage()
    stage_merge(nc, k)
    k.end_stage()
    stage_ffn_up(nc, k)
    k.end_stage()
    stage_ffn_down(nc, k)


INPUTS = ['x', 'c', 'w_ada', 'b_ada', 'w_in', 'w_gla_gate2', 'b_gla_gate', 'gla_norm_w', 'hgrn_lb_logits',
          'hgrn_norm_w', 'w_out', 'final_norm_w', 'positions_2', 'norm_mix_g_2', 'w_in_2', 'idx_k_norm_g_2',
          'q_a_norm_g_2', 'kv_a_norm_g_2', 'w_uq_2', 'w_uk_2', 'w_uv_2', 'w_branch_a_2', 'w_branch_b_2',
          'w_out_2', 'norm_ffn_g_2', 'w_up_2', 'conv_w_2', 'conv_b_2', 'w_down_2', 'norm_final_g_2']


def kernel(**inputs):
    import numpy as _np
    import concourse.bacc as _bacc
    from concourse import mybir as _mybir
    from concourse.bass_utils import run_bass_kernel_spmd as _run

    nc = _bacc.Bacc("TRN2", target_bir_lowering=False, num_devices=1, dynamic_dma_scratch_size=1024)
    arrays, views = {}, {}
    for name in INPUTS:
        a = _np.ascontiguousarray(inputs[name])
        arrays[f"in_{name}"] = a
        views[name] = nc.dram_tensor(f"in_{name}", a.shape, _mybir.dt.from_np(a.dtype), kind="ExternalInput").ap()
    views["out"] = nc.dram_tensor("out_0", (1, T, D), _mybir.dt.float32, kind="ExternalOutput").ap()
    build(nc, views)
    r = _run(nc, [arrays], core_ids=[0])
    return r.results[0]["out_0"]
```

```python
import math
import numpy as np
import concourse.bass as bass
from concourse import mybir

F32 = mybir.dt.float32
F32R = mybir.dt.float32r
U32 = mybir.dt.uint32
I32 = mybir.dt.int32
ALU = mybir.AluOpType
ACT = mybir.ActivationFunctionType
AX = mybir.AxisListType

P = 128
T = 1024
NT = T // P
D = 1024
KB = D // P
W512 = 512
EPS = 1e-6
MASKED = -1e30
SBUF_BASE = 1280

QA, KA, VA, LRA, GA, QB, FB, IB, GB, QC, KC, VC, GC = (
    0, 256, 512, 1024, 1040, 1552, 1808, 2064, 2320, 2576, 2832, 3088, 3344)
GLA_TAU = 16.0
RANK = 16
HEADS1 = 4
DK = 64
AQ, AK, AV, IQ, IK, IW, CQ, CKV, KR, GTA, GTB = (
    0, 512, 640, 768, 1280, 1344, 1352, 1608, 1736, 1768, 2792)
TOPK = 256
THETA = 500000.0
DFF = 2816
FBLK = DFF // P


class Steps:

    def __init__(self, k, name):
        self.sem, self.n = k.sem(name), 0

    def mark(self, ins):
        ins.then_inc(self.sem, 1)
        self.n += 1
        return self.n


class Weights:

    RING = 2

    def __init__(self, nc, place):
        self.slot = [place(f"weights_{i}", [P, KB * W512], 8 + 16 * i) for i in range(self.RING)]
        self.landed = [nc.alloc_semaphore(name=f"weights_landed_{i}") for i in range(self.RING)]
        self.freed = {}
        self.chunks = []
        self.issued = 0
        self.count = [0] * self.RING
        self.need = []

    def add(self, pieces, blocks, width):
        self.chunks.append((pieces, blocks, width))
        return len(self.chunks) - 1

    def view(self, n):
        _, blocks, width = self.chunks[n]
        return self.slot[n % self.RING][:, 0:blocks * width].rearrange("p (k n) -> p k n", n=width)

    def load(self, sp, n):
        if n >= self.RING:
            sp.wait_ge(*self.freed[n - self.RING])
        v, i = self.view(n), n % self.RING
        for at, src, width in self.chunks[n][0]:
            sp.dma_start(v[:, :, at:at + width], src.rearrange("(k p) n -> p k n", p=P)).then_inc(self.landed[i], 16)
            self.count[i] += 16
        self.need.append(self.count[i])

    def load_up_to(self, sp, n):
        while self.issued <= min(n, len(self.chunks) - 1):
            self.load(sp, self.issued)
            self.issued += 1

    def wait(self, pe, n):
        pe.wait_ge(self.landed[n % self.RING], self.need[n])


class Kernel:

    def __init__(self, nc):
        self.nc, self.own, self.cleared = nc, [], []

    def sem(self, name):
        self.own.append(self.nc.alloc_semaphore(name=name))
        return self.own[-1]

    def kept_sem(self, name):
        return self.nc.alloc_semaphore(name=name)

    def end_stage(self):
        for sem in self.cleared:
            self.nc.release_semaphore(sem)
        for sem in self.own:
            self.nc.gpsimd.sem_clear(sem)
        self.own, self.cleared = [], self.own


def plan(nc, k):

    def place(name, shape, kb, dt=F32):
        return nc.alloc_sbuf_tensor_at(name, shape, dt, offset=SBUF_BASE + int(kb * 1024))

    k.place = place
    k.ident = place("ident", [P, P], 0)
    k.levels = place("level_masks", [P, 7, P], 0.5)
    k.strict = place("strict_mask", [P, P], 4)
    k.shiftcol = place("shift_col", [P, KB], 4.5)
    k.scalecol = place("scale_col", [P, KB], 4.5625)
    k.small = place("small", [P, 256], 5)
    k.w = Weights(nc, place)
    k.output_stored = k.kept_sem("output_stored")
    k.hT = place("hT", [P, KB, T], 40)
    k.keep = place("keep", [P, T], 208)
    k.oT = place("mixed_outT", [P, KB, T], 72)
    k.banks = nc.alloc_psum_tensor("banks", [P, 8, W512], F32)
    w = k.w
    cols = lambda a, lo, hi: a[:, lo:hi]
    w_in, w_in2 = k.w_in[0], k.w_in_2[0]
    k.c_qka = w.add([(0, cols(w_in, QA, VA), 512)], KB, 512)
    k.c_va = w.add([(0, cols(w_in, VA, LRA), 512)], KB, 512)
    k.c_ga = w.add([(0, cols(w_in, GA, QB), 512)], KB, 512)
    k.c_qfb = w.add([(0, cols(w_in, QB, IB), 512)], KB, 512)
    k.c_igb = w.add([(0, cols(w_in, IB, QC), 512)], KB, 512)
    k.c_qkc = w.add([(0, cols(w_in, QC, VC), 512)], KB, 512)
    k.c_vgc = w.add([(0, cols(w_in, VC, 3600), 512)], KB, 512)
    k.c_out = [w.add([(0, cols(k.w_out[0], h * 512, h * 512 + 512), 512)], KB, 512) for h in range(2)]
    k.c_aq = w.add([(0, cols(w_in2, AQ, AK), 512)], KB, 512)
    k.c_akv = w.add([(0, cols(w_in2, AK, IQ), 256)], KB, 256)
    k.c_iq = w.add([(0, cols(w_in2, IQ, IK), 512)], KB, 512)
    k.c_mix = w.add([(0, cols(w_in2, IK, GTA), GTA - IK)], KB, GTA - IK)
    k.c_gate = [w.add([(0, cols(w_in2, GTA + h * 512, GTA + h * 512 + 512), 512)], KB, 512) for h in range(4)]
    k.c_ba = w.add([(0, k.w_branch_a_2[0], D)], 4, D)
    k.c_bb = w.add([(0, k.w_branch_b_2[0], D)], 4, D)
    k.c_out2 = [w.add([(0, cols(k.w_out_2[0], h * 512, h * 512 + 512), 512)], KB, 512) for h in range(2)]
    up = k.w_up_2[0]
    k.c_up = [w.add([(0, cols(up, f * 256, f * 256 + 256), 256),
                     (256, cols(up, DFF + f * 256, DFF + f * 256 + 256), 256)], KB, 512) for f in range(FBLK // 2)]
    down = k.w_down_2[0]
    k.c_down = [[w.add([(0, down[b * P:min(b + 8, FBLK) * P, h * 512:h * 512 + 512], 512)], min(8, FBLK - b), 512)
                 for b in range(0, FBLK, 8)] for h in range(2)]


class NormTranspose:

    def __init__(self, nc, k, name, x, scratch, out=None):
        self.nc, self.k, self.x, self.scratch, self.bank0 = nc, k, x, scratch, 0
        self.out = x if out is None else out
        self.squares = k.small[:, 0:8]
        self.rms = k.small[:, 8:16]
        self.rstd = k.small[:, 16:24]
        self.root = k.small[:, 24:32]
        s = lambda n: k.sem(f"{name}_{n}")
        self.summed, self.mean, self.rooted, self.inverted = s("summed"), s("mean"), s("rooted"), s("inverted")
        self.divided, self.turned, self.by_act, self.by_dve = s("divided"), s("turned"), s("stored_act"), s("stored_dve")

    def act_stats(self, act, ready):
        for i in range(NT):
            ready(act, i)
            slots = self.scratch.shape[1]
            if i >= slots:
                act.wait_ge(self.summed, i - slots + 1)
            self.nc.scalar.activation(self.scratch[:, i % slots, :], self.x[:, i, :], ACT.Square,
                                      accum_out=self.squares[:, i:i + 1]).then_inc(self.summed, 1)
        act.wait_ge(self.mean, 1)
        self.nc.scalar.activation(self.root, self.rms, ACT.Sqrt).then_inc(self.rooted, 1)

    def dve_stats(self, dve):
        dve.wait_ge(self.summed, NT)
        self.nc.vector.tensor_scalar(self.rms, self.squares, 1.0 / D, EPS, ALU.mult, ALU.add).then_inc(self.mean, 1)
        dve.wait_ge(self.rooted, 1)
        self.nc.vector.reciprocal(self.rstd, self.root).then_inc(self.inverted, 1)
        dve.wait_ge(self.inverted, 1)

    def dve_divide(self, dve):
        for i in range(NT):
            self.nc.vector.tensor_scalar(self.out[:, i, :], self.x[:, i, :], self.rstd[:, i:i + 1], None,
                                         ALU.mult).then_inc(self.divided, 1)

    def pe_transpose(self, pe):
        for i in range(NT):
            pe.wait_ge(self.divided, i + 1)
            for g in range(2):
                j = 2 * i + g
                if j >= 4:
                    pe.wait_ge(self.by_dve if g else self.by_act, (j - 4) // 2 + 1)
                for b in range(4):
                    ins = self.nc.tensor.transpose(self.k.banks[:, self.bank0 + j % 4, b * P:(b + 1) * P],
                                                   self.out[:, i, (4 * g + b) * P:(4 * g + b + 1) * P], self.k.ident[:, :])
                ins.then_inc(self.turned, 1)

    def store(self, eng, g):
        for i in range(NT):
            j = 2 * i + g
            eng.wait_ge(self.turned, j + 1)
            src = self.k.banks[:, self.bank0 + j % 4, :].rearrange("p (b t) -> p b t", t=P)
            dst = self.k.hT[:, 4 * g:4 * g + 4, i * P:(i + 1) * P]
            if g:
                self.nc.vector.tensor_copy(dst, src).then_inc(self.by_dve, 1)
            else:
                self.nc.scalar.activation(dst, src, ACT.Copy).then_inc(self.by_act, 1)


def weigh_rows(eng, ready, w, cact, total, step):
    eng.wait_ge(*ready)
    for b in range(KB):
        if b == 0:
            n = step.mark(eng.tensor_scalar(total, w[:, b, :], cact[:, 0:1], None, ALU.mult))
        else:
            n = step.mark(eng.scalar_tensor_tensor(out=total, in0=w[:, b, :], scalar=cact[:, b:b + 1], in1=total,
                                                   op0=ALU.mult, op1=ALU.add))
        eng.wait_ge(step.sem, n)


def stage_input(nc, k):
    x = k.place("x_tiles", [P, NT, D], 72)
    ada = k.place("ada_weights", [P, 4, KB, 512], 104)
    total = k.place("ada_totals", [P, 4, 512], 168)
    k.ada_gate = k.place("ada_gate_weights", [P, 2, KB, 512], 72)
    k.gate_bias = k.place("gate_bias", [P, D], 216)
    k.gate_row = k.place("gate_row", [P, D], 212)
    k.ones = k.place("ones_square", [P, P], 7)
    k.ada_gate_in = [k.kept_sem(f"ada_gate_in_{i}") for i in range(2)]
    ccol, cact, bcol = k.small[:, 32:40], k.small[:, 40:48], k.small[:, 48:64]
    k.cact = cact
    norm = NormTranspose(nc, k, "norm1", x, k.hT)
    s = lambda n: k.sem(n)
    x_in = [s(f"x_in_{i}") for i in range(2)]
    vec_in, ada_in = s("c_in"), [s(f"ada_in_{i}") for i in range(4)]
    built, silu_done = s("constants_built"), s("c_silu")
    ada_mm, cols_done, hmod = s("ada_cols"), s("mod_cols_done"), s("h_modulated")
    weighed = Steps(k, "rows_weighed")
    pool_step = Steps(k, "pool_step1")
    xd = k.x[0].rearrange("(i p) d -> i p d", p=P)
    wd = k.w_ada[0]
    with nc.Block() as block:
        @block.sync
        def _(sp):
            for h in range(2):
                sp.dma_start(x[:, 4 * h:4 * h + 4, :], xd[4 * h:4 * h + 4].rearrange("i p d -> p i d")).then_inc(x_in[h], 16)
            for n in range(4):
                sp.dma_start(ada[:, n, :, :], wd[:, n * 512:(n + 1) * 512].rearrange("(k p) n -> p k n", p=P)).then_inc(ada_in[n], 16)
            k.w.load_up_to(sp, 0)
            sp.wait_ge(norm.turned, 2 * NT)
            for n in range(2):
                sp.dma_start(k.ada_gate[:, n, :, :],
                             wd[:, (n + 4) * 512:(n + 5) * 512].rearrange("(k p) n -> p k n", p=P)).then_inc(k.ada_gate_in[n], 16)
            k.w.load_up_to(sp, 1)

        @block.gpsimd
        def _(pool):
            pool.memset(k.ones[:, :], 1.0).then_inc(pool_step.sem, 1)
            pool.memset(k.ident[:, :], 0.0).then_inc(pool_step.sem, 1)
            pool.memset(k.strict[:, :], 1.0).then_inc(pool_step.sem, 1)
            pool.memset(k.levels[:, :, :], 0.0).then_inc(pool_step.sem, 1)
            n = 4
            pool.wait_ge(pool_step.sem, n)
            pool.affine_select(out=k.ident[:, :], in_=k.ident[:, :], compare_op=ALU.not_equal, fill=1.0, base=0,
                               pattern=[[-1, P]], channel_multiplier=1).then_inc(built, 1)
            pool.affine_select(out=k.strict[:, :], in_=k.strict[:, :], compare_op=ALU.is_gt, fill=0.0, base=0,
                               pattern=[[-1, P]], channel_multiplier=1).then_inc(built, 1)
            for l in range(7):
                h = 1 << l
                v = k.levels[:, l, :].rearrange("p (b two h) -> p b two h", two=2, h=h)[:, :, 1, :]
                nb = P // (2 * h)
                pool.memset(v, 1.0).then_inc(pool_step.sem, 1)
                n += 1
                pool.wait_ge(pool_step.sem, n)
                pool.affine_select(out=v, in_=v, compare_op=ALU.is_ge, fill=0.0, base=0,
                                   pattern=[[-2 * h, nb], [0, h]], channel_multiplier=1).then_inc(pool_step.sem, 1)
                n += 1
                pool.wait_ge(pool_step.sem, n)
                pool.affine_select(out=v, in_=v, compare_op=ALU.is_ge, fill=0.0, base=h - 1,
                                   pattern=[[2 * h, nb], [0, h]], channel_multiplier=-1).then_inc(built, 1)
        @block.scalar
        def _(act):
            act.dma_start(ccol, k.c.rearrange("o (k p) -> p (o k)", p=P), allow_slow_non_contiguous=True).then_inc(vec_in, 16)
            act.dma_start(bcol, k.b_ada[0, 0:2 * D].rearrange("(k p) -> p k", p=P), allow_slow_non_contiguous=True).then_inc(vec_in, 16)
            act.dma_start(k.gate_bias[:, :], k.b_ada[0, 2 * D:3 * D].partition_broadcast(P)).then_inc(vec_in, 16)
            norm.act_stats(act, lambda e, i: e.wait_ge(x_in[i // 4], 16))
            act.wait_ge(vec_in, 48)
            nc.scalar.activation(cact, ccol, ACT.Silu).then_inc(silu_done, 1)
            norm.store(act, 0)
            act.wait_ge(cols_done, 2)
            act.wait_ge(norm.by_dve, NT)
            act.wait_ge(norm.by_act, NT)
            for b in range(0, KB, 2):
                nc.scalar.activation(k.hT[:, b, :], k.hT[:, b, :], ACT.Identity, bias=k.shiftcol[:, b:b + 1],
                                     scale=k.scalecol[:, b:b + 1]).then_inc(hmod, 1)

        @block.tensor
        def _(pe):
            pe.wait_ge(built, 1)
            norm.pe_transpose(pe)
            for n in range(4):
                pe.wait_ge(weighed.sem, KB * (n + 1))
                for j in range(4):
                    ins = nc.tensor.matmul(k.banks[:, 4, 4 * n + j:4 * n + j + 1], total[:, n, j * P:(j + 1) * P],
                                           k.ones[:, 0:1], start=True, stop=True)
                ins.then_inc(ada_mm, 1)

        @block.vector
        def _(dve):
            norm.dve_stats(dve)
            norm.dve_divide(dve)
            dve.wait_ge(silu_done, 1)
            weigh_rows(nc.vector, (ada_in[0], 16), ada[:, 0], cact, total[:, 0, :], weighed)
            norm.store(dve, 1)
            for n in range(1, 4):
                weigh_rows(nc.vector, (ada_in[n], 16), ada[:, n], cact, total[:, n, :], weighed)
            dve.wait_ge(vec_in, 48)
            dve.wait_ge(ada_mm, 4)
            nc.vector.tensor_tensor(k.shiftcol[:, :], k.banks[:, 4, 0:8], bcol[:, 0:8], ALU.add).then_inc(cols_done, 1)
            nc.vector.scalar_tensor_tensor(out=k.scalecol[:, :], in0=k.banks[:, 4, 8:16], scalar=1.0, in1=bcol[:, 8:16],
                                           op0=ALU.add, op1=ALU.add).then_inc(cols_done, 1)
            dve.wait_ge(cols_done, 2)
            dve.wait_ge(norm.by_act, NT)
            dve.wait_ge(norm.by_dve, NT)
            for b in range(1, KB, 2):
                nc.vector.tensor_scalar(k.hT[:, b, :], k.hT[:, b, :], k.scalecol[:, b:b + 1], k.shiftcol[:, b:b + 1],
                                        ALU.mult, ALU.add).then_inc(hmod, 1)


class Projection:

    def __init__(self, nc, k, name, jobs, banks=8, src=None, parts=None):
        self.parts = parts
        self.nc, self.k, self.jobs, self.nb, self.src = nc, k, jobs, banks, src
        self.done = k.sem(f"{name}_product")
        self.stored = {e: k.sem(f"{name}_stored_{e}") for e in ("act", "dve")}
        self.nth = []
        count = {"act": 0, "dve": 0}
        for job in jobs:
            count[job["by"]] += 1
            self.nth.append(count[job["by"]])
            k.w.freed[job["chunk"]] = (self.done, len(self.nth))
        self.count = count

    def bank(self, j):
        return self.k.banks[:, j % self.nb, :]

    def pe_jobs(self, pe, lo, hi):
        k, w = self.k, self.k.w
        src = self.src if self.src is not None else k.hT
        for j in range(lo, hi):
            job = self.jobs[j]
            if self.parts is None and (j == 0 or self.jobs[j - 1]["chunk"] != job["chunk"]):
                w.wait(pe, job["chunk"])
            if j >= self.nb:
                o = j - self.nb
                pe.wait_ge(self.stored[self.jobs[o]["by"]], self.nth[o])
            wv = w.view(job["chunk"])
            for b in range(KB):
                if self.parts is not None:
                    i, width = job["tile"], job["width"]
                    ins = self.parts.product(pe, self.bank(j)[:, 0:width], job["chunk"], i, b, width)
                elif job["kind"] == "tokens":
                    i, c0, width = job["tile"], job["col"], job["width"]
                    ins = self.nc.tensor.matmul(self.bank(j)[:, 0:width], src[:, b, i * P:(i + 1) * P],
                                                wv[:, b, c0:c0 + width], start=(b == 0), stop=(b == KB - 1))
                else:
                    c, h = job["col"], job["half"]
                    ins = self.nc.tensor.matmul(self.bank(j), wv[:, b, c:c + P], src[:, b, h * 512:(h + 1) * 512],
                                                start=(b == 0), stop=(b == KB - 1))
            ins.then_inc(self.done, 1)


def feature_jobs(chunk, col, dest, how="copy", by=None):
    return [dict(chunk=chunk, kind="features", col=col, half=h, dest=dest, how=how,
                 by=by or ("act" if h == 0 else "dve")) for h in range(2)]


def token_jobs(chunk, col, width, dest, how="copy", by=None):
    return [dict(chunk=chunk, kind="tokens", tile=i, col=col, width=width, dest=dest, how=how,
                 by=by or ("act" if i % 2 == 0 else "dve")) for i in range(NT)]


def products_of_parts(nc, out, a_hi, a_lo, b_hi, b_lo, start, stop):
    nc.tensor.matmul(out, a_hi, b_hi, start=start, stop=False)
    nc.tensor.matmul(out, a_hi, b_lo, start=False, stop=False)
    return nc.tensor.matmul(out, a_lo, b_hi, start=False, stop=stop)


class Parts:

    def __init__(self, nc, k, name, chunks, h_hi, h_lo, kb, ready=None):
        self.ready = ready
        self.tiles = 0
        self.nc, self.k, self.chunks, self.h_hi, self.h_lo = nc, k, chunks, h_hi, h_lo
        self.hi = [k.place(f"{name}_hi_{i}", [P, KB * W512], at, F32R) for i, at in enumerate(kb)]
        self.lo = [k.place(f"{name}_lo_{n % 2}", [P, KB * W512], 8 + 16 * (n % 2), F32R) for n in chunks[:2]]
        self.hi_done, self.lo_done = k.sem(f"{name}_hi_done"), k.sem(f"{name}_lo_done")
        self.waited = 0

    def view(self, buf, n):
        _, blocks, width = self.k.w.chunks[n]
        return buf[self.chunks.index(n) % 2][:, 0:blocks * width].rearrange("p (k n) -> p k n", n=width)

    def split_act(self, act, n):
        if self.chunks.index(n) >= 2:
            act.wait_ge(*self.k.w.freed[n - 2])
        self.k.w.wait(act, n)
        for b in range(KB):
            self.nc.scalar.activation(self.view(self.hi, n)[:, b, :], self.k.w.view(n)[:, b, :], ACT.Copy).then_inc(self.hi_done, 1)

    def split_dve(self, dve, n):
        self.k.w.wait(dve, n)
        for b in range(KB):
            dve.wait_ge(self.hi_done, KB * self.chunks.index(n) + b + 1)
            self.nc.vector.tensor_tensor(self.view(self.lo, n)[:, b, :], self.k.w.view(n)[:, b, :],
                                         self.view(self.hi, n)[:, b, :], ALU.subtract).then_inc(self.lo_done, 1)

    def product(self, pe, out, n, i, b, width):
        need = KB * self.chunks.index(n) + b + 1
        if self.waited < need:
            pe.wait_ge(self.lo_done, need)
            self.waited = need
        if self.ready is not None and self.tiles <= i:
            self.tiles = i + 1
            pe.wait_ge(self.ready, i + 1)
        tok = slice(i * P, (i + 1) * P)
        return products_of_parts(self.nc, out, self.h_hi[:, b, tok], self.h_lo[:, b, tok],
                                 self.view(self.hi, n)[:, b, 0:width], self.view(self.lo, n)[:, b, 0:width], b == 0, b == KB - 1)


def store_act(nc, out, src, how):
    if how == "copy":
        return nc.scalar.activation(out, src, ACT.Copy)
    if how == "silu":
        return nc.scalar.activation(out, src, ACT.Silu)
    if how == "sigmoid":
        return nc.scalar.activation(out, src, ACT.Sigmoid)
    return nc.scalar.activation(out, src, ACT.Copy, scale=float(how))


def store_dve(nc, out, src, how):
    if how == "copy":
        return nc.vector.tensor_copy(out, src)
    return nc.vector.tensor_scalar(out, src, float(how), None, ALU.mult)


def job_out(job):
    if job["kind"] == "tokens":
        return job["dest"](job["tile"])
    return job["dest"][:, job["half"] * 512:(job["half"] + 1) * 512]


def run_stores(nc, proj, eng, who):
    for j, job in enumerate(proj.jobs):
        if job["by"] != who:
            continue
        width = job["width"] if job["kind"] == "tokens" else 512
        eng.wait_ge(proj.done, j + 1)
        store = store_act if who == "act" else store_dve
        store(nc, job_out(job), proj.bank(j)[:, 0:width], job["how"]).then_inc(proj.stored[who], 1)


class Mixer:

    def __init__(self, k, name, dv):
        p = k.place
        self.name, self.dv = name, dv
        self.qT = p(f"{name}_qT", [P, 2, T], 104)
        self.kT = p(f"{name}_kT", [P, 2, T], 112)
        self.bT = p(f"{name}_bT", [P, 2, T], 120)
        self.v = p(f"{name}_v", [P, NT, 4 * dv], 128)
        self.g = p(f"{name}_g", [P, NT, 4 * dv], 144)
        self.t0 = p(f"{name}_t0", [P, 2, T], 160)
        self.t1 = p(f"{name}_t1", [P, 2, T], 168)
        self.t2 = p(f"{name}_t2", [P, 2, T], 176)
        self.keep = k.keep
        self.gain = p(f"{name}_gain", [P, dv], 6)


def softplus_act(nc, act, m, chain, ready):
    ready(act)
    n = chain.mark(nc.scalar.activation(m.t1[:, :, :], m.t0[:, :, :], ACT.Abs))
    act.wait_ge(chain.sem, n)
    n = chain.mark(nc.scalar.activation(m.t1[:, :, :], m.t1[:, :, :], ACT.Exp, scale=-1.0))
    act.wait_ge(chain.sem, n)
    return chain.mark(nc.scalar.activation(m.t1[:, :, :], m.t1[:, :, :], ACT.Ln, bias=1.0))


def summed_decay_dve(nc, dve, m, chain):
    for g in range(2):
        n = chain.mark(nc.vector.tensor_tensor_scan(m.bT[:, g, :], m.keep[:, :], m.t1[:, g, :], 0.0, ALU.mult, ALU.add))
    return n


def stage_gla_projection(nc, k):
    m = k.gla = Mixer(k, "gla", 128)
    p = k.place
    lra_w = p("lra_w", [P, KB, RANK], 184)
    gate2 = p("gate2_w", [RANK, 256], 185)
    lraT = p("lraT", [RANK, T], 188)
    bias = k.small[:, 64:66]
    jobs = []
    for g in range(2):
        jobs += feature_jobs(k.c_qka, g * P, m.qT[:, g, :], DK ** -0.5)
    for g in range(2):
        jobs += feature_jobs(k.c_qka, 256 + g * P, m.kT[:, g, :])
    jobs += token_jobs(k.c_va, 0, 512, lambda i: m.v[:, i, :])
    jobs += token_jobs(k.c_ga, 0, 512, lambda i: m.g[:, i, :], "silu", "act")
    proj = Projection(nc, k, "gla_proj", jobs, banks=6)
    s = lambda n: k.sem(n)
    vec_in, lra_mm, lra_st, z_mm, z_st = s("gla_vec_in"), s("lra_mm"), s("lra_stored"), s("gate_z"), s("gate_z_stored")
    a, d = Steps(k, "gla_gate_act"), Steps(k, "gla_gate_dve")
    weighed, gate_mm = Steps(k, "gate_rows_weighed"), k.sem("ada_gate")
    totals = p("ada_gate_totals", [P, 2, 512], 192)
    with nc.Block() as block:
        @block.sync
        def _(sp):
            k.w.load_up_to(sp, k.c_qfb + 1)

        @block.gpsimd
        def _(pool):
            n = Steps(k, "pool_step2")
            c = n.mark(pool.memset(m.keep[:, :], 1.0))
            pool.wait_ge(n.sem, c)
            pool.memset(m.keep[:, :].rearrange("p (i t) -> p i t", t=P)[:, :, 0:1], 0.0).then_inc(d.sem, 1)


        d.n += 1

        @block.scalar
        def _(act):
            act.dma_start(lra_w[:, :, :], k.w_in[0][:, LRA:GA].rearrange("(k p) n -> p k n", p=P)).then_inc(vec_in, 16)
            act.dma_start(gate2[:, :], k.w_gla_gate2[0]).then_inc(vec_in, 16)
            act.dma_start(bias, k.b_gla_gate[0].rearrange("(k p) -> p k", p=P), allow_slow_non_contiguous=True).then_inc(vec_in, 16)
            act.dma_start(m.gain[:, :], k.gla_norm_w[0].partition_broadcast(P)).then_inc(vec_in, 16)
            for h in range(2):
                act.wait_ge(lra_mm, h + 1)
                nc.scalar.activation(lraT[:, h * 512:(h + 1) * 512], k.banks[0:RANK, 6 + h, :], ACT.Copy).then_inc(lra_st, 1)
            run_stores_range(nc, proj, act, "act", 0, 16)
            softplus_act(nc, act, m, a, lambda e: e.wait_ge(z_st, 4))
            run_stores_range(nc, proj, act, "act", 16, 24)

        @block.tensor
        def _(pe):
            pe.wait_ge(vec_in, 64)
            for h in range(2):
                for b in range(KB):
                    ins = nc.tensor.matmul(k.banks[0:RANK, 6 + h, :], lra_w[:, b, :], k.hT[:, b, h * 512:(h + 1) * 512],
                                           start=(b == 0), stop=(b == KB - 1))
                ins.then_inc(lra_mm, 1)
            proj.pe_jobs(pe, 0, 8)
            pe.wait_ge(lra_st, 2)
            for g in range(2):
                if g:
                    proj.pe_jobs(pe, 8, 16)
                    pe.wait_ge(z_st, 2)
                for h in range(2):
                    nc.tensor.matmul(k.banks[:, 6 + h, :], gate2[:, g * P:(g + 1) * P], lraT[:, h * 512:(h + 1) * 512],
                                     start=True, stop=True).then_inc(z_mm, 1)
            proj.pe_jobs(pe, 16, 24)
            pe.wait_ge(z_st, 4)
            pe.wait_ge(weighed.sem, 2 * KB)
            for h in range(2):
                nc.tensor.matmul(k.banks[:, 6 + h, :], k.ones[:, :], totals[:, h, :], start=True, stop=True).then_inc(gate_mm, 1)

        @block.vector
        def _(dve):
            def negated(g):
                for h in range(2):
                    dve.wait_ge(z_mm, 2 * g + h + 1)
                    nc.vector.tensor_scalar(m.t0[:, g, h * 512:(h + 1) * 512], k.banks[:, 6 + h, :], bias[:, g:g + 1], -1.0,
                                            ALU.add, ALU.mult).then_inc(z_st, 1)
            dve.wait_ge(vec_in, 64)
            run_stores_range(nc, proj, dve, "dve", 0, 8)
            negated(0)
            run_stores_range(nc, proj, dve, "dve", 8, 16)
            negated(1)
            for h in range(2):
                weigh_rows(nc.vector, (k.ada_gate_in[h], 16), k.ada_gate[:, h], k.cact, totals[:, h, :], weighed)
            dve.wait_ge(a.sem, 3)
            dve.wait_ge(z_st, 4)
            n = d.mark(nc.vector.scalar_tensor_tensor(out=m.t1[:, :, :], in0=m.t0[:, :, :], scalar=0.0, in1=m.t1[:, :, :],
                                                      op0=ALU.max, op1=ALU.add))
            dve.wait_ge(d.sem, n)
            n = d.mark(nc.vector.tensor_scalar(m.t1[:, :, :], m.t1[:, :, :], -1.0 / GLA_TAU, None, ALU.mult))
            dve.wait_ge(d.sem, n)
            summed_decay_dve(nc, dve, m, d)
            for h in range(2):
                dve.wait_ge(gate_mm, h + 1)
                cols = slice(h * 512, (h + 1) * 512)
                d.mark(nc.vector.tensor_tensor(k.gate_row[:, cols], k.banks[:, 6 + h, :], k.gate_bias[:, cols], ALU.add))


def run_stores_range(nc, proj, eng, who, lo, hi):
    for j in range(lo, hi):
        job = proj.jobs[j]
        if job["by"] != who:
            continue
        width = job["width"] if job["kind"] == "tokens" else 512
        eng.wait_ge(proj.done, j + 1)
        store = store_act if who == "act" else store_dve
        store(nc, job_out(job), proj.bank(j)[:, 0:width], job["how"]).then_inc(proj.stored[who], 1)


def stage_hgrn_projection(nc, k):
    m = k.hgrn = Mixer(k, "hgrn", 64)
    lg, ex, tot, pr, lb, om = (k.small[:, c:c + 2] for c in (66, 68, 70, 72, 74, 76))
    jobs = []
    for g in range(2):
        jobs += feature_jobs(k.c_qfb, g * P, m.qT[:, g, :], "silu", "act")
    for g in range(2):
        jobs += feature_jobs(k.c_qfb, 256 + g * P, m.t2[:, g, :], "copy", "dve")
    jobs += token_jobs(k.c_igb, 0, 256, lambda i: m.v[:, i, :])
    jobs += token_jobs(k.c_igb, 256, 256, lambda i: m.g[:, i, :], "silu", "act")
    proj = Projection(nc, k, "hgrn_proj", jobs)
    vec_in = k.sem("hgrn_vec_in")
    a, d = Steps(k, "hgrn_act"), Steps(k, "hgrn_dve")
    with nc.Block() as block:
        @block.sync
        def _(sp):
            k.w.load_up_to(sp, k.c_qkc + 1)

        @block.scalar
        def _(act):
            act.dma_start(lg, k.hgrn_lb_logits[0].rearrange("(k p) -> p k", p=P), allow_slow_non_contiguous=True).then_inc(vec_in, 16)
            act.dma_start(m.gain[:, :], k.hgrn_norm_w[0].partition_broadcast(P)).then_inc(vec_in, 16)
            run_stores_range(nc, proj, act, "act", 0, 4)
            act.wait_ge(proj.stored["dve"], 4)
            a.mark(nc.scalar.activation(m.kT[:, :, :], m.t2[:, :, :], ACT.Sigmoid, scale=-1.0))
            a.mark(nc.scalar.activation(m.t1[:, :, :], m.t2[:, :, :], ACT.Abs))
            act.wait_ge(d.sem, 1)
            a.mark(nc.scalar.activation(ex, tot, ACT.Exp))
            act.wait_ge(a.sem, 2)
            a.mark(nc.scalar.activation(m.t1[:, :, :], m.t1[:, :, :], ACT.Exp, scale=-1.0))
            act.wait_ge(a.sem, 4)
            a.mark(nc.scalar.activation(m.t1[:, :, :], m.t1[:, :, :], ACT.Ln, bias=1.0))
            act.wait_ge(a.sem, 5)
            a.mark(nc.scalar.activation(m.t0[:, :, :], m.t2[:, :, :], ACT.Exp, scale=-1.0))
            act.wait_ge(d.sem, 8)
            a.mark(nc.scalar.activation(m.t0[:, :, :], m.t0[:, :, :], ACT.Ln))
            run_stores_range(nc, proj, act, "act", 4, len(jobs))

        @block.tensor
        def _(pe):
            proj.pe_jobs(pe, 0, len(jobs))

        @block.vector
        def _(dve):
            run_stores_range(nc, proj, dve, "dve", 0, 8)
            dve.wait_ge(vec_in, 32)
            d.mark(nc.vector.tensor_tensor(tot, lg, lg, ALU.subtract))
            dve.wait_ge(a.sem, 3)
            d.mark(nc.vector.reciprocal(tot, ex))
            dve.wait_ge(d.sem, 2)
            d.mark(nc.vector.tensor_tensor(pr, ex, tot, ALU.mult))
            dve.wait_ge(d.sem, 3)
            d.mark(nc.vector.tensor_tensor(lb, pr, pr, ALU.subtract))
            dve.wait_ge(d.sem, 4)
            d.mark(nc.vector.tensor_scalar(om, lb, -1.0, 1.0, ALU.mult, ALU.add))
            dve.wait_ge(a.sem, 6)
            for g in range(2):
                d.mark(nc.vector.tensor_scalar(m.t0[:, g, :], m.t0[:, g, :], 3e38, lb[:, g:g + 1], ALU.min, ALU.mult))
            dve.wait_ge(d.sem, 7)
            n = d.mark(nc.vector.tensor_scalar(m.t0[:, :, :], m.t0[:, :, :], 1.0, 1.0, ALU.add, ALU.mult))
            for g in range(2):
                d.mark(nc.vector.tensor_scalar(m.kT[:, g, :], m.kT[:, g, :], om[:, g:g + 1], None, ALU.mult))
            n = d.mark(nc.vector.scalar_tensor_tensor(out=m.t1[:, :, :], in0=m.t2[:, :, :], scalar=0.0, in1=m.t1[:, :, :],
                                                      op0=ALU.min, op1=ALU.subtract))
            dve.wait_ge(a.sem, 7)
            dve.wait_ge(d.sem, n)
            n = d.mark(nc.vector.tensor_tensor(m.t1[:, :, :], m.t1[:, :, :], m.t0[:, :, :], ALU.add))
            dve.wait_ge(d.sem, n)
            summed_decay_dve(nc, dve, m, d)
            run_stores_range(nc, proj, dve, "dve", 8, len(jobs))


def stage_gated_attention(nc, k, m, first_block):
    dv, nm = m.dv, m.name
    p = k.place
    E = p(f"{nm}_decay", [P, 2, T], 160)
    C = p(f"{nm}_level_keys", [P, 2, T], 168)
    S = p(f"{nm}_scores", [P, 2, NT, P], 176)
    O = p(f"{nm}_out", [P, NT, 2 * dv], 184)
    slot = 1 if dv == P else 3
    ST = p(f"{nm}_state", [P, NT, slot + 1, dv], 192)
    qe = p(f"{nm}_q_decayed", [P, T], 200)
    ke = p(f"{nm}_k_decayed", [P, T], 204)
    ktok = p(f"{nm}_k_tokens", [P, NT, P], 216)
    junk = p(f"{nm}_square_scratch", [P, 2, P], 220)
    qpad = p(f"{nm}_q_padded", [P, 2, T], 88 if dv == P else 136)
    Q = p(f"{nm}_level_queries", [P, 2, 2, T // 2], 96)
    own = k.small[:, 248:250]
    dec = k.small[:, 80:88]
    ssq, ms, root, rstd = (k.small[:, c:c + 16] for c in (96, 112, 128, 144))
    nob = 2 * dv // P
    sname = lambda n: k.sem(f"{nm}_{n}")
    diff, expd, level_k, level_q = sname("diff"), sname("exp"), sname("level_keys"), sname("level_queries")
    score, picked, prod, diag = sname("score"), sname("picked"), sname("qk"), sname("diagonal")
    pre, eb, kd, qd, padq = sname("state_diff"), sname("state_exp"), sname("k_decayed"), sname("q_decayed"), sname("q_padded")
    kt_mm, kt_st, u_mm, rec, zeroed = sname("k_turned"), sname("k_stored"), sname("state_added"), sname("state_done"), sname("zeroed")
    o_mm, o_st, turned, t_st = sname("o_product"), sname("o_stored"), sname("o_turned"), sname("oT_stored")
    cleared = sname("cleared")
    squares, gained, rec0 = sname("squares"), sname("gate_gained"), sname("state_head0")
    dn, an, an_o = Steps(k, f"{nm}_dve_norm"), Steps(k, f"{nm}_act_norm"), Steps(k, f"{nm}_act_out")
    bank = lambda b: k.banks[:, b, :]
    base = lambda s: 4 + 2 * (s % 2)
    PICKS = 1 + 4 * 7
    picks = lambda s: PICKS * (s // 8) + 1 + 4 * (s % 8)

    def halves(ap2d, h):
        return ap2d.rearrange("p (n two h) -> p n two h", two=2, h=h)

    def out_of(i, hh):
        c = (i % 2) * 256 + hh * P
        return bank(i // 2), c, c + (hh * dv if dv < P else 0)

    with nc.Block() as block:
        @block.gpsimd
        def _(pool):
            for g in range(2):
                if g:
                    pool.wait_ge(o_mm, 4)
                pool.tensor_tensor(qe[:, :], m.qT[:, g, :], m.kT[:, g, :], ALU.mult).then_inc(prod, 1)
                if g == 0:
                    pool.memset(C[:, :, :], 0.0).then_inc(cleared, 1)
                    pool.memset(ST[:, :, :, :], 0.0).then_inc(cleared, 1)
                for l in range(7):
                    s, h = 7 * g + l, 1 << l
                    pool.wait_ge(expd, s + 1)
                    pool.wait_ge(padq, 2 * g + 2)
                    if s >= 2:
                        pool.wait_ge(score, 2 * (s - 1))
                    for hh in range(2):
                        q4 = halves(qpad[:, hh, :], h)[:, :, 1, :]
                        pool.tensor_tensor(Q[:, s % 2, hh, :].rearrange("p (n h) -> p n h", h=h),
                                           halves(E[:, s % 2, :], h)[:, :, 1, :], q4, ALU.mult).then_inc(level_q, 1)
                    if l == 4:
                        pool.wait_ge(eb, 3 * g + 3)
                        pool.tensor_tensor(qe[:, :], qe[:, :], m.qT[:, g, :], ALU.mult).then_inc(qd, 1)
                if g == 0:
                    gv = m.g[:, :, :].rearrange("p i (h v) -> p (i h) v", v=dv)
                    pool.tensor_tensor(gv, gv, m.gain[:, :].unsqueeze(1).to_broadcast([P, 4 * NT, dv]), ALU.mult).then_inc(gained, 1)

        @block.scalar
        def _(act):
            def exponential(s):
                act.wait_ge(diff, 2 * (s + 1))
                nc.scalar.activation(E[:, s % 2, :], E[:, s % 2, :], ACT.Exp).then_inc(expd, 1)

            def store_out(g):
                for b in range(4):
                    act.wait_ge(o_mm, 4 * g + b + 1)
                    if b == 0 and g:
                        act.wait_ge(turned, nob * 2)
                    for i in (2 * b, 2 * b + 1):
                        for hh in range(2):
                            c, n = out_of(i, hh)[2], 2 * i + hh + 16 * g
                            if n >= 2:
                                act.wait_ge(squares, n - 1)
                            nc.scalar.activation(junk[:, n % 2, 0:dv], bank(b)[:, c:c + dv], ACT.Square,
                                                 accum_out=ssq[:, 2 * i + hh:2 * i + hh + 1]).then_inc(squares, 1)
                    if dv == P:
                        dst, src = O[:, 2 * b:2 * b + 2, :], bank(b).rearrange("p (i v) -> p i v", i=2)
                        nc.scalar.activation(dst, src, ACT.Copy).then_inc(o_st, 1)
                    else:
                        for i in (0, 1):
                            src = bank(b)[:, i * 256:(i + 1) * 256].rearrange("p (four f) -> p four f", f=dv)[:, 0::3, :]
                            ins = nc.scalar.activation(O[:, 2 * b + i, :].rearrange("p (h f) -> p h f", f=dv), src, ACT.Copy)
                            if i:
                                ins.then_inc(o_st, 1)
                            else:
                                an_o.mark(ins)

            def take_root(g):
                act.wait_ge(dn.sem, 4 * g + 1)
                an.mark(nc.scalar.activation(root, ms, ACT.Sqrt))

            def store_turned(g):
                for b in range(nob * 2):
                    act.wait_ge(turned, nob * 2 * g + b + 1)
                    fb, half = b // 2, b % 2
                    nc.scalar.activation(k.oT[:, first_block + nob * g + fb, half * 512:(half + 1) * 512], bank(4 + b),
                                         ACT.Copy).then_inc(t_st, 1)

            for g in range(2):
                act.wait_ge(pre, g + 1)
                nc.scalar.activation(ke[:, :], ke[:, :], ACT.Exp).then_inc(eb, 1)
                if g:
                    act.wait_ge(rec, NT)
                nc.scalar.activation(dec, m.bT[:, g, :].rearrange("p (i t) -> p i t", t=P)[:, :, P - 1], ACT.Exp).then_inc(eb, 1)
                exponential(7 * g)
                act.wait_ge(zeroed, 4)
                if g:
                    act.wait_ge(level_q, 14)
                for hh in range(2):
                    nc.scalar.activation(qpad[:, hh, :], m.qT[:, g, :], ACT.Copy, scale=own[:, hh:hh + 1]).then_inc(padq, 1)
                exponential(7 * g + 1)
                for h in range(2):
                    act.wait_ge(kt_mm, 2 * g + h + 1)
                    nc.scalar.activation(ktok[:, 4 * h:4 * h + 4, :], bank(h).rearrange("p (i t) -> p i t", t=P),
                                         ACT.Copy).then_inc(kt_st, 1)
                act.wait_ge(diag, g + 1)
                nc.scalar.activation(qe[:, :], m.bT[:, g, :], ACT.Exp).then_inc(eb, 1)
                for l in range(2, 7):
                    exponential(7 * g + l)
                if g:
                    take_root(0)
                    store_turned(0)
                store_out(g)
            take_root(1)
            store_turned(1)

        @block.tensor
        def _(pe):
            def turn_out(g):
                pe.wait_ge(dn.sem, 4 * (g + 1))
                if g:
                    pe.wait_ge(t_st, nob * 2)
                for b in range(nob * 2):
                    fb, half = b // 2, b % 2
                    for i in range(4):
                        ins = nc.tensor.transpose(bank(4 + b)[:, i * P:(i + 1) * P], O[:, 4 * half + i, fb * P:(fb + 1) * P],
                                                  k.ident[:, :])
                    ins.then_inc(turned, 1)

            pe.wait_ge(zeroed, 4)
            for g in range(2):
                pe.wait_ge(kd, g + 1)
                if g:
                    pe.wait_ge(o_st, 4)
                for i in range(NT):
                    ins = nc.tensor.transpose(bank(i // 4)[:, (i % 4) * P:(i % 4 + 1) * P], ke[:, i * P:(i + 1) * P], k.ident[:, :])
                    if i % 4 == 3:
                        ins.then_inc(kt_mm, 1)
                pe.wait_ge(prod, g + 1)
                if g:
                    pe.wait_ge(picked, picks(8 * g - 2))
                d16 = bank(base(8 * g))[:, 0:16].rearrange("p (h i) -> p h i", i=NT)
                for i in range(NT):
                    ins = nc.tensor.matmul(d16[:, :, i], qe[:, i * P:(i + 1) * P], own, start=True, stop=True)
                ins.then_inc(diag, 1)
                for st in range(1, 8):
                    s, l = 8 * g + st, 7 * g + st - 1
                    pe.wait_ge(level_k, l + 1)
                    pe.wait_ge(level_q, 2 * (l + 1))
                    if s >= 2:
                        pe.wait_ge(picked, picks(s - 2))
                    for i in range(NT):
                        out = bank(base(s) + i // 4).rearrange("p (h i t) -> p h i t", h=2, i=4)[:, :, i % 4, :]
                        ins = nc.tensor.matmul(out, C[:, l % 2, i * P:(i + 1) * P], Q[:, l % 2, :, i * 64:(i + 1) * 64],
                                               start=True, stop=True)
                        if i % 4 == 3:
                            ins.then_inc(score, 1)
                    if st == 1:
                        pe.wait_ge(kt_st, 2 * g + 2)
                        for i in range(NT):
                            for hh in range(2):
                                c = i * dv
                                ins = nc.tensor.matmul(bank(2 + c // 512)[64 * hh:64 * hh + 64, c % 512:c % 512 + dv],
                                                       ktok[:, i, 64 * hh:64 * hh + 64],
                                                       m.v[:, i, (2 * g + hh) * dv:(2 * g + hh + 1) * dv], start=True, stop=True)
                        ins.then_inc(u_mm, 1)
                pe.wait_ge(picked, PICKS * (g + 1))
                if g:
                    turn_out(0)
                pe.wait_ge(rec, NT * (g + 1))
                pe.wait_ge(qd, g + 1)
                for i in range(NT):
                    if i:
                        c = (i % 2) * 256
                        nc.tensor.matmul(bank(i // 2)[:, c:c + 256], qe[:, i * P:(i + 1) * P], ST[:, i, :, :], start=True, stop=False)
                    for hh in range(2):
                        bk, c, _ = out_of(i, hh)
                        lo = (2 * g + hh) * dv if dv == P else 2 * g * dv
                        ins = nc.tensor.matmul(bk[:, c:c + P], S[:, hh, i, :], m.v[:, i, lo:lo + P], start=(i == 0),
                                               stop=(i == 0 or hh == 1))
                    if i % 2:
                        ins.then_inc(o_mm, 1)
            turn_out(1)

        @block.vector
        def _(dve):
            V = nc.vector

            def norm(g):
                v3 = lambda ap: ap.rearrange("p i (h v) -> p (i h) v", v=dv)
                dve.wait_ge(squares, 16 * (g + 1))
                dn.mark(V.tensor_scalar(ms, ssq, 1.0 / dv, EPS, ALU.mult, ALU.add))
                dve.wait_ge(an.sem, g + 1)
                dn.mark(V.reciprocal(rstd, root))
                dve.wait_ge(dn.sem, 4 * g + 2)
                dve.wait_ge(o_st, 4 * (g + 1))
                dn.mark(V.tensor_tensor(v3(O[:, :, :]), v3(O[:, :, :]), rstd.unsqueeze(2).to_broadcast([P, 16, dv]), ALU.mult))
                dve.wait_ge(dn.sem, 4 * g + 3)
                dve.wait_ge(gained, 1)
                dn.mark(V.tensor_tensor(O[:, :, :], O[:, :, :], m.g[:, :, 2 * g * dv:(2 * g + 2) * dv], ALU.mult))

            for g in range(2):
                b3 = m.bT[:, g, :].rearrange("p (i t) -> p i t", t=P)
                V.tensor_tensor(ke[:, :].rearrange("p (i t) -> p i t", t=P),
                                b3[:, :, P - 1:P].to_broadcast([P, NT, P]), b3, ALU.subtract).then_inc(pre, 1)

                def differences(l):
                    s, h = 7 * g + l, 1 << l
                    b4, e = halves(m.bT[:, g, :], h), halves(E[:, s % 2, :], h)
                    mid = b4[:, :, 0, h - 1:h].to_broadcast([P, T // (2 * h), h])
                    if s >= 2:
                        dve.wait_ge(level_q, 2 * (s - 1))
                        dve.wait_ge(level_k, s - 1)
                    V.tensor_tensor(e[:, :, 0, :], mid, b4[:, :, 0, :], ALU.subtract).then_inc(diff, 1)
                    V.tensor_tensor(e[:, :, 1, :], b4[:, :, 1, :], mid, ALU.subtract).then_inc(diff, 1)

                def keys(l):
                    s, h = 7 * g + l, 1 << l
                    dve.wait_ge(expd, s + 1)
                    if s >= 2:
                        dve.wait_ge(score, 2 * (s - 1))
                    V.tensor_tensor(halves(C[:, s % 2, :], h)[:, :, 0, :], halves(E[:, s % 2, :], h)[:, :, 0, :],
                                    halves(m.kT[:, g, :], h)[:, :, 0, :], ALU.mult).then_inc(level_k, 1)

                def pick(l):
                    h = 1 << l
                    s = 8 * g + l + 1
                    mask = halves(k.levels[:, l, :], h)[:, :, 1, :].bitcast(U32).unsqueeze(1).to_broadcast([P, 4, 64 // h, h])
                    dve.wait_ge(picked, picks(s - 1))
                    for half in range(2):
                        dve.wait_ge(score, 2 * (7 * g + l) + half + 1)
                        src = bank(base(s) + half).rearrange("p (hh i b h) -> p hh i b h", hh=2, i=4, h=h)
                        for hh in range(2):
                            dst = S[:, hh, 4 * half:4 * half + 4, :].rearrange("p i (b two h) -> p i b two h", two=2, h=h)
                            V.copy_predicated(dst[:, :, :, 1, :], mask, src[:, hh, :, :, :]).then_inc(picked, 1)

                def diagonal():
                    dve.wait_ge(diag, g + 1)
                    if g:
                        dve.wait_ge(o_mm, 4)
                    d16 = bank(base(8 * g))[:, 0:16].rearrange("p (h i) -> p h i", i=NT)
                    V.tensor_tensor(S[:, :, :, :], k.ident[:, :].unsqueeze(1).unsqueeze(1).to_broadcast([P, 2, NT, P]),
                                    d16.unsqueeze(3).to_broadcast([P, 2, NT, P]), ALU.mult).then_inc(picked, 1)

                def states():
                    dve.wait_ge(u_mm, g + 1)
                    dve.wait_ge(cleared, 2)
                    dve.wait_ge(eb, 3 * g + 2)
                    for i in range(NT - 1):
                        c = i * dv
                        if i:
                            dve.wait_ge(rec, NT * g + i)
                        for hh in range(2):
                            rows = slice(64 * hh, 64 * hh + 64)
                            u = k.banks[rows, 2 + c // 512, c % 512:c % 512 + dv]
                            if i == 0:
                                ins = V.tensor_copy(ST[rows, 1, slot * hh, :], u)
                            else:
                                ins = V.scalar_tensor_tensor(out=ST[rows, i + 1, slot * hh, :], in0=ST[rows, i, slot * hh, :],
                                                             scalar=dec[rows, i:i + 1], in1=u, op0=ALU.mult, op1=ALU.add)
                            if hh:
                                ins.then_inc(rec, 1)
                            else:
                                ins.then_inc(rec0, 1)
                        dve.wait_ge(rec0, (NT - 1) * g + i + 1)
                    V.memset(k.small[:, 78:79], 0.0).then_inc(rec, 1)

                differences(0)
                if g == 0:
                    for hh in range(2):
                        for rows in range(2):
                            V.memset(own[64 * rows:64 * rows + 64, hh:hh + 1], float(hh == rows)).then_inc(zeroed, 1)
                dve.wait_ge(eb, 3 * g + 1)
                V.tensor_tensor(ke[:, :], ke[:, :], m.kT[:, g, :], ALU.mult).then_inc(kd, 1)
                differences(1)
                dve.wait_ge(cleared, 1)
                keys(0)
                differences(2)
                diagonal()
                for l in range(1, 7):
                    keys(l)
                    if l <= 4:
                        differences(l + 2)
                    pick(l - 1)
                    if l == 2:
                        states()
                    if l == 4 and g:
                        norm(0)
                pick(6)
            norm(1)


def stage_stick_projection(nc, k):
    p = k.place
    k.sb_qT, k.sb_kT = p("sb_qT", [P, 2, T], 104), p("sb_kT", [P, 2, T], 112)
    k.sb_v, k.sb_gT = p("sb_v", [P, NT, 256], 120), p("sb_gT", [P, 2, T], 128)
    k.sb_k = p("sb_keys_padded", [P, 4, T], 192)
    padded = Steps(k, "sb_keys_padded")
    jobs = []
    for g in range(2):
        jobs += feature_jobs(k.c_qkc, g * P, k.sb_qT[:, g, :])
    for g in range(2):
        jobs += feature_jobs(k.c_qkc, 256 + g * P, k.sb_kT[:, g, :])
    jobs += token_jobs(k.c_vgc, 0, 256, lambda i: k.sb_v[:, i, :])
    for g in range(2):
        jobs += feature_jobs(k.c_vgc, 256 + g * P, k.sb_gT[:, g, :], "silu", "act")
    proj = Projection(nc, k, "stick_proj", jobs)
    with nc.Block() as block:
        @block.sync
        def _(sp):
            k.w.load_up_to(sp, k.c_out[1])

        @block.gpsimd
        def _(pool):
            pool.wait_ge(proj.stored["act"], 4)
            pool.wait_ge(proj.stored["dve"], 4)
            for g in range(2):
                pad_keys(pool, k.sb_k[:, 2 * g:2 * g + 2, :], lambda rows: k.sb_kT[rows, g, :], padded)

        @block.scalar
        def _(act):
            run_stores(nc, proj, act, "act")

        @block.tensor
        def _(pe):
            proj.pe_jobs(pe, 0, len(jobs))

        @block.vector
        def _(dve):
            run_stores(nc, proj, dve, "dve")


def stage_stick_attention(nc, k):
    p = k.place
    A = p("sb_rest", [P, 2, T], 136)
    B = p("sb_weight", [P, 2, T], 144)
    WT = p("sb_weightT", [P, 2, NT, P], 152)
    R = p("sb_rest_product", [P, T], 216)
    other = p("not_strict", [P, P], 6.5)
    ones = p("ones", [P, P], 220)
    items = [(i, h) for i in range(NT) for h in range(4)]
    N = len(items)
    nb = [2 if i >= 4 else 1 for i, h in items]
    upto = [sum(nb[:n + 1]) for n in range(N)]
    two = [sum(b == 2 for b in nb[:n + 1]) for n in range(N)]
    s = lambda n: k.sem("sb_" + n)
    z_mm, rest, taken, w_done = s("z"), s("rest"), s("taken"), s("w")
    t_mm, wt_act, wt_dve, pv, o_done = s("turned"), s("wT_act"), s("wT_dve"), s("out"), s("out_stored")
    d = Steps(k, "sb_dve")
    x_in = k.kept_sem("x_again")
    k.x_again = x_in
    k.xres = p("x_residual", [P, NT, D], 160)
    sc = DK ** -0.5

    def width(n):
        return (items[n][0] + 1) * P

    def z(n):
        return k.banks[:, 2 * (n % 2):2 * (n % 2) + 2, :].rearrange("p b c -> p (b c)")[:, 0:width(n)]

    with nc.Block() as block:
        @block.sync
        def _(sp):
            sp.dma_start(k.xres[:, :, :], k.x[0].rearrange("(i p) d -> p i d", p=P)).then_inc(x_in, 16)

        @block.scalar
        def _(act):
            def sigmoids(n):
                w = width(n)
                act.wait_ge(z_mm, n + 1)
                if n >= 2:
                    act.wait_ge(w_done, n - 1)
                    act.wait_ge(t_mm, upto[n - 2])
                nc.scalar.activation(A[:, n % 2, 0:w], z(n), ACT.Sigmoid, scale=-sc).then_inc(rest, 1)
                nc.scalar.activation(B[:, n % 2, 0:w], z(n), ACT.Sigmoid, scale=sc).then_inc(taken, 1)

            sigmoids(0)
            for n in range(N):
                if n + 1 < N:
                    sigmoids(n + 1)
                act.wait_ge(t_mm, (upto[n - 1] if n else 0) + 1)
                if n >= 2:
                    act.wait_ge(pv, n - 1)
                m = min(items[n][0] + 1, 4)
                nc.scalar.activation(WT[:, n % 2, 0:m, :], k.banks[:, 4, 0:m * P].rearrange("p (j t) -> p j t", t=P),
                                     ACT.Copy).then_inc(wt_act, 1)

        @block.tensor
        def _(pe):
            def scores(n):
                i, h = items[n]
                w = width(n)
                if n >= 2:
                    pe.wait_ge(taken, n - 1)
                for c in range(0, w, 512):
                    e = min(w, c + 512)
                    ins = nc.tensor.matmul(z(n)[:, c:e], k.sb_qT[:, h // 2, i * P:(i + 1) * P],
                                           k.sb_k[:, h, c:e], start=True, stop=True)
                ins.then_inc(z_mm, 1)

            def values(n):
                i, h = items[n]
                if n >= 2:
                    pe.wait_ge(o_done, n - 1)
                out = k.banks[64 * (h % 2):64 * (h % 2) + 64, 6 + n % 2, 0:P]
                for j in range(i + 1):
                    if j == 0:
                        pe.wait_ge(wt_act, n + 1)
                    if j == 4:
                        pe.wait_ge(wt_dve, two[n])
                    ins = nc.tensor.matmul(out, k.sb_v[:, j, h * 64:(h + 1) * 64], WT[:, n % 2, j, :],
                                           start=(j == 0), stop=(j == i))
                ins.then_inc(pv, 1)

            scores(0)
            scores(1)
            for n, (i, h) in enumerate(items):
                pe.wait_ge(w_done, n + 1)
                for j in range(i + 1):
                    if j == 0 and n:
                        pe.wait_ge(wt_act, n)
                    if j == 4 and two[n] > 1:
                        pe.wait_ge(wt_dve, two[n] - 1)
                    ins = nc.tensor.transpose(k.banks[:, 4 + j // 4, (j % 4) * P:(j % 4 + 1) * P],
                                              B[:, n % 2, j * P:(j + 1) * P], k.ident[:, :])
                    if j == min(i, 3) or j == i:
                        ins.then_inc(t_mm, 1)
                if n:
                    values(n - 1)
                if n + 2 < N:
                    scores(n + 2)
            values(N - 1)

        @block.vector
        def _(dve):
            d.mark(nc.vector.memset(ones[:, :], 1.0))
            c0 = d.mark(nc.vector.tensor_scalar(other[:, :], k.strict[:, :], -1.0, 1.0, ALU.mult, ALU.add))
            dve.wait_ge(d.sem, c0)

            def weights(n):
                w = width(n)
                a, b, r = A[:, n % 2, 0:w], B[:, n % 2, 0:w], R[:, 0:w]
                dve.wait_ge(rest, n + 1)
                c = d.mark(nc.vector.copy_predicated(a[:, w - P:w], other[:, :].bitcast(U32), ones[:, :]))
                dve.wait_ge(taken, n + 1)
                d.mark(nc.vector.tensor_tensor(b[:, w - P:w], b[:, w - P:w], k.strict[:, :], ALU.mult))
                dve.wait_ge(d.sem, c)
                d.mark(nc.vector.tensor_tensor_scan(r[:, ::-1], a[:, ::-1], a[:, ::-1], 1.0, ALU.mult, ALU.min))
                dve.wait_ge(d.sem, d.n)
                nc.vector.tensor_tensor(b[:, 0:w - 1], b[:, 0:w - 1], r[:, 1:w], ALU.mult).then_inc(w_done, 1)
                dve.wait_ge(w_done, n + 1)

            def turned_weights(n):
                if nb[n] == 2:
                    dve.wait_ge(t_mm, upto[n])
                    if two[n] > 2:
                        dve.wait_ge(pv, n - 1)
                    nc.vector.tensor_copy(WT[:, n % 2, 4:items[n][0] + 1, :],
                                          k.banks[:, 5, 0:(items[n][0] - 3) * P].rearrange("p (j t) -> p j t", t=P)).then_inc(wt_dve, 1)

            def store(n):
                i, h = items[n]
                dve.wait_ge(pv, n + 1)
                rows = slice(64 * (h % 2), 64 * (h % 2) + 64)
                tok = slice(i * P, (i + 1) * P)
                nc.vector.tensor_tensor(k.oT[rows, 6 + h // 2, tok], k.banks[rows, 6 + n % 2, 0:P],
                                        k.sb_gT[rows, h // 2, tok], ALU.mult).then_inc(o_done, 1)

            weights(0)
            for n, (i, h) in enumerate(items):
                if n + 1 < N:
                    weights(n + 1)
                turned_weights(n)
                if n:
                    store(n - 1)
            store(N - 1)


def stage_first_output(nc, k):
    p = k.place
    x = k.xres
    fnw = p("final_norm_row", [P, D], 104)
    tmp = p("gated_y", [P, 2, 512], 108)
    mixg = k.small[:, 160:168]
    sq1, ms1, rt1, rs1 = (k.small[:, c:c + 8] for c in (168, 176, 184, 192))
    jobs = [dict(chunk=k.c_out[h], kind="tokens", tile=i, col=0, width=512, by="dve", dest=h, how="gate")
            for i in range(NT) for h in range(2)]
    o_hi, o_lo = p("mixed_hi", [P, KB, T], 112, F32R), p("mixed_lo", [P, KB, T], 72, F32R)
    o_rounded, o_split = k.sem("mixed_rounded"), k.sem("mixed_split")
    parts = Parts(nc, k, "first_out", k.c_out, o_hi, o_lo, (144, 192), o_split)
    proj = Projection(nc, k, "first_out", jobs, banks=6, parts=parts)
    norm = NormTranspose(nc, k, "norm2", x, k.hT, p("x1_normed", [P, NT, D], 112))
    s = lambda n: k.sem(n)
    vec_in, added, summed, gained, x1_done = s("fnw_in"), s("residual_added"), s("x1_summed"), s("hT_gained"), s("x1_done")
    x1_out, rounded = k.sem("x1_out"), k.sem("n_rounded")
    k.n_hi = p("normed_hi", [P, KB, T], 128, F32R)
    k.n_lo = p("normed_lo", [P, KB, T], 40, F32R)
    d = Steps(k, "first_out_dve")
    a = Steps(k, "first_out_act")
    with nc.Block() as block:
        @block.sync
        def _(sp):
            sp.wait_ge(x1_done, NT)
            sp.dma_start(k.x1_dram.rearrange("(i p) d -> p i d", p=P), x[:, :, :]).then_inc(x1_out, 16)
            k.w.load_up_to(sp, k.c_akv)
            sp.wait_ge(x1_out, 16)

        @block.gpsimd
        def _(pool):
            for i in range(NT):
                tok = slice(i * P, (i + 1) * P)
                pool.tensor_copy(o_hi[:, :, tok], k.oT[:, :, tok]).then_inc(o_rounded, 1)
            pool.wait_ge(k.x_again, 16)
            for j, job in enumerate(jobs):
                i, h = job["tile"], job["dest"]
                pool.wait_ge(proj.stored["dve"], j + 1)
                xs = x[:, i, h * 512:(h + 1) * 512]
                pool.tensor_tensor(xs, xs, tmp[:, j % 2, :], ALU.add).then_inc(added, 1)

        @block.scalar
        def _(act):
            act.dma_start(fnw[:, :], k.final_norm_w.partition_broadcast(P)).then_inc(vec_in, 16)
            act.dma_start(mixg, k.norm_mix_g_2[0].rearrange("(k p) -> p k", p=P), allow_slow_non_contiguous=True).then_inc(vec_in, 16)
            for h in range(2):
                parts.split_act(act, k.c_out[h])
            for i in range(NT):
                act.wait_ge(added, 2 * i + 2)
                nc.scalar.activation(k.hT[:, i, :], x[:, i, :], ACT.Square, accum_out=sq1[:, i:i + 1]).then_inc(summed, 1)
            act.wait_ge(d.sem, 1)
            a.mark(nc.scalar.activation(rt1, ms1, ACT.Sqrt))
            act.wait_ge(summed, NT)
            norm.act_stats(act, lambda e, i: e.wait_ge(x1_done, i + 1))
            norm.store(act, 0)
            act.wait_ge(norm.by_act, NT)
            act.wait_ge(norm.by_dve, NT)
            for b in range(KB):
                nc.scalar.activation(k.n_hi[:, b, :], k.hT[:, b, :], ACT.Copy, scale=mixg[:, b:b + 1]).then_inc(rounded, 1)

        @block.tensor
        def _(pe):
            proj.pe_jobs(pe, 0, len(jobs))
            pe.wait_ge(proj.stored["dve"], len(jobs))
            norm.pe_transpose(pe)

        @block.vector
        def _(dve):
            def rest_of_mixed(i):
                tok = slice(i * P, (i + 1) * P)
                dve.wait_ge(o_rounded, i + 1)
                nc.vector.tensor_tensor(o_lo[:, :, tok], k.oT[:, :, tok], o_hi[:, :, tok], ALU.subtract).then_inc(o_split, 1)

            rest_of_mixed(0)
            for h in range(2):
                parts.split_dve(dve, k.c_out[h])
            rest_of_mixed(1)
            for j, job in enumerate(jobs):
                if j % 2 == 0 and j // 2 + 2 < NT:
                    rest_of_mixed(j // 2 + 2)
                dve.wait_ge(proj.done, j + 1)
                if j >= 2:
                    dve.wait_ge(added, j - 1)
                h = job["dest"]
                nc.vector.tensor_tensor(tmp[:, j % 2, :], proj.bank(j), k.gate_row[:, h * 512:(h + 1) * 512],
                                        ALU.mult).then_inc(proj.stored["dve"], 1)
            dve.wait_ge(summed, NT)
            d.mark(nc.vector.tensor_scalar(ms1, sq1, 1.0 / D, EPS, ALU.mult, ALU.add))
            dve.wait_ge(a.sem, 1)
            n = d.mark(nc.vector.reciprocal(rs1, rt1))
            dve.wait_ge(d.sem, n)
            dve.wait_ge(vec_in, 32)
            dve.wait_ge(added, 16)
            for i in range(NT):
                nc.vector.scalar_tensor_tensor(out=x[:, i, :], in0=x[:, i, :], scalar=rs1[:, i:i + 1], in1=fnw[:, :],
                                               op0=ALU.mult, op1=ALU.mult).then_inc(x1_done, 1)
            norm.dve_stats(dve)
            norm.dve_divide(dve)
            norm.store(dve, 1)
            dve.wait_ge(norm.by_act, NT)
            dve.wait_ge(norm.by_dve, NT)
            for b in range(KB):
                dve.wait_ge(rounded, b + 1)
                nc.vector.scalar_tensor_tensor(out=k.n_lo[:, b, :], in0=k.hT[:, b, :], scalar=mixg[:, b:b + 1],
                                               in1=k.n_hi[:, b, :], op0=ALU.mult, op1=ALU.subtract).then_inc(gained, 1)


def rope_dve(nc, dve, d, x1, x2, cos, sin, t):
    V = nc.vector
    d.mark(V.tensor_tensor(t[0], x1, cos, ALU.mult))
    d.mark(V.tensor_tensor(t[1], x2, sin, ALU.mult))
    d.mark(V.tensor_tensor(t[2], x1, sin, ALU.mult))
    n = d.mark(V.tensor_tensor(t[3], x2, cos, ALU.mult))
    dve.wait_ge(d.sem, n)
    d.mark(V.tensor_tensor(x1, t[0], t[1], ALU.subtract))
    return d.mark(V.tensor_tensor(x2, t[2], t[3], ALU.add))


def stage_second_projection(nc, k):
    p = k.place
    aq = p("aq_tok", [P, NT, 512], 72)
    k.akv = p("akv_tok", [P, NT, 256], 88)
    iq = p("iq_tok", [P, NT, 512], 96)
    mix = p("mix_tok", [P, NT, GTA - IK], 112)
    k.cos, k.sin = p("cos_table", [P, NT, 24], 0.5), p("sin_table", [P, NT, 24], 1.25)
    k.aqT, k.iqT = p("aqT", [P, 4, T], 129), p("iqT", [P, 4, T], 145)
    k.akT, k.ikT = p("akT", [P, 2, T], 161), p("ikT", [P, T], 169)
    k.cqT, k.ckvT, k.krT = p("cqT", [P, 2, T], 173), p("ckvT", [P, T], 181), p("krT", [P, T], 185)
    sq = p("mix_squares", [P, NT, 456], 189)
    t4 = p("rope_products", [P, 4, 512], 203.5)
    ik2 = p("ik_twice", [P, NT, P], 211.5)
    ak4 = p("ak_twice", [P, NT, 256], 189)
    sm = k.small
    k.posq, k.iw = p("pos_col", [P, NT], 7), p("iw", [P, NT, 8], 7.0625)
    posi = sm[:, 200:208].bitcast(I32)
    inv = p("inv_freq", [P, 24], 7.375)
    ikg = p("ik_gain", [P, 64], 7.5)
    qg, kvg = sm[:, 208:210], sm[:, 210:211]
    ms, rt, rs = p("mix_mean", [P, 3, NT], 7.875), p("mix_root", [P, 3, NT], 6.0), p("mix_rstd", [P, 3, NT], 6.125)
    r, turns, ab, angv = (t4[:, c, 0:192].rearrange("p (i f) -> p i f", i=NT) for c in range(4))
    c_ik, c_iw, c_cq, c_ckv, c_kr = 0, IW - IK, CQ - IK, CKV - IK, KR - IK
    jobs = token_jobs(k.c_aq, 0, 512, lambda i: aq[:, i, :], 64 ** -0.5)
    jobs += token_jobs(k.c_akv, 0, 256, lambda i: k.akv[:, i, :])
    jobs += token_jobs(k.c_iq, 0, 512, lambda i: iq[:, i, :], 64 ** -0.5)
    jobs += token_jobs(k.c_mix, 0, GTA - IK, lambda i: mix[:, i, :])
    parts = Parts(nc, k, "second", [k.c_aq, k.c_akv, k.c_iq, k.c_mix], k.n_hi, k.n_lo, (161, 177))
    proj = Projection(nc, k, "second_proj", jobs, parts=parts)
    restored = k.sem("hT_restored")
    s = lambda n: k.sem(n)
    vec_in, table, rooted, copies, turned = s("second_vec_in"), s("angles"), s("mix_rooted"), s("twice"), s("heads_turned")
    by_act, by_dve, ready = s("heads_act"), s("heads_dve"), s("heads_ready")
    d = Steps(k, "second_dve")
    pl = Steps(k, "second_pool")
    C1 = 6.28125
    C2 = float(np.float32(np.round((2 * math.pi - C1) * 2 ** 20) / 2 ** 20))
    C3 = float(np.float32(2 * math.pi - C1 - C2))
    MAGIC = 1.5 * 2 ** 23
    freq = [float(THETA ** (-np.float32(2 * j) / np.float32(16))) for j in range(8)]
    freq += [float(THETA ** (-np.float32(2 * j) / np.float32(32))) for j in range(16)]

    with nc.Block() as block:
        @block.sync
        def _(sp):
            k.w.load_up_to(sp, k.c_gate[1])

        @block.gpsimd
        def _(pool):
            for f, v in enumerate(freq):
                pool.memset(inv[:, f:f + 1], v).then_inc(pl.sem, 1)
            pool.wait_ge(proj.done, len(jobs))
            for b in range(KB):
                pool.tensor_tensor(k.hT[:, b, :], k.n_hi[:, b, :], k.n_lo[:, b, :], ALU.add).then_inc(restored, 1)

        @block.scalar
        def _(act):
            slow = dict(allow_slow_non_contiguous=True)
            act.dma_start(posi, k.positions_2[0].rearrange("(i p) -> p i", p=P), **slow).then_inc(vec_in, 16)
            act.dma_start(ikg[:, :], k.idx_k_norm_g_2[0].partition_broadcast(P)).then_inc(vec_in, 16)
            act.dma_start(qg, k.q_a_norm_g_2[0].rearrange("(k p) -> p k", p=P), **slow).then_inc(vec_in, 16)
            act.dma_start(kvg, k.kv_a_norm_g_2[0].rearrange("(k p) -> p k", p=P), **slow).then_inc(vec_in, 16)
            parts.split_act(act, k.c_aq)
            parts.split_act(act, k.c_akv)
            run_stores_range(nc, proj, act, "act", 0, 8)
            act.wait_ge(table, 1)
            nc.scalar.activation(k.sin[:, :, :], r, ACT.Sin).then_inc(rooted, 1)
            nc.scalar.activation(k.cos[:, :, :], ab, ACT.Sin).then_inc(rooted, 1)
            parts.split_act(act, k.c_iq)
            run_stores_range(nc, proj, act, "act", 8, 16)
            parts.split_act(act, k.c_mix)
            run_stores_range(nc, proj, act, "act", 16, len(jobs))
            act.wait_ge(table, 2)
            nc.scalar.activation(rt[:, :, :], ms[:, :, :], ACT.Sqrt).then_inc(rooted, 1)
            act.wait_ge(ready, 1)
            for c in range(2):
                nc.scalar.activation(ik2[:, :, c * 64:c * 64 + 64], mix[:, :, 0:64], ACT.Copy).then_inc(copies, 1)
            act.wait_ge(ready, 2)
            for g in range(2):
                for c in range(2):
                    nc.scalar.activation(ak4[:, :, g * P + c * 64:g * P + c * 64 + 64], k.akv[:, :, g * 64:(g + 1) * 64],
                                         ACT.Copy).then_inc(copies, 1)
            act.wait_ge(restored, KB)
            for i in range(NT):
                tok = slice(i * P, (i + 1) * P)
                act.wait_ge(turned, 4 * i + 1)
                nc.scalar.activation(k.aqT[:, :, tok], k.banks[:, 4 * (i % 2), :].rearrange("p (b t) -> p b t", t=P),
                                     ACT.Copy).then_inc(by_act, 1)
                act.wait_ge(turned, 4 * i + 3)
                bk = k.banks[:, 4 * (i % 2) + 2, :].rearrange("p (b t) -> p b t", t=P)
                nc.scalar.activation(k.akT[:, :, tok], bk[:, 0:2, :], ACT.Copy).then_inc(by_act, 1)
                for b in range(2):
                    nc.scalar.activation(k.cqT[:, b, tok], bk[:, 2 + b, :], ACT.Copy, scale=1.0).then_inc(by_act, 1)

        @block.tensor
        def _(pe):
            proj.pe_jobs(pe, 0, len(jobs))
            pe.wait_ge(proj.stored["act"], proj.count["act"])
            pe.wait_ge(proj.stored["dve"], proj.count["dve"])
            pe.wait_ge(ready, 4)
            pe.wait_ge(copies, 6)
            tr = lambda bank, slot, src, w=P: nc.tensor.transpose(k.banks[0:w, bank, slot * P:(slot + 1) * P], src, k.ident[:, :])
            for i in range(NT):
                base = 4 * (i % 2)
                if i >= 2:
                    pe.wait_ge(by_act, 4 * (i - 1))
                    pe.wait_ge(by_dve, 4 * (i - 1))
                for b in range(4):
                    ins = tr(base, b, aq[:, i, b * P:(b + 1) * P])
                ins.then_inc(turned, 1)
                for b in range(4):
                    ins = tr(base + 1, b, iq[:, i, b * P:(b + 1) * P])
                ins.then_inc(turned, 1)
                for b in range(2):
                    tr(base + 2, b, ak4[:, i, b * P:(b + 1) * P])
                for b in range(2):
                    ins = tr(base + 2, 2 + b, mix[:, i, c_cq + b * P:c_cq + (b + 1) * P])
                ins.then_inc(turned, 1)
                tr(base + 3, 0, ik2[:, i, :])
                tr(base + 3, 1, mix[:, i, c_ckv:c_ckv + P])
                ins = tr(base + 3, 2, mix[:, i, c_kr - 64:c_kr + 32], 96)
                ins.then_inc(turned, 1)

        @block.vector
        def _(dve):
            V = nc.vector
            parts.split_dve(dve, k.c_aq)
            parts.split_dve(dve, k.c_akv)
            run_stores_range(nc, proj, dve, "dve", 0, 8)
            dve.wait_ge(vec_in, 64)
            d.mark(V.tensor_copy(k.posq[:, :], posi))
            dve.wait_ge(d.sem, d.n)
            dve.wait_ge(pl.sem, 24)
            d.mark(V.tensor_tensor(angv, k.posq[:, :].unsqueeze(2).to_broadcast([P, NT, 24]),
                                   inv[:, :].unsqueeze(1).to_broadcast([P, NT, 24]), ALU.mult))
            dve.wait_ge(d.sem, d.n)
            d.mark(V.tensor_scalar(turns, angv, 1.0 / (2 * math.pi), None, ALU.mult))
            dve.wait_ge(d.sem, d.n)
            d.mark(V.tensor_scalar(turns, turns, MAGIC, None, ALU.add))
            dve.wait_ge(d.sem, d.n)
            d.mark(V.tensor_scalar(turns, turns, MAGIC, None, ALU.subtract))
            src = angv
            for c in (C1, C2, C3):
                dve.wait_ge(d.sem, d.n)
                d.mark(V.scalar_tensor_tensor(out=r, in0=turns, scalar=-c, in1=src, op0=ALU.mult, op1=ALU.add))
                src = r
            dve.wait_ge(d.sem, d.n)
            d.mark(V.tensor_scalar(r, r, 3.1415925, -3.1415925, ALU.min, ALU.max))
            dve.wait_ge(d.sem, d.n)
            d.mark(V.scalar_tensor_tensor(out=ab, in0=r, scalar=-1.0, in1=r, op0=ALU.mult, op1=ALU.min))
            dve.wait_ge(d.sem, d.n)
            V.tensor_scalar(ab, ab, math.pi / 2, None, ALU.add).then_inc(table, 1)
            parts.split_dve(dve, k.c_iq)
            run_stores_range(nc, proj, dve, "dve", 8, 16)
            parts.split_dve(dve, k.c_mix)
            run_stores_range(nc, proj, dve, "dve", 16, len(jobs))
            for e in ("act", "dve"):
                dve.wait_ge(proj.stored[e], proj.count[e])
            cols = [(c_ik, 64), (c_cq, 256), (c_ckv, P)]
            at = [0, 64, 320]
            for n, (c, w) in enumerate(cols):
                d.mark(V.tensor_tensor(sq[:, :, at[n]:at[n] + w], mix[:, :, c:c + w], mix[:, :, c:c + w], ALU.mult))
            dve.wait_ge(d.sem, d.n)
            for n, (c, w) in enumerate(cols):
                d.mark(V.tensor_reduce(ms[:, n, :], sq[:, :, at[n]:at[n] + w], AX.X, ALU.add))
            dve.wait_ge(d.sem, d.n)
            for n, (c, w) in enumerate(cols):
                ins = V.tensor_scalar(ms[:, n, :], ms[:, n, :], 1.0 / w, EPS, ALU.mult, ALU.add)
                d.mark(ins)
            dve.wait_ge(d.sem, d.n)
            V.memset(sm[:, 79:80], 0.0).then_inc(table, 1)
            dve.wait_ge(rooted, 3)
            d.mark(V.reciprocal(rs[:, :, :], rt[:, :, :]))
            dve.wait_ge(d.sem, d.n)
            for n, (c, w) in enumerate(cols):
                d.mark(V.tensor_tensor(mix[:, :, c:c + w], mix[:, :, c:c + w], rs[:, n, :].unsqueeze(2).to_broadcast([P, NT, w]),
                                       ALU.mult))
            dve.wait_ge(d.sem, d.n)
            d.mark(V.tensor_tensor(mix[:, :, 0:64], mix[:, :, 0:64], ikg[:, :].unsqueeze(1).to_broadcast([P, NT, 64]), ALU.mult))
            d.mark(V.tensor_scalar(k.iw[:, :, :], mix[:, :, c_iw:c_iw + 8], float(np.float32(8 ** -0.5)), None, ALU.mult))
            dve.wait_ge(d.sem, d.n)

            def rope(x, heads, half, f0):
                t = [t4[:, c, 0:NT * heads * half].rearrange("p (i h f) -> p i h f", i=NT, h=heads) for c in range(4)]
                tab = [a[:, :, f0:f0 + half].unsqueeze(2).to_broadcast([P, NT, heads, half]) for a in (k.cos, k.sin)]
                rope_dve(nc, dve, d, x[:, :, :, 0:half], x[:, :, :, half:2 * half], tab[0], tab[1], t)
                dve.wait_ge(d.sem, d.n)

            heads = lambda a, w: a.rearrange("p i (h f) -> p i h f", f=w)
            rope(heads(mix[:, :, 0:64], 64), 1, 8, 0)
            V.memset(sm[:, 79:80], 0.0).then_inc(ready, 1)
            dve.wait_ge(ready, 1)
            rope(heads(k.akv[:, :, 0:128], 64), 2, 8, 0)
            V.memset(sm[:, 79:80], 0.0).then_inc(ready, 1)
            rope(heads(mix[:, :, c_kr:c_kr + 32], 32), 1, 16, 8)
            rope(heads(iq[:, :, :], 64), 8, 8, 0)
            dve.wait_ge(ready, 2)
            V.memset(sm[:, 79:80], 0.0).then_inc(ready, 1)
            rope(heads(aq[:, :, :], 64), 8, 8, 0)
            dve.wait_ge(ready, 3)
            V.memset(sm[:, 79:80], 0.0).then_inc(ready, 1)
            dve.wait_ge(restored, KB)
            for i in range(NT):
                tok = slice(i * P, (i + 1) * P)
                dve.wait_ge(turned, 4 * i + 2)
                V.tensor_copy(k.iqT[:, :, tok], k.banks[:, 4 * (i % 2) + 1, :].rearrange("p (b t) -> p b t", t=P)).then_inc(by_dve, 1)
                dve.wait_ge(turned, 4 * i + 4)
                bk = k.banks[:, 4 * (i % 2) + 3, :]
                V.tensor_copy(k.ikT[:, tok], bk[:, 0:P]).then_inc(by_dve, 1)
                V.tensor_scalar(k.ckvT[:, tok], bk[:, P:2 * P], kvg[:, 0:1], None, ALU.mult).then_inc(by_dve, 1)
                V.tensor_copy(k.krT[64:96, tok], bk[64:96, 2 * P:3 * P]).then_inc(by_dve, 1)
            dve.wait_ge(by_act, 4 * NT)
            for b in range(2):
                d.mark(V.tensor_scalar(k.cqT[:, b, :], k.cqT[:, b, :], qg[:, b:b + 1], None, ALU.mult))


def pad_keys(pool, out, keys, padded):
    for half in range(2):
        own, other = slice(64 * half, 64 * half + 64), slice(64 - 64 * half, 128 - 64 * half)
        pool.wait_ge(padded.sem, padded.mark(pool.memset(out[other, half, :], 0.0)))
        pool.wait_ge(padded.sem, padded.mark(pool.tensor_copy(out[own, half, :], keys(own))))


def stage_index_scores(nc, k):
    p = k.place
    k.isc = p("index_scores", [P, NT, T], 189)
    k.posrow = p("pos_row", [P, T], 125)
    R = p("index_relu", [P, 2, T], 96)
    posi = p("pos_row_int", [P, T], 120, I32)
    k_hi, k_lo = p("index_keys_hi", [P, 2, T], 112, F32R), p("index_keys_lo", [P, 2, T], 104, F32R)
    q_hi, q_lo = p("index_queries_hi", [P, 4, T], 72, F32R), p("index_queries_lo", [P, 4, T], 145, F32R)
    s = lambda n: k.sem("idx_" + n)
    pos_in, mm, relu, base, acc = s("pos_in"), s("product"), s("relu"), s("base"), s("sum")
    zeroed, keys_hi, keys_lo, queries_hi, queries_lo = (s(n) for n in ("zeroed", "keys_hi", "keys_lo", "queries_hi", "queries_lo"))
    items = [(i, h) for i in range(NT) for h in range(8)]
    pair = lambda n: k.banks[:, 2 * (n % 4):2 * (n % 4) + 2, :].rearrange("p b c -> p (b c)")
    with nc.Block() as block:
        @block.gpsimd
        def _(pool):
            for c in range(2):
                for part in (k_hi, k_lo):
                    pool.memset(part[64 - 64 * c:128 - 64 * c, c, :].bitcast(F32), 0.0).then_inc(zeroed, 1)

        @block.scalar
        def _(act):
            act.dma_start(posi[:, :], k.positions_2[0].partition_broadcast(P)).then_inc(pos_in, 16)

            def round_queries(i):
                tok = slice(i * P, (i + 1) * P)
                nc.scalar.activation(q_hi[:, :, tok], k.iqT[:, :, tok], ACT.Copy).then_inc(queries_hi, 1)

            round_queries(0)
            for c in range(2):
                rows = slice(64 * c, 64 * c + 64)
                nc.scalar.activation(k_hi[rows, c, :], k.ikT[rows, :], ACT.Copy).then_inc(keys_hi, 1)
            for n, (i, h) in enumerate(items):
                if h == 0 and i + 1 < NT:
                    round_queries(i + 1)
                act.wait_ge(mm, n + 1)
                if n >= 2:
                    act.wait_ge(acc, n - 1)
                nc.scalar.activation(R[:, n % 2, :], pair(n), ACT.Relu).then_inc(relu, 1)

        @block.tensor
        def _(pe):
            pe.wait_ge(zeroed, 4)
            for n, (i, h) in enumerate(items):
                if n < 2:
                    pe.wait_ge(keys_lo, n + 1)
                if h == 0:
                    pe.wait_ge(queries_lo, i + 1)
                if n >= 4:
                    pe.wait_ge(relu, n - 3)
                tok = slice(i * P, (i + 1) * P)
                for c in range(2):
                    cols = slice(c * 512, (c + 1) * 512)
                    ins = products_of_parts(nc, pair(n)[:, cols], q_hi[:, h // 2, tok], q_lo[:, h // 2, tok],
                                            k_hi[:, h % 2, cols], k_lo[:, h % 2, cols], True, True)
                ins.then_inc(mm, 1)

        @block.vector
        def _(dve):
            def rest_of_queries(i):
                tok = slice(i * P, (i + 1) * P)
                dve.wait_ge(queries_hi, i + 1)
                nc.vector.tensor_tensor(q_lo[:, :, tok], k.iqT[:, :, tok], q_hi[:, :, tok], ALU.subtract).then_inc(queries_lo, 1)

            rest_of_queries(0)
            for c in range(2):
                rows = slice(64 * c, 64 * c + 64)
                dve.wait_ge(keys_hi, c + 1)
                nc.vector.tensor_tensor(k_lo[rows, c, :], k.ikT[rows, :], k_hi[rows, c, :], ALU.subtract).then_inc(keys_lo, 1)
            dve.wait_ge(pos_in, 16)
            nc.vector.tensor_copy(k.posrow[:, :], posi[:, :]).then_inc(base, 1)
            dve.wait_ge(base, 1)
            for i in range(NT):
                nc.vector.tensor_scalar(k.isc[:, i, :], k.posrow[:, :], k.posq[:, i:i + 1], MASKED, ALU.is_gt,
                                        ALU.mult).then_inc(base, 1)
            for n, (i, h) in enumerate(items):
                if h == 0 and i + 1 < NT:
                    rest_of_queries(i + 1)
                dve.wait_ge(relu, n + 1)
                if h == 0:
                    dve.wait_ge(base, i + 2)
                else:
                    dve.wait_ge(acc, n)
                nc.vector.scalar_tensor_tensor(out=k.isc[:, i, :], in0=R[:, n % 2, :], scalar=k.iw[:, i, h:h + 1],
                                               in1=k.isc[:, i, :], op0=ALU.mult, op1=ALU.add).then_inc(acc, 1)


def stage_select(nc, k):
    p = k.place
    V = nc.vector
    SPLIT = 4
    BIG = 3e38
    junk = p("count_scratch", [P, 2, T], 96)
    junk_act = p("sign_scratch", [P, T], 104)
    Q, RK = (p(n, [P, T], at) for n, at in (("equal", 108), ("rank", 112)))
    G = p("excluded", [P, 2, T], 161)
    stage = p("gate_stage", [P, 4, 512], 116)
    ints = p("threshold_bits", [P, 4, NT], 6.25, I32)
    best, cand, took = (ints[:, c, :] for c in range(3))
    thr = best.bitcast(F32)
    cnt = k.small[:, 216:224]
    left = k.small[:, 224:232]
    least = k.small[:, 240:248]
    jobs = []
    for c in range(16):
        jobs += feature_jobs(k.c_gate[c // 4], (c % 4) * P, None, "sigmoid", "act")
    proj = Projection(nc, k, "gates", jobs)
    d = Steps(k, "select_dve")
    cs = Steps(k, "select_count")
    tried, signs = k.sem("candidate"), k.sem("signs_summed")
    padded = Steps(k, "sparse_keys_padded")
    k.ak_pad = p("sparse_keys_padded", [P, 4, T], 145)
    left_out, biased = k.sem("left_out"), k.sem("bias_done")
    gate_out = [k.sem(f"gate_out_{i}") for i in range(4)]
    with nc.Block() as block:
        @block.sync
        def _(sp):
            for j, job in enumerate(jobs):
                if j % 8 == 0:
                    k.w.load_up_to(sp, k.c_gate[0] + j // 8 + 1)
                sp.wait_ge(proj.stored["act"], j + 1)
                sp.dma_start(k.gate_dram[j // 2, :, (j % 2) * 512:(j % 2 + 1) * 512], stage[:, j % 4, :]).then_inc(gate_out[j % 4], 16)
            k.w.load_up_to(sp, k.c_bb)
            for g in gate_out:
                sp.wait_ge(g, 16 * len(jobs) // 4)

        @block.gpsimd
        def _(pool):
            for g in range(2):
                pad_keys(pool, k.ak_pad[:, 2 * g:2 * g + 2, :], lambda rows: k.akT[rows, g, :], padded)

        @block.scalar
        def _(act):
            def gate(j):
                act.wait_ge(proj.done, j + 1)
                if j >= 4:
                    act.wait_ge(gate_out[j % 4], 16 * (j // 4))
                nc.scalar.activation(stage[:, j % 4, :], proj.bank(j), ACT.Sigmoid).then_inc(proj.stored["act"], 1)

            for bit in range(32):
                act.wait_ge(tried, bit + 1)
                for i in range(SPLIT, NT):
                    if bit or i > SPLIT:
                        act.wait_ge(signs, (NT - SPLIT) * bit + i - SPLIT)
                    nc.scalar.activation(junk_act[:, :], k.isc[:, i, :], ACT.Sign, scale=-1.0, bias=cand.bitcast(F32)[:, i:i + 1],
                                         accum_out=cnt[:, i:i + 1]).then_inc(signs, 1)
                for j in range(4 * bit // 5, 4 * (bit + 1) // 5):
                    gate(j)
            for j in range(4 * 32 // 5, len(jobs) - 3):
                gate(j)
            for i in range(NT):
                if i < 3:
                    gate(len(jobs) - 3 + i)
                act.wait_ge(left_out, i + 1)
                nc.scalar.activation(k.isc[:, i, :], G[:, i % 2, :], ACT.Copy, scale=MASKED).then_inc(biased, 1)

        @block.tensor
        def _(pe):
            proj.pe_jobs(pe, 0, len(jobs))

        @block.vector
        def _(dve):
            def step(ins):
                d.mark(ins)
                dve.wait_ge(d.sem, d.n)

            top = -2 ** 31
            for n, bit in enumerate(range(31, -1, -1)):
                if n == 0:
                    V.memset(cand, 0).then_inc(tried, 1)
                else:
                    V.tensor_scalar(cand, best, 1 << bit, None, ALU.bitwise_xor).then_inc(tried, 1)
                dve.wait_ge(tried, n + 1)
                for i in range(SPLIT):
                    if cs.n >= 2:
                        dve.wait_ge(cs.sem, cs.n - 1)
                    cs.mark(V.tensor_scalar(junk[:, i % 2, :], k.isc[:, i, :], cand.bitcast(F32)[:, i:i + 1], 0.0, ALU.is_ge, ALU.add,
                                            accum_out=cnt[:, i:i + 1]))
                dve.wait_ge(cs.sem, cs.n)
                dve.wait_ge(signs, (NT - SPLIT) * (n + 1))
                d.mark(V.tensor_scalar(took[:, 0:SPLIT], cnt[:, 0:SPLIT], float(TOPK), None, ALU.is_ge))
                step(V.tensor_scalar(took[:, SPLIT:NT], cnt[:, SPLIT:NT], float(T - 2 * TOPK), None, ALU.is_le))
                if n == 0:
                    step(V.tensor_scalar(best, took, 1.0, None, ALU.subtract))
                else:
                    step(V.copy_predicated(best, took.bitcast(U32), cand))
            for i in range(SPLIT, NT):
                x, t = k.isc[:, i, :], thr[:, i:i + 1]
                step(V.tensor_scalar(junk[:, 0, :], x, t, 0.0, ALU.is_gt, ALU.add, accum_out=cnt[:, i:i + 1]))
                step(V.tensor_scalar(junk[:, 0, :], x, t, BIG, ALU.is_le, ALU.mult))
                step(V.tensor_tensor_reduce(junk[:, 1, :], junk[:, 0, :], x, 1.0, BIG, ALU.add, ALU.min, least[:, i:i + 1]))
            step(V.tensor_scalar(took[:, SPLIT:NT], cnt[:, SPLIT:NT], float(TOPK), None, ALU.is_ge))
            step(V.copy_predicated(best[:, SPLIT:NT], took[:, SPLIT:NT].bitcast(U32), least[:, SPLIT:NT].bitcast(I32)))
            step(V.tensor_scalar(thr, thr, MASKED / 2, None, ALU.max))
            dve.wait_ge(padded.sem, 8)
            for i in range(NT):
                x, t, c = k.isc[:, i, :], thr[:, i:i + 1], i % 2
                d.mark(V.tensor_scalar(junk[:, 0, :], x, t, 0.0, ALU.is_gt, ALU.add, accum_out=cnt[:, i:i + 1]))
                step(V.tensor_scalar(Q[:, :], x, t, None, ALU.is_equal))
                d.mark(V.tensor_scalar(left[:, i:i + 1], cnt[:, i:i + 1], -1.0, float(TOPK), ALU.mult, ALU.add))
                step(V.tensor_tensor_scan(RK[:, :], Q[:, :], Q[:, :], 0.0, ALU.add, ALU.max))
                if i >= 2:
                    dve.wait_ge(biased, i - 1)
                step(V.scalar_tensor_tensor(out=G[:, c, :], in0=RK[:, :], scalar=left[:, i:i + 1], in1=Q[:, :],
                                            op0=ALU.is_gt, op1=ALU.mult))
                V.scalar_tensor_tensor(out=G[:, c, :], in0=x, scalar=t, in1=G[:, c, :], op0=ALU.is_lt,
                                       op1=ALU.add).then_inc(left_out, 1)
            dve.wait_ge(biased, NT)


def attention(nc, k, name, q, kk, v, bias, scale, oT, at, at_turned):
    p = k.place
    L = p(f"{name}_logits", [P, 2, T], at)
    E = p(f"{name}_probs", [P, 2, T], at + 8)
    ET = [p(f"{name}_probsT_{c}", [P, 2, NT, P], at_turned[c]) for c in range(2)]
    wide = p(f"{name}_inverse_wide", [P, 2, 512], at + 16)
    spread = p(f"{name}_inverse_spread", [P, 2, 512], at + 20)
    low = p(f"{name}_minus_max", [P, NT * 8], at + 28)
    tot = p(f"{name}_total", [P, NT * 8], at + 28.25)
    inv = p(f"{name}_inverse", [P, NT * 8], at + 28.5)
    items = [(i, h) for i in range(NT) for h in range(8)]
    N = len(items)
    s = lambda n: k.sem(f"{name}_{n}")
    mm, logit, prob, turned = s("scores"), s("logits"), s("probs"), s("probs_turned")
    t_act, t_dve, pv, invd, wided = s("pT_act"), s("pT_dve"), s("out"), s("inverse"), s("inverse_wide")
    sp_mm, sp_st, o_done = s("inverse_product"), s("inverse_spread"), s("oT_stored")
    pair = lambda n: k.banks[:, 2 * (n % 2):2 * (n % 2) + 2, :].rearrange("p b c -> p (b c)")
    turned_at = lambda n: ET[(n // 2) % 2][:, n % 2, :, :]

    def act_program(act):
        def softmax(n):
            act.wait_ge(logit, n + 1)
            if n >= 2:
                act.wait_ge(turned, 2 * (n - 1))
            nc.scalar.activation(E[:, n % 2, :], L[:, n % 2, :], ACT.Exp, scale=-1.0, bias=low[:, n:n + 1],
                                 accum_out=tot[:, n:n + 1]).then_inc(prob, 1)

        def store_spread(i):
            act.wait_ge(sp_mm, i + 1)
            if i >= 2:
                act.wait_ge(o_done, i - 1)
            nc.scalar.activation(spread[:, i % 2, :], k.banks[:, 7, :], ACT.Copy).then_inc(sp_st, 1)

        softmax(0)
        for n, (i, h) in enumerate(items):
            if n + 1 < N:
                softmax(n + 1)
            act.wait_ge(turned, 2 * n + 1)
            if n >= 4:
                act.wait_ge(pv, n // 2 - 1)
            nc.scalar.activation(turned_at(n)[:, 0:4, :], k.banks[:, 4, :].rearrange("p (j t) -> p j t", t=P),
                                 ACT.Copy).then_inc(t_act, 1)
            if h == 1 and i:
                store_spread(i - 1)
        store_spread(NT - 1)

    def pe_program(pe):
        def scores(n):
            i, h = items[n]
            if n >= 2:
                pe.wait_ge(logit, n - 1)
            for c in range(2):
                ins = nc.tensor.matmul(pair(n)[:, c * 512:(c + 1) * 512], q(h, i), kk(h, c), start=True, stop=True)
            ins.then_inc(mm, 1)

        def spread_inverse(i):
            pe.wait_ge(wided, i + 1)
            if i:
                pe.wait_ge(sp_st, i)
            for b in range(4):
                ins = nc.tensor.matmul(k.banks[:, 7, b * P:(b + 1) * P], wide[:, i % 2, b * P:(b + 1) * P], k.ident[:, :],
                                       start=True, stop=True)
            ins.then_inc(sp_mm, 1)

        def values(m, second):
            i, b = m // 4, m % 4
            if b == 0 and not second and i:
                pe.wait_ge(o_done, i)
            if not second:
                pe.wait_ge(t_act, 2 * m + 2)
                pe.wait_ge(t_dve, 2 * m + 2)
            for j in range(4 * second, 4 * second + 4):
                for c in range(2):
                    ins = nc.tensor.matmul(k.banks[64 * c:64 * c + 64, 6, b * P:(b + 1) * P], v(2 * b + c, j),
                                           ET[m % 2][:, c, j, :], start=(j == 0), stop=(j == NT - 1))
            if second:
                ins.then_inc(pv, 1)

        scores(0)
        scores(1)
        for n, (i, h) in enumerate(items):
            pe.wait_ge(prob, n + 1)
            for j in range(NT):
                if n and j % 4 == 0:
                    pe.wait_ge(t_dve if j else t_act, n)
                ins = nc.tensor.transpose(k.banks[:, 4 + j // 4, (j % 4) * P:(j % 4 + 1) * P],
                                          E[:, n % 2, j * P:(j + 1) * P], k.ident[:, :])
                if j % 4 == 3:
                    ins.then_inc(turned, 1)
            if n >= 2:
                values(n // 2 - 1, n % 2)
            if n + 2 < N:
                scores(n + 2)
            if h == 0 and i:
                spread_inverse(i - 1)
        values(N // 2 - 1, 0)
        values(N // 2 - 1, 1)
        spread_inverse(NT - 1)

    def dve_program(dve):
        def logits(n):
            i, h = items[n]
            dve.wait_ge(mm, n + 1)
            if n >= 2:
                dve.wait_ge(prob, n - 1)
            nc.vector.tensor_tensor_reduce(L[:, n % 2, :], pair(n), bias(dve, i), -scale, -MASKED, ALU.add, ALU.min,
                                           low[:, n:n + 1]).then_inc(logit, 1)

        def invert(i):
            dve.wait_ge(prob, 8 * i + 8)
            nc.vector.reciprocal(inv[:, 8 * i:8 * i + 8], tot[:, 8 * i:8 * i + 8]).then_inc(invd, 1)
            dve.wait_ge(invd, i + 1)
            if i >= 2:
                dve.wait_ge(sp_mm, i - 1)
            nc.vector.tensor_copy(wide[:, i % 2, :].rearrange("p (h f) -> p h f", f=64),
                                  inv[:, 8 * i:8 * i + 8].unsqueeze(2).to_broadcast([P, 8, 64])).then_inc(wided, 1)

        def store_out(i):
            dve.wait_ge(sp_st, i + 1)
            dve.wait_ge(pv, 4 * i + 4)
            nc.vector.tensor_tensor(oT[:, :, i * P:(i + 1) * P], k.banks[:, 6, :].rearrange("p (b t) -> p b t", t=P),
                                    spread[:, i % 2, :].rearrange("p (b t) -> p b t", t=P), ALU.mult).then_inc(o_done, 1)

        logits(0)
        for n, (i, h) in enumerate(items):
            if n + 1 < N:
                logits(n + 1)
            dve.wait_ge(turned, 2 * n + 2)
            if n >= 4:
                dve.wait_ge(pv, n // 2 - 1)
            nc.vector.tensor_copy(turned_at(n)[:, 4:8, :], k.banks[:, 5, :].rearrange("p (j t) -> p j t", t=P)).then_inc(t_dve, 1)
            if h == 7:
                invert(i)
            if h == 1 and i:
                store_out(i - 1)
        store_out(NT - 1)

    return act_program, pe_program, dve_program, logit


def stage_sparse_attention(nc, k):
    k.oaT = k.place("sparse_oT", [P, 4, T], 72)
    act_p, pe_p, dve_p, _ = attention(
        nc, k, "sparse",
        lambda h, i: k.aqT[:, h // 2, i * P:(i + 1) * P],
        lambda h, c: k.ak_pad[:, 2 * (h // 4) + h % 2, c * 512:(c + 1) * 512],
        lambda h, j: k.akv[:, j, 128 + (h // 4) * 64:128 + (h // 4) * 64 + 64],
        lambda dve, i: k.isc[:, i, :], 1.0, k.oaT, 96, (40, 48))
    with nc.Block() as block:
        block.scalar(act_p)
        block.tensor(pe_p)
        block.vector(dve_p)


def stage_latent_projection(nc, k):
    p = k.place
    wuq, wuk, wuv = p("w_uq", [P, 2, 768], 209), p("w_uk", [P, 512], 215), p("w_uv", [P, 512], 217)
    k.qf = p("latent_qT", [P, 8, T], 129)
    k.kf = p("latent_kT", [P, 8, T], 40)
    k.vb = p("latent_v", [P, NT, 512], 161)
    qb = p("latent_q_tok", [P, NT, 768], 92)
    t4 = p("latent_rope", [P, 4, 512], 116)
    s = lambda n: k.sem("lat_" + n)
    w_in, mm, st_a, st_d, kr, ready, turned, q_a, q_d = (s(n) for n in ("w_in", "product", "act", "dve", "rope_keys", "ready", "turned", "q_act", "q_dve"))
    d = Steps(k, "lat_rotate")
    jobs = [("q", i, c) for i in range(NT) for c in range(2)] + [("v", i, 0) for i in range(NT)] + \
           [("k", h, c) for h in range(8) for c in range(2)]
    by = ["act" if n % 2 == 0 else "dve" for n in range(len(jobs))]
    with nc.Block() as block:
        @block.sync
        def _(sp):
            sp.dma_start(wuq[:, :, :], k.w_uq_2[0].rearrange("(k p) h f -> p k (h f)", p=P)).then_inc(w_in, 16)
            sp.dma_start(wuk[:, :], k.w_uk_2[0].rearrange("r h f -> r (h f)")).then_inc(w_in, 16)
            sp.dma_start(wuv[:, :], k.w_uv_2[0].rearrange("r h f -> r (h f)")).then_inc(w_in, 16)

        def dest(n):
            kind, a, c = jobs[n]
            if kind == "q":
                return qb[:, a, c * 384:(c + 1) * 384], k.banks[:, n % 8, 0:384]
            if kind == "v":
                return k.vb[:, a, :], k.banks[:, n % 8, :]
            return k.kf[0:64, a, c * 512:(c + 1) * 512], k.banks[0:64, n % 8, :]

        @block.gpsimd
        def _(pool):
            for h in range(8):
                pool.tensor_copy(k.kf[64:96, h, :], k.krT[64:96, :]).then_inc(kr, 1)

        @block.scalar
        def _(act):
            for n in range(0, len(jobs), 2):
                out, src = dest(n)
                act.wait_ge(mm, n + 1)
                nc.scalar.activation(out, src, ACT.Copy).then_inc(st_a, 1)
            for i in range(NT):
                for b in range(0, 2):
                    if b == 0:
                        act.wait_ge(turned, 2 * i + 1)
                        nc.scalar.activation(k.qf[0:96, 0:4, i * P:(i + 1) * P],
                                             k.banks[0:96, 2 * (i % 2), :].rearrange("p (h t) -> p h t", t=P), ACT.Copy).then_inc(q_a, 1)

        @block.tensor
        def _(pe):
            pe.wait_ge(w_in, 48)
            for n, (kind, a, c) in enumerate(jobs):
                out = dest(n)[1]
                if n >= 8:
                    pe.wait_ge(st_a if n % 2 == 0 else st_d, (n - 8) // 2 + 1)
                if kind == "q":
                    for b in range(2):
                        ins = nc.tensor.matmul(out, k.cqT[:, b, a * P:(a + 1) * P], wuq[:, b, c * 384:(c + 1) * 384],
                                               start=(b == 0), stop=(b == 1))
                elif kind == "v":
                    ins = nc.tensor.matmul(out, k.ckvT[:, a * P:(a + 1) * P], wuv[:, :], start=True, stop=True)
                else:
                    ins = nc.tensor.matmul(out, wuk[:, a * 64:(a + 1) * 64], k.ckvT[:, c * 512:(c + 1) * 512], start=True, stop=True)
                ins.then_inc(mm, 1)
            pe.wait_ge(st_a, len(jobs) // 2)
            pe.wait_ge(st_d, len(jobs) // 2)
            pe.wait_ge(ready, 1)
            for i in range(NT):
                if i >= 2:
                    pe.wait_ge(q_a, i - 1)
                    pe.wait_ge(q_d, i - 1)
                for h in range(8):
                    ins = nc.tensor.transpose(k.banks[0:96, 2 * (i % 2) + h // 4, (h % 4) * P:(h % 4 + 1) * P],
                                              qb[:, i, h * 96:(h + 1) * 96], k.ident[:, :])
                    if h % 4 == 3:
                        ins.then_inc(turned, 1)

        @block.vector
        def _(dve):
            for n in range(1, len(jobs), 2):
                out, src = dest(n)
                dve.wait_ge(mm, n + 1)
                nc.vector.tensor_copy(out, src).then_inc(st_d, 1)
                if n == 15:
                    dve.wait_ge(st_a, 8)
                    dve.wait_ge(st_d, 8)
                    for i0 in range(0, NT, 4):
                        x = qb[:, i0:i0 + 4, :].rearrange("p i (h f) -> p i h f", f=96)
                        t = [t4[:, c, :].rearrange("p (i h f) -> p i h f", i=4, h=8) for c in range(4)]
                        tab = [a[:, i0:i0 + 4, 8:24].unsqueeze(2).to_broadcast([P, 4, 8, 16]) for a in (k.cos, k.sin)]
                        rope_dve(nc, dve, d, x[:, :, :, 64:80], x[:, :, :, 80:96], tab[0], tab[1], t)
                        dve.wait_ge(d.sem, d.n)
                    nc.vector.memset(k.small[:, 79:80], 0.0).then_inc(ready, 1)
            for i in range(NT):
                dve.wait_ge(turned, 2 * i + 2)
                nc.vector.tensor_copy(k.qf[0:96, 4:8, i * P:(i + 1) * P],
                                      k.banks[0:96, 2 * (i % 2) + 1, :].rearrange("p (h t) -> p h t", t=P)).then_inc(q_d, 1)


def stage_latent_attention(nc, k):
    p = k.place
    k.obT = p("latent_oT", [P, 4, T], 193)
    pen = p("causal_bias", [P, 2, T], 177)
    made = k.sem("lat_bias")
    state = {"made": -1}
    hold = {}

    def bias(dve, i):
        if state["made"] < i:
            state["made"] = i
            dve.wait_ge(made, i + 1)
        return pen[:, i % 2, :]

    act_p, pe_p, dve_p, logit = attention(
        nc, k, "latent",
        lambda h, i: k.qf[0:96, h, i * P:(i + 1) * P],
        lambda h, c: k.kf[0:96, h, c * 512:(c + 1) * 512],
        lambda h, j: k.vb[:, j, h * 64:(h + 1) * 64],
        bias, float(np.float32(96 ** -0.5)), k.obT, 92, (185, 209))
    with nc.Block() as block:
        @block.gpsimd
        def _(pool):
            for i in range(NT):
                if i >= 2:
                    pool.wait_ge(logit, 8 * (i - 1))
                pool.tensor_scalar(pen[:, i % 2, :], k.posrow[:, :], k.posq[:, i:i + 1], MASKED, ALU.is_gt,
                                   ALU.mult).then_inc(made, 1)
        block.scalar(act_p)
        block.tensor(pe_p)
        block.vector(dve_p)


def stage_merge(nc, k):
    p = k.place
    mT = p("merged_T", [P, KB, T], 100)
    gates = p("gates_in", [P, 4, T], 132)
    pa, pb = p("part_a", [P, 2, 512], 148), p("part_b", [P, 2, 512], 152)
    k.h2 = p("h2", [P, NT, D], 160)
    k.h_hi = p("h_hi", [P, KB, T], 160, F32R)
    k.h_lo = p("h_lo", [P, KB, T], 40, F32R)
    ffng = k.small[:, 232:240]
    s = lambda n: k.sem("mrg_" + n)
    g_in = [s(f"gate_in_{c}") for c in range(2)]
    x1_in, vec_in, mm_a, mm_b, st_a, st_b, merged, gained, res = (s(n) for n in ("x1_in", "vec_in", "a", "b", "a_st", "b_st", "sum", "gained", "residual"))
    h2_out, rounded = s("h2_out"), s("h_rounded")
    k.w.freed[k.c_ba] = (mm_a, 16)
    k.w.freed[k.c_bb] = (mm_b, 16)
    jobs = [dict(chunk=k.c_out2[h], kind="tokens", tile=i, col=0, width=512, by="dve", dest=h, how="add")
            for i in range(NT) for h in range(2)]
    m_hi, m_lo = p("merged_hi", [P, KB, T], 40, F32R), p("merged_lo", [P, KB, T], 100, F32R)
    m_rounded, m_split = s("rounded"), s("split")
    parts = Parts(nc, k, "second_out", k.c_out2, m_hi, m_lo, (72, 193))
    proj = Projection(nc, k, "second_out", jobs, banks=8, parts=parts)
    norm = NormTranspose(nc, k, "norm3", k.h2, p("square_scratch", [P, 4, D], 132), p("h2_normed", [P, NT, D], 100))
    ga = lambda n: k.gate_dram[n]
    with nc.Block() as block:
        @block.sync
        def _(sp):
            for n in range(KB):
                if n >= 2:
                    sp.wait_ge(st_a, 2 * (n - 1))
                    sp.wait_ge(st_b, 2 * (n - 1))
                for br in range(2):
                    sp.dma_start(gates[:, 2 * (n % 2) + br, :], ga(8 * br + n)).then_inc(g_in[n % 2], 16)
                if n == 0:
                    sp.dma_start(k.h2[:, :, :], k.x1_dram.rearrange("(i p) d -> p i d", p=P)).then_inc(x1_in, 16)
            k.w.load_up_to(sp, k.c_up[1])
            for i in range(NT):
                sp.wait_ge(proj.stored["dve"], 2 * i + 2)
                sp.dma_start(k.h2_dram[i * P:(i + 1) * P, :], k.h2[:, i, :]).then_inc(h2_out, 16)
            sp.wait_ge(h2_out, 16 * NT)

        @block.gpsimd
        def _(pool):
            for n in range(16):
                pool.wait_ge(st_a, n + 1)
                pool.wait_ge(st_b, n + 1)
                pool.tensor_tensor(mT[:, n // 2, (n % 2) * 512:(n % 2 + 1) * 512], pa[:, n % 2, :], pb[:, n % 2, :],
                                   ALU.add).then_inc(merged, 1)

        @block.scalar
        def _(act):
            act.dma_start(ffng, k.norm_ffn_g_2[0].rearrange("(k p) -> p k", p=P), allow_slow_non_contiguous=True).then_inc(vec_in, 16)
            for n in range(16):
                act.wait_ge(merged, n + 1)
                nc.scalar.activation(m_hi[:, n // 2, (n % 2) * 512:(n % 2 + 1) * 512],
                                     mT[:, n // 2, (n % 2) * 512:(n % 2 + 1) * 512], ACT.Copy).then_inc(m_rounded, 1)
            act.wait_ge(mm_a, 16)
            act.wait_ge(mm_b, 16)
            for h in range(2):
                parts.split_act(act, k.c_out2[h])
            norm.act_stats(act, lambda e, i: e.wait_ge(proj.stored["dve"], 2 * i + 2))
            norm.store(act, 0)
            act.wait_ge(vec_in, 16)
            act.wait_ge(h2_out, 16 * NT)
            act.wait_ge(norm.divided, NT)
            act.wait_ge(norm.by_act, NT)
            act.wait_ge(norm.by_dve, NT)
            for b in range(KB):
                nc.scalar.activation(k.h_hi[:, b, :], k.hT[:, b, :], ACT.Copy, scale=ffng[:, b:b + 1]).then_inc(rounded, 1)

        @block.tensor
        def _(pe):
            for n in range(16):
                f, c = n // 2, n % 2
                for br, (chunk, src, mm, st) in enumerate(((k.c_ba, k.oaT, mm_a, st_a), (k.c_bb, k.obT, mm_b, st_b))):
                    if n == 0:
                        k.w.wait(pe, chunk)
                    if n >= 4:
                        pe.wait_ge(st, n - 3)
                    wv = k.w.view(chunk)
                    for b in range(4):
                        ins = nc.tensor.matmul(k.banks[:, 2 * (n % 4) + br, :], wv[:, b, f * P:(f + 1) * P],
                                               src[:, b, c * 512:(c + 1) * 512], start=(b == 0), stop=(b == 3))
                    ins.then_inc(mm, 1)
            pe.wait_ge(m_split, 16)
            proj.pe_jobs(pe, 0, len(jobs))
            pe.wait_ge(proj.stored["dve"], len(jobs))
            norm.pe_transpose(pe)

        @block.vector
        def _(dve):
            def rest_of_merged(n):
                cols = slice((n % 2) * 512, (n % 2 + 1) * 512)
                dve.wait_ge(m_rounded, n + 1)
                nc.vector.tensor_tensor(m_lo[:, n // 2, cols], mT[:, n // 2, cols], m_hi[:, n // 2, cols],
                                        ALU.subtract).then_inc(m_split, 1)

            for n in range(16):
                f, c = n // 2, n % 2
                if c == 0:
                    dve.wait_ge(g_in[f % 2], 32 * (f // 2 + 1))
                for br, (buf, mm, st) in enumerate(((pa, mm_a, st_a), (pb, mm_b, st_b))):
                    dve.wait_ge(mm, n + 1)
                    if n >= 2:
                        dve.wait_ge(merged, n - 1)
                    nc.vector.tensor_tensor(buf[:, n % 2, :], k.banks[:, 2 * (n % 4) + br, :],
                                            gates[:, 2 * (f % 2) + br, c * 512:(c + 1) * 512], ALU.mult).then_inc(st, 1)
                if n:
                    rest_of_merged(n - 1)
            rest_of_merged(15)
            for h in range(2):
                parts.split_dve(dve, k.c_out2[h])
            dve.wait_ge(x1_in, 16)
            for j, job in enumerate(jobs):
                i, h = job["tile"], job["dest"]
                dve.wait_ge(proj.done, j + 1)
                xs = k.h2[:, i, h * 512:(h + 1) * 512]
                nc.vector.tensor_tensor(xs, proj.bank(j), xs, ALU.add).then_inc(proj.stored["dve"], 1)
            norm.dve_stats(dve)
            norm.dve_divide(dve)
            norm.store(dve, 1)
            dve.wait_ge(norm.by_act, NT)
            dve.wait_ge(norm.by_dve, NT)
            dve.wait_ge(vec_in, 16)
            for b in range(KB):
                dve.wait_ge(rounded, b + 1)
                nc.vector.scalar_tensor_tensor(out=k.h_lo[:, b, :], in0=k.hT[:, b, :], scalar=ffng[:, b:b + 1],
                                               in1=k.h_hi[:, b, :], op0=ALU.mult, op1=ALU.subtract).then_inc(gained, 1)


def stage_ffn_up(nc, k):
    p = k.place
    k.act = p("ffn_act", [P, FBLK, T], 72)
    Y = p("ffn_conv", [P, 4, T], 192)
    w_hi = [p(f"up_hi_{c}", [P, KB, P], (208, 212)[c], F32R) for c in range(2)]
    w_lo = [p(f"up_lo_{c}", [P, KB, P], (216, 0.5)[c], F32R) for c in range(2)]
    cw = p("conv_taps", [P, 3, 2 * FBLK], 6)
    cb = p("conv_bias", [P, 2 * FBLK], 7)
    vec_in = k.sem("conv_in")
    s = lambda n: k.sem("ffn_" + n)
    mm, y0, y1, y2, gate, out, hi_done, lo_done = (s(n) for n in ("u", "tap2", "tap1", "tap0", "silu", "act", "hi", "lo"))
    N = 2 * FBLK
    for n, c in enumerate(k.c_up):
        k.w.freed[c] = (lo_done, 4 * n + 4)
    pair = lambda n: k.banks[:, 2 * (n % 4):2 * (n % 4) + 2, :].rearrange("p b c -> p (b c)")

    def weights(n):
        f, v = n // 2, n % 2
        c0 = v * 256 + (f % 2) * P
        return k.w.view(k.c_up[f // 2])[:, :, c0:c0 + P]

    with nc.Block() as block:
        @block.sync
        def _(sp):
            k.w.load_up_to(sp, k.c_down[0][1])

        @block.gpsimd
        def _(pool):
            for f in range(FBLK):
                pool.wait_ge(gate, f + 1)
                pool.wait_ge(y2, 2 * f + 2)
                b = 2 * (f % 2)
                pool.tensor_tensor(k.act[:, f, :], Y[:, b, :], Y[:, b + 1, :], ALU.mult).then_inc(out, 1)

        @block.scalar
        def _(act):
            slow = dict(allow_slow_non_contiguous=True)
            for j in range(3):
                act.dma_start(cw[:, j, :], k.conv_w_2[0, j].rearrange("(f p) -> p f", p=P), **slow).then_inc(vec_in, 16)
            act.dma_start(cb[:, :], k.conv_b_2[0].rearrange("(f p) -> p f", p=P), **slow).then_inc(vec_in, 16)

            def round_weights(n):
                if n >= N:
                    return
                k.w.wait(act, k.c_up[n // 4])
                if n >= 2:
                    act.wait_ge(mm, n - 1)
                nc.scalar.activation(w_hi[n % 2][:, :, :], weights(n), ACT.Copy).then_inc(hi_done, 1)

            round_weights(0)
            round_weights(1)
            act.wait_ge(vec_in, 64)
            for n in range(N + 2):
                if n < N:
                    f, v = n // 2, n % 2
                    c = f + v * FBLK
                    act.wait_ge(mm, n + 1)
                    round_weights(n + 2)
                    if f >= 2:
                        act.wait_ge(out, f - 1)
                    nc.scalar.activation(Y[:, 2 * (f % 2) + v, :], pair(n), ACT.Identity, bias=cb[:, c:c + 1],
                                         scale=cw[:, 2, c:c + 1]).then_inc(y0, 1)
                if n >= 2 and n % 2 == 0:
                    f = n // 2 - 1
                    act.wait_ge(y2, 2 * f + 1)
                    nc.scalar.activation(Y[:, 2 * (f % 2), :], Y[:, 2 * (f % 2), :], ACT.Silu).then_inc(gate, 1)

        @block.tensor
        def _(pe):
            for n in range(N):
                pe.wait_ge(lo_done, n + 1)
                if n >= 4:
                    pe.wait_ge(y2, n - 3)
                for h in range(2):
                    tok = slice(h * 512, (h + 1) * 512)
                    for b in range(KB):
                        ins = products_of_parts(nc, pair(n)[:, tok], w_hi[n % 2][:, b, :], w_lo[n % 2][:, b, :],
                                                k.h_hi[:, b, tok], k.h_lo[:, b, tok], b == 0, b == KB - 1)
                ins.then_inc(mm, 1)

        @block.vector
        def _(dve):
            def rest_of_weights(n):
                if n >= N:
                    return
                k.w.wait(dve, k.c_up[n // 4])
                dve.wait_ge(hi_done, n + 1)
                if n >= 2:
                    dve.wait_ge(mm, n - 1)
                nc.vector.tensor_tensor(w_lo[n % 2][:, :, :], weights(n), w_hi[n % 2][:, :, :], ALU.subtract).then_inc(lo_done, 1)

            rest_of_weights(0)
            rest_of_weights(1)
            dve.wait_ge(vec_in, 64)
            for n in range(N):
                f, v = n // 2, n % 2
                c, y = f + v * FBLK, Y[:, 2 * (f % 2) + v, :]
                dve.wait_ge(mm, n + 1)
                rest_of_weights(n + 2)
                dve.wait_ge(y0, n + 1)
                nc.vector.scalar_tensor_tensor(out=y[:, 1:T], in0=pair(n)[:, 0:T - 1], scalar=cw[:, 1, c:c + 1],
                                               in1=y[:, 1:T], op0=ALU.mult, op1=ALU.add).then_inc(y1, 1)
                dve.wait_ge(y1, n + 1)
                nc.vector.scalar_tensor_tensor(out=y[:, 2:T], in0=pair(n)[:, 0:T - 2], scalar=cw[:, 0, c:c + 1],
                                               in1=y[:, 2:T], op0=ALU.mult, op1=ALU.add).then_inc(y2, 1)


def stage_ffn_down(nc, k):
    p = k.place
    x = k.h2
    row = p("last_gain", [P, D], 192)
    a_hi, a_lo = p("act_hi", [P, 2, T], 196, F32R), p("act_lo", [P, 2, T], 204, F32R)
    w_hi, w_lo = p("down_hi", [P, 2, 512], 212, F32R), p("down_lo", [P, 2, 512], 216, F32R)
    s = lambda n: k.sem("down_" + n)
    vec_in, h2_in, used, done, added, summed = (s(n) for n in ("vec_in", "h2_in", "used", "product", "added", "summed"))
    ahi_done, alo_done, whi_done, wlo_done = s("act_hi"), s("act_lo"), s("w_hi"), s("w_lo")
    out = k.output_stored
    rstd_s, root_s, mean_s, fin = s("rstd"), s("root"), s("mean"), s("normed")
    sq, ms, rt, rs = (k.small[:, c:c + 8] for c in (168, 176, 184, 192))
    steps = [(h, f) for h in range(2) for f in range(FBLK)]
    N = len(steps)
    for t, (h, f) in enumerate(steps):
        k.w.freed[k.c_down[h][f // 8]] = (wlo_done, t + 1)
    with nc.Block() as block:
        @block.sync
        def _(sp):
            sp.dma_start(x[:, :, :], k.h2_dram.rearrange("(i p) d -> p i d", p=P)).then_inc(h2_in, 16)
            k.w.load_up_to(sp, k.c_down[1][2])
            for i in range(NT):
                sp.wait_ge(fin, i + 1)
                sp.dma_start(k.out[0, i * P:(i + 1) * P, :], x[:, i, :]).then_inc(out, 16)
            sp.wait_ge(out, 16 * NT)

        @block.gpsimd
        def _(pool):
            for t, (h, f) in enumerate(steps):
                chunk = k.c_down[h][f // 8]
                k.w.wait(pool, chunk)
                if t >= 2:
                    pool.wait_ge(used, t - 1)
                w = k.w.view(chunk)[:, f % 8, :]
                pool.tensor_copy(w_hi[:, t % 2, :], w).then_inc(whi_done, 1)
                pool.wait_ge(whi_done, t + 1)
                pool.tensor_tensor(w_lo[:, t % 2, :], w, w_hi[:, t % 2, :], ALU.subtract).then_inc(wlo_done, 1)

        @block.scalar
        def _(act):
            act.dma_start(row[:, :], k.norm_final_g_2.partition_broadcast(P)).then_inc(vec_in, 16)
            for t, (h, f) in enumerate(steps):
                if t >= 2:
                    act.wait_ge(used, t - 1)
                nc.scalar.activation(a_hi[:, t % 2, :], k.act[:, f, :], ACT.Copy).then_inc(ahi_done, 1)
            for i in range(NT):
                act.wait_ge(added, NT + i + 1)
                nc.scalar.activation(k.hT[:, i, :], x[:, i, :], ACT.Square, accum_out=sq[:, i:i + 1]).then_inc(summed, 1)
                act.wait_ge(mean_s, i + 1)
                nc.scalar.activation(rt[:, i:i + 1], ms[:, i:i + 1], ACT.Sqrt).then_inc(root_s, 1)

        @block.tensor
        def _(pe):
            for t, (h, f) in enumerate(steps):
                pe.wait_ge(alo_done, t + 1)
                pe.wait_ge(wlo_done, t + 1)
                for i in range(NT):
                    if h and f == 0:
                        pe.wait_ge(added, i + 1)
                    tok = slice(i * P, (i + 1) * P)
                    ins = products_of_parts(nc, k.banks[:, i, :], a_hi[:, t % 2, tok], a_lo[:, t % 2, tok],
                                            w_hi[:, t % 2, :], w_lo[:, t % 2, :], f == 0, f == FBLK - 1)
                    if f == FBLK - 1 and i < NT - 1:
                        ins.then_inc(done, 1)
                ins.then_inc(used, 1)

        @block.vector
        def _(dve):
            def add(h, i):
                if i < NT - 1:
                    dve.wait_ge(done, 7 * h + i + 1)
                else:
                    dve.wait_ge(used, FBLK * (h + 1))
                xs = x[:, i, h * 512:(h + 1) * 512]
                nc.vector.tensor_tensor(xs, k.banks[:, i, :], xs, ALU.add).then_inc(added, 1)

            def finish(i):
                dve.wait_ge(summed, i + 1)
                nc.vector.tensor_scalar(ms[:, i:i + 1], sq[:, i:i + 1], 1.0 / D, EPS, ALU.mult, ALU.add).then_inc(mean_s, 1)
                dve.wait_ge(root_s, i + 1)
                nc.vector.reciprocal(rs[:, i:i + 1], rt[:, i:i + 1]).then_inc(rstd_s, 1)
                dve.wait_ge(rstd_s, i + 1)
                nc.vector.scalar_tensor_tensor(out=x[:, i, :], in0=x[:, i, :], scalar=rs[:, i:i + 1], in1=row[:, :],
                                               op0=ALU.mult, op1=ALU.mult).then_inc(fin, 1)

            for t, (h, f) in enumerate(steps):
                dve.wait_ge(ahi_done, t + 1)
                if t >= 2:
                    dve.wait_ge(used, t - 1)
                nc.vector.tensor_tensor(a_lo[:, t % 2, :], k.act[:, f, :], a_hi[:, t % 2, :], ALU.subtract).then_inc(alo_done, 1)
                if t == FBLK:
                    dve.wait_ge(h2_in, 16)
                    for i in range(NT):
                        add(0, i)
            dve.wait_ge(vec_in, 16)
            for i in range(NT):
                add(1, i)
                if i:
                    finish(i - 1)
            finish(NT - 1)


def build(nc, views):
    k = Kernel(nc)
    k.x = views["x"]
    k.c = views["c"]
    k.w_ada = views["w_ada"]
    k.b_ada = views["b_ada"]
    k.w_in = views["w_in"]
    k.w_gla_gate2 = views["w_gla_gate2"]
    k.b_gla_gate = views["b_gla_gate"]
    k.gla_norm_w = views["gla_norm_w"]
    k.hgrn_lb_logits = views["hgrn_lb_logits"]
    k.hgrn_norm_w = views["hgrn_norm_w"]
    k.w_out = views["w_out"]
    k.final_norm_w = views["final_norm_w"]
    k.positions_2 = views["positions_2"]
    k.norm_mix_g_2 = views["norm_mix_g_2"]
    k.w_in_2 = views["w_in_2"]
    k.idx_k_norm_g_2 = views["idx_k_norm_g_2"]
    k.q_a_norm_g_2 = views["q_a_norm_g_2"]
    k.kv_a_norm_g_2 = views["kv_a_norm_g_2"]
    k.w_uq_2 = views["w_uq_2"]
    k.w_uk_2 = views["w_uk_2"]
    k.w_uv_2 = views["w_uv_2"]
    k.w_branch_a_2 = views["w_branch_a_2"]
    k.w_branch_b_2 = views["w_branch_b_2"]
    k.w_out_2 = views["w_out_2"]
    k.norm_ffn_g_2 = views["norm_ffn_g_2"]
    k.w_up_2 = views["w_up_2"]
    k.conv_w_2 = views["conv_w_2"]
    k.conv_b_2 = views["conv_b_2"]
    k.w_down_2 = views["w_down_2"]
    k.norm_final_g_2 = views["norm_final_g_2"]
    k.out = views["out"]
    k.x1_dram = nc.dram_tensor("x1_scratch", (T, D), F32, kind="Internal").ap()
    k.h2_dram = nc.dram_tensor("h2_scratch", (T, D), F32, kind="Internal").ap()
    k.gate_dram = nc.dram_tensor("gate_scratch", (16, P, T), F32, kind="Internal").ap()
    plan(nc, k)
    stage_input(nc, k)
    k.end_stage()
    stage_gla_projection(nc, k)
    k.end_stage()
    stage_gated_attention(nc, k, k.gla, 0)
    k.end_stage()
    stage_hgrn_projection(nc, k)
    k.end_stage()
    stage_gated_attention(nc, k, k.hgrn, 4)
    k.end_stage()
    stage_stick_projection(nc, k)
    k.end_stage()
    stage_stick_attention(nc, k)
    k.end_stage()
    stage_first_output(nc, k)
    k.end_stage()
    stage_second_projection(nc, k)
    k.end_stage()
    stage_index_scores(nc, k)
    k.end_stage()
    stage_select(nc, k)
    k.end_stage()
    stage_sparse_attention(nc, k)
    k.end_stage()
    stage_latent_projection(nc, k)
    k.end_stage()
    stage_latent_attention(nc, k)
    k.end_stage()
    stage_merge(nc, k)
    k.end_stage()
    stage_ffn_up(nc, k)
    k.end_stage()
    stage_ffn_down(nc, k)


INPUTS = ['x', 'c', 'w_ada', 'b_ada', 'w_in', 'w_gla_gate2', 'b_gla_gate', 'gla_norm_w', 'hgrn_lb_logits',
          'hgrn_norm_w', 'w_out', 'final_norm_w', 'positions_2', 'norm_mix_g_2', 'w_in_2', 'idx_k_norm_g_2',
          'q_a_norm_g_2', 'kv_a_norm_g_2', 'w_uq_2', 'w_uk_2', 'w_uv_2', 'w_branch_a_2', 'w_branch_b_2',
          'w_out_2', 'norm_ffn_g_2', 'w_up_2', 'conv_w_2', 'conv_b_2', 'w_down_2', 'norm_final_g_2']


def kernel(**inputs):
    import numpy as _np
    import concourse.bacc as _bacc
    from concourse import mybir as _mybir
    from concourse.bass_utils import run_bass_kernel_spmd as _run

    nc = _bacc.Bacc("TRN2", target_bir_lowering=False, num_devices=1, dynamic_dma_scratch_size=1024)
    arrays, views = {}, {}
    for name in INPUTS:
        a = _np.ascontiguousarray(inputs[name])
        arrays[f"in_{name}"] = a
        views[name] = nc.dram_tensor(f"in_{name}", a.shape, _mybir.dt.from_np(a.dtype), kind="ExternalInput").ap()
    views["out"] = nc.dram_tensor("out_0", (1, T, D), _mybir.dt.float32, kind="ExternalOutput").ap()
    build(nc, views)
    r = _run(nc, [arrays], core_ids=[0])
    return r.results[0]["out_0"]
```
